# Optimizing a Trainium2 kernel written in Bass

```python
import math
import jax
import jax.numpy as jnp
from jax import lax
import numpy as np

D_MODEL = 1024
BATCH = 1
SEQ = 1024
DEPTH = 2
DEC_BATCH = 8
DEC_SEQ = 4
PAST_LEN = 2048
PAGE_SIZE = 128

N_EVEN = (DEPTH + 1) // 2
N_ODD = DEPTH // 2
H_A = 4
DK_A = D_MODEL // 16
DV_A = D_MODEL // 8
CHUNK_RET = 128
H_B = 4
DH_B = D_MODEL // 16
DV_B = 2 * DH_B
Q_BLOCK = 128
H_C = 4
DK_C = D_MODEL // 8
DV_C = D_MODEL // 4
GATE_RANK = 16
GATE_TAU = 16.0
CHUNK_GLA = 64
D_FF = ((8 * D_MODEL // 3 + 127) // 128) * 128
CONV_W = 3
ROPE_THETA = 10000.0
EPS = 1e-6
AB_WIDTHS = (H_A * DK_A, H_A * DK_A, H_A * DV_A, H_A * DV_A, H_B * 2 * DH_B, H_B * 2 * DH_B, H_B * DV_B)
MIX_AB = H_A * DV_A + H_B * DV_B
C_WIDTHS = (H_C * DK_C, H_C * DK_C, H_C * DV_C, H_C * DV_C, GATE_RANK)
MIX_C = H_C * DV_C

kernel_name = 'hybrid_retention_diffattn_gla_convffn_step'

def _cuts(widths):
    return [int(v) for v in np.cumsum(widths)[:-1]]

def _chunk(L, C):
    return C if L % C == 0 else L

def _rmsnorm(x, g=None):
    xf = x.astype(jnp.float32)
    y = xf * lax.rsqrt(jnp.mean(xf * xf, axis=-1, keepdims=True) + EPS)
    if g is not None:
        y = y * g.astype(jnp.float32)
    return y.astype(x.dtype)

def _rotary(x, pos):
    d = x.shape[-1]
    inv = ROPE_THETA ** (-jnp.arange(0, d, 2, dtype=jnp.float32) / d)
    ang = pos.astype(jnp.float32)[:, None] * inv[None, :]
    shape = (ang.shape[0],) + (1,) * (x.ndim - 3) + (d // 2,)
    cos = jnp.cos(ang).reshape(shape)
    sin = jnp.sin(ang).reshape(shape)
    xf = x.astype(jnp.float32)
    x1, x2 = xf[..., : d // 2], xf[..., d // 2:]
    return jnp.concatenate([x1 * cos - x2 * sin, x2 * cos + x1 * sin], axis=-1).astype(x.dtype)

def _adaln(c, w, b):
    return jnp.split(jax.nn.silu(c) @ w + b, 6, axis=-1)

def _modulate(x, g, shift, scale):
    return _rmsnorm(x, g) * (1.0 + scale[:, None, :]) + shift[:, None, :]

def _residual(x, y, g, gate):
    return x + gate[:, None, :] * _rmsnorm(y, g)

def _retention(q, k, v, s0):
    B, L, H, dk = q.shape
    dv = v.shape[-1]
    C = _chunk(L, CHUNK_RET)
    n = L // C
    log_gamma = jnp.log1p(-jnp.exp2(-5.0 - jnp.arange(H, dtype=jnp.float32)))
    idx = jnp.arange(C, dtype=jnp.float32)
    rel = idx[:, None] - idx[None, :]
    dec_intra = jnp.exp(jnp.where(rel[None] >= 0, rel[None] * log_gamma[:, None, None], -jnp.inf))
    dec_q = jnp.exp((idx + 1.0)[:, None] * log_gamma[None, :])
    dec_k = jnp.exp((C - 1.0 - idx)[:, None] * log_gamma[None, :])
    dec_c = jnp.exp(C * log_gamma)

    def to_chunks(t):
        return t.astype(jnp.float32).reshape(B, n, C, H, t.shape[-1]).transpose(1, 0, 2, 3, 4)

    def step(S, xs):
        qc, kc, vc = xs
        sc = jnp.einsum('bihd,bjhd->bhij', qc, kc) * dec_intra[None]
        o = (jnp.einsum('bhij,bjhe->bihe', sc, vc)
             + jnp.einsum('bihd,bhde->bihe', qc, S) * dec_q[None, :, :, None])
        S = S * dec_c[None, :, None, None] + jnp.einsum('bjhd,bjhe->bhde', kc * dec_k[None, :, :, None], vc)
        return S, o

    S, o = lax.scan(step, s0.astype(jnp.float32), (to_chunks(q), to_chunks(k), to_chunks(v)))
    return o.transpose(1, 0, 2, 3, 4).reshape(B, L, H, dv), S

def _gla(q, k, v, logg, s0):
    B, L, H, dk = q.shape
    dv = v.shape[-1]
    C = _chunk(L, CHUNK_GLA)
    n = L // C
    causal = jnp.tril(jnp.ones((C, C), dtype=bool))

    def to_chunks(t):
        return t.astype(jnp.float32).reshape(B, n, C, H, t.shape[-1]).transpose(1, 0, 2, 3, 4)

    def step(S, xs):
        qc, kc, vc, gc = xs
        b = jnp.cumsum(gc, axis=1)
        diff = b[:, :, None] - b[:, None, :]
        dec = jnp.exp(jnp.where(causal[None, :, :, None, None], diff, -jnp.inf))
        att = jnp.einsum('bihd,bjhd,bijhd->bhij', qc, kc, dec)
        o = jnp.einsum('bhij,bjhe->bihe', att, vc) + jnp.einsum('bihd,bhde->bihe', qc * jnp.exp(b), S)
        b_last = b[:, -1]
        S = S * jnp.exp(b_last)[..., None] + jnp.einsum('bjhd,bjhe->bhde', kc * jnp.exp(b_last[:, None] - b), vc)
        return S, o

    S, o = lax.scan(step, s0.astype(jnp.float32), (to_chunks(q), to_chunks(k), to_chunks(v), to_chunks(logg)))
    return o.transpose(1, 0, 2, 3, 4).reshape(B, L, H, dv), S

def _diff_attend(q, k, v, q_pos, k_pos, lam):
    s = jnp.einsum('bqhmd,bkhmd->bhmqk', q, k).astype(jnp.float32) * (DH_B ** -0.5)
    mask = k_pos[None, :] <= q_pos[:, None]
    p = jax.nn.softmax(jnp.where(mask, s, -jnp.inf), axis=-1)
    a = p[:, :, 0] - lam * p[:, :, 1]
    return jnp.einsum('bhqk,bkhe->bqhe', a.astype(v.dtype), v)

def _diff_attn_blocks(q, k, v, lam):
    B, L = q.shape[:2]
    nb = L // Q_BLOCK
    pos = jnp.arange(L)
    qb = q.reshape(B, nb, Q_BLOCK, H_B, 2, DH_B).transpose(1, 0, 2, 3, 4, 5)
    pb = pos.reshape(nb, Q_BLOCK)
    out = lax.map(lambda xs: _diff_attend(xs[0], k, v, xs[1], pos, lam), (qb, pb))
    return out.transpose(1, 0, 2, 3, 4).reshape(B, L, H_B, DV_B)

def _ab_mixer(h, pos, s0, k_past, v_past, w_in, w_out, lam, lam_init, g_diff):
    B, L, _ = h.shape
    qa, ka, va, ga, qb, kb, vb = jnp.split(h @ w_in, _cuts(AB_WIDTHS), axis=-1)
    qa = _rotary(qa.reshape(B, L, H_A, DK_A), pos)
    ka = _rotary(ka.reshape(B, L, H_A, DK_A), pos) * (DK_A ** -0.5)
    o_ret, s_new = _retention(qa, ka, va.reshape(B, L, H_A, DV_A), s0)
    qb = _rotary(qb.reshape(B, L, H_B, 2, DH_B), pos)
    kb = _rotary(kb.reshape(B, L, H_B, 2, DH_B), pos)
    vb = vb.reshape(B, L, H_B, DV_B)
    if k_past is None:
        o_dif = _diff_attn_blocks(qb, kb, vb, lam)
    else:
        k_all = jnp.concatenate([k_past.astype(kb.dtype), kb], axis=1)
        v_all = jnp.concatenate([v_past.astype(vb.dtype), vb], axis=1)
        o_dif = _diff_attend(qb, k_all, v_all, pos, jnp.arange(k_all.shape[1]), lam)
    ret = _rmsnorm(o_ret.astype(h.dtype)) * jax.nn.silu(ga.reshape(B, L, H_A, DV_A))
    dif = _rmsnorm(o_dif, g_diff) * (1.0 - lam_init)
    mix = jnp.concatenate([ret.reshape(B, L, -1), dif.reshape(B, L, -1)], axis=-1)
    return mix @ w_out, s_new.astype(h.dtype), kb.reshape(B, L, H_B, 2 * DH_B), vb

def _gla_mixer(h, s0, w_in, w_gate, b_gate, g_norm, w_out):
    B, L, _ = h.shape
    q, k, v, r, a = jnp.split(h @ w_in, _cuts(C_WIDTHS), axis=-1)
    q = q.reshape(B, L, H_C, DK_C) * (DK_C ** -0.5)
    k = k.reshape(B, L, H_C, DK_C)
    v = v.reshape(B, L, H_C, DV_C)
    logg = (jax.nn.log_sigmoid((a @ w_gate + b_gate).astype(jnp.float32)) / GATE_TAU).reshape(B, L, H_C, DK_C)
    o, s_new = _gla(q, k, v, logg, s0)
    o = _rmsnorm(o.astype(h.dtype), g_norm) * jax.nn.silu(r.reshape(B, L, H_C, DV_C))
    return o.reshape(B, L, MIX_C) @ w_out, s_new.astype(h.dtype)

def _conv_ffn(h, buf, w_up, conv_w, conv_b, w_down):
    L = h.shape[1]
    up = jnp.concatenate([buf.astype(h.dtype), h @ w_up], axis=1)
    y = conv_b
    for i in range(CONV_W):
        y = y + conv_w[i] * up[:, i:i + L]
    a, b = jnp.split(y, 2, axis=-1)
    return (jax.nn.gelu(a) * b) @ w_down, up[:, L:]

def setup_inputs(seed: int = 0) -> dict:
    key = jax.random.key(seed)
    ks = iter(jax.random.split(key, 40))

    def nrm(shape, scale):
        return jax.random.normal(next(ks), shape, jnp.float32) * scale

    n_pages = PAST_LEN // PAGE_SIZE
    n_used = DEC_BATCH * n_pages
    n_phys = n_used + n_used // 4
    page_table = jax.random.permutation(next(ks), n_phys)[:n_used].reshape(DEC_BATCH, n_pages).astype(jnp.int32)
    d_in_ab = sum(AB_WIDTHS)
    d_in_c = sum(C_WIDTHS)
    return {
        'x_prompt': nrm((BATCH, SEQ, D_MODEL), 1.0),
        'x_sample': nrm((DEC_BATCH, DEC_SEQ, D_MODEL), 1.0),
        'cache_k': nrm((N_EVEN, n_phys, PAGE_SIZE, H_B, 2 * DH_B), 1.0),
        'cache_v': nrm((N_EVEN, n_phys, PAGE_SIZE, H_B, DV_B), 1.0),
        'state_ret': nrm((N_EVEN, DEC_BATCH, H_A, DK_A, DV_A), 1.0),
        'state_gla': nrm((N_ODD, DEC_BATCH, H_C, DK_C, DV_C), 1.0),
        'state_conv': nrm((DEPTH, DEC_BATCH, CONV_W - 1, 2 * D_FF), 1.0),
        'page_table': page_table,
        'c_prompt': nrm((BATCH, D_MODEL), 1.0),
        'c_sample': nrm((DEC_BATCH, D_MODEL), 1.0),
        'w_ada': nrm((DEPTH, D_MODEL, 6 * D_MODEL), 0.3 * D_MODEL ** -0.5),
        'b_ada': nrm((DEPTH, 6 * D_MODEL), 0.01),
        'g_pre_mix': 1.0 + nrm((DEPTH, D_MODEL), 0.05),
        'g_post_mix': 1.0 + nrm((DEPTH, D_MODEL), 0.05),
        'g_pre_ffn': 1.0 + nrm((DEPTH, D_MODEL), 0.05),
        'g_post_ffn': 1.0 + nrm((DEPTH, D_MODEL), 0.05),
        'w_in_ab': nrm((N_EVEN, D_MODEL, d_in_ab), D_MODEL ** -0.5),
        'w_out_ab': nrm((N_EVEN, MIX_AB, D_MODEL), MIX_AB ** -0.5),
        'lam_q1': nrm((N_EVEN, DH_B), 0.1),
        'lam_k1': nrm((N_EVEN, DH_B), 0.1),
        'lam_q2': nrm((N_EVEN, DH_B), 0.1),
        'lam_k2': nrm((N_EVEN, DH_B), 0.1),
        'g_diff': 1.0 + nrm((N_EVEN, DV_B), 0.05),
        'w_in_c': nrm((N_ODD, D_MODEL, d_in_c), D_MODEL ** -0.5),
        'w_gate_c': nrm((N_ODD, GATE_RANK, H_C * DK_C), GATE_RANK ** -0.5),
        'b_gate_c': nrm((N_ODD, H_C * DK_C), 0.1),
        'g_gla': 1.0 + nrm((N_ODD, DV_C), 0.05),
        'w_out_c': nrm((N_ODD, MIX_C, D_MODEL), MIX_C ** -0.5),
        'w_up': nrm((DEPTH, D_MODEL, 2 * D_FF), D_MODEL ** -0.5),
        'conv_w': nrm((DEPTH, CONV_W, 2 * D_FF), CONV_W ** -0.5),
        'conv_b': nrm((DEPTH, 2 * D_FF), 0.01),
        'w_down': nrm((DEPTH, D_FF, D_MODEL), D_FF ** -0.5),
    }

def reference(x_prompt, x_sample, cache_k, cache_v, state_ret, state_gla, state_conv, page_table,
              c_prompt, c_sample, w_ada, b_ada, g_pre_mix, g_post_mix, g_pre_ffn, g_post_ffn,
              w_in_ab, w_out_ab, lam_q1, lam_k1, lam_q2, lam_k2, g_diff,
              w_in_c, w_gate_c, b_gate_c, g_gla, w_out_c, w_up, conv_w, conv_b, w_down):
    pos_p = jnp.arange(SEQ)
    pos_s = PAST_LEN + jnp.arange(DEC_SEQ)
    xp, xs = x_prompt, x_sample
    k_p, v_p, k_s, v_s, ret_p, ret_s, gla_p, gla_s, conv_p, conv_s = ([] for _ in range(10))
    for l in range(DEPTH):
        mp = _adaln(c_prompt, w_ada[l], b_ada[l])
        ms = _adaln(c_sample, w_ada[l], b_ada[l])
        hp = _modulate(xp, g_pre_mix[l], mp[0], mp[1])
        hs = _modulate(xs, g_pre_mix[l], ms[0], ms[1])
        if l % 2 == 0:
            e = l // 2
            lam_init = 0.8 - 0.6 * math.exp(-0.3 * l)
            lam = (jnp.exp(jnp.sum(lam_q1[e].astype(jnp.float32) * lam_k1[e].astype(jnp.float32)))
                   - jnp.exp(jnp.sum(lam_q2[e].astype(jnp.float32) * lam_k2[e].astype(jnp.float32))) + lam_init)
            s0 = jnp.zeros((BATCH, H_A, DK_A, DV_A), jnp.float32)
            yp, sp, kp_new, vp_new = _ab_mixer(hp, pos_p, s0, None, None, w_in_ab[e], w_out_ab[e],
                                               lam, lam_init, g_diff[e])
            k_past = cache_k[e][page_table].reshape(DEC_BATCH, PAST_LEN, H_B, 2, DH_B)
            v_past = cache_v[e][page_table].reshape(DEC_BATCH, PAST_LEN, H_B, DV_B)
            ys, ss, ks_new, vs_new = _ab_mixer(hs, pos_s, state_ret[e], k_past, v_past, w_in_ab[e], w_out_ab[e],
                                               lam, lam_init, g_diff[e])
            k_p.append(kp_new)
            v_p.append(vp_new)
            k_s.append(ks_new)
            v_s.append(vs_new)
            ret_p.append(sp)
            ret_s.append(ss)
        else:
            o = l // 2
            s0 = jnp.zeros((BATCH, H_C, DK_C, DV_C), jnp.float32)
            yp, sp = _gla_mixer(hp, s0, w_in_c[o], w_gate_c[o], b_gate_c[o], g_gla[o], w_out_c[o])
            ys, ss = _gla_mixer(hs, state_gla[o], w_in_c[o], w_gate_c[o], b_gate_c[o], g_gla[o], w_out_c[o])
            gla_p.append(sp)
            gla_s.append(ss)
        xp = _residual(xp, yp, g_post_mix[l], mp[2])
        xs = _residual(xs, ys, g_post_mix[l], ms[2])
        hp = _modulate(xp, g_pre_ffn[l], mp[3], mp[4])
        hs = _modulate(xs, g_pre_ffn[l], ms[3], ms[4])
        buf_p = jnp.zeros((BATCH, CONV_W - 1, 2 * D_FF), hp.dtype)
        fp, cbp = _conv_ffn(hp, buf_p, w_up[l], conv_w[l], conv_b[l], w_down[l])
        fs, cbs = _conv_ffn(hs, state_conv[l], w_up[l], conv_w[l], conv_b[l], w_down[l])
        conv_p.append(cbp)
        conv_s.append(cbs)
        xp = _residual(xp, fp, g_post_ffn[l], mp[5])
        xs = _residual(xs, fs, g_post_ffn[l], ms[5])
    return (xp, xs, jnp.stack(k_p), jnp.stack(v_p), jnp.stack(k_s), jnp.stack(v_s),
            jnp.stack(ret_p), jnp.stack(ret_s), jnp.stack(gla_p), jnp.stack(gla_s),
            jnp.stack(conv_p), jnp.stack(conv_s))


_drawn_inputs = setup_inputs


def setup_inputs(seed=0):
    import zlib

    import numpy as np

    out = dict(_drawn_inputs(seed))
    spreads = {}
    factors = {'g_post_mix': 3.644,
     'g_post_ffn': 4.446,
     'lam_q2': 7.634,
     'lam_k2': 5.241,
     'g_diff': 4.716,
     'g_gla': 7.182,
     'conv_b': 8.0}
    for name, (base, spread) in spreads.items():
        noise = np.random.default_rng([zlib.crc32(name.encode()), seed]).standard_normal(out[name].shape)
        drawn = base * np.exp(spread * noise) if base else spread * noise
        out[name] = jnp.asarray(drawn.astype(out[name].dtype))
    for name, factor in factors.items():
        out[name] = (out[name] * factor).astype(out[name].dtype)
    return out
```

```python
from contextlib import ExitStack

import numpy as np
import concourse.bass as bass
from concourse import mybir

F32 = mybir.dt.float32
F32R = mybir.dt.float32r
I32 = mybir.dt.int32
ALU = mybir.AluOpType
ACT = mybir.ActivationFunctionType
AX = mybir.AxisListType

P = 128
D = 1024
KB = D // P
SEQ = 1024
NB = 8
NS = 4
TS = NB * NS
T = SEQ + TS
NT = 3
TT = T // NT
PT = SEQ - 2 * TT
CH = 128
NCH = SEQ // CH
TILES = NCH + 1
H = 4
DV = 128
PAST = 2048
PAGE = 128
NPG = PAST // PAGE
FB = 22
UW = KB * P
GW = 256
EPS = 1e-6
TAU = 16.0
LAM_INIT = 0.2
NEG = -1e30
C9 = 1 + NB
NMOD = 6 * KB
LEVELS = [64, 32, 16, 8, 4, 2, 1]

def const_columns():
    at, n = {}, 0
    for name, w in (("ident", P), ("causal", P), ("decay", H * P), ("decq", H * P), ("deck", H),
                    ("decc", 2), ("cos", TILES * 32), ("sin", TILES * 64), ("sdecay", H * TS),
                    ("sdecq", H * TS), ("sdeck", H), ("sdecc", 2), ("smask", NS), ("sel", H * NS),
                    ("bmask", NB), ("maps", 2)):
        at[name] = (n, n + w)
        n += w
    return at, n


CONST, NCONST = const_columns()
VEC = {}
NVEC = 0
for _n, _w in (("b_ada", 2 * NMOD), ("g_pre_mix", 2 * KB), ("g_post_mix", 2 * KB), ("g_pre_ffn", 2 * KB),
               ("g_post_ffn", 2 * KB), ("g_diff", 1), ("g_gla", 2), ("b_gate", 4), ("conv_b", 4 * FB),
               ("conv_w", 12 * FB)):
    VEC[_n] = (NVEC, NVEC + _w)
    NVEC += _w


class Kit:

    def __init__(self, nc, stack, tag, spare=None):
        self.nc, self.stack, self.tag, self.spare, self.used = nc, stack, tag, spare, 0

    def sb(self, name, shape, dt=F32):
        n = int(np.prod(shape[1:]))
        if self.spare is not None and dt != F32R and self.used + n <= self.spare.shape[1]:
            view = self.spare[0:shape[0], self.used:self.used + n]
            self.used += n
            if dt != F32:
                view = view.bitcast(dt)
            names = "abcd"[:len(shape) - 1]
            return view.rearrange(f"p ({' '.join(names)}) -> p {' '.join(names)}",
                                  **dict(zip(names[1:], shape[2:]))) if len(shape) > 2 else view
        return self.stack.enter_context(self.nc.sbuf_tensor(f"{self.tag}_{name}", shape, dt))

    def ps(self, name, shape, dt=F32):
        return self.stack.enter_context(self.nc.psum_tensor(f"{self.tag}_{name}", shape, dt))

    taken = []

    def sem(self, name):
        Kit.taken.append(self.nc.alloc_semaphore(f"{self.tag}_{name}"))
        return Kit.taken[-1]


def recycle_semaphores(nc):
    nc.clear_and_free_semaphores(Kit.taken)
    Kit.taken = []
    with nc.Block():
        pass


class Seq:

    def __init__(self, eng, sem):
        self.eng, self.sem, self.n, self.base = eng, sem, 0, 0

    def link(self, ins):
        ins.then_inc(self.sem, 1)
        self.n += 1
        self.eng.wait_ge(self.sem, self.base + self.n)
        return ins


def cols(t, name, table=CONST):
    a, b = table[name]
    return t[:, a:b]


def third(ap, n):
    return ap[:, :, n * TT:(n + 1) * TT]


def bc(ap, shape):
    return ap.to_broadcast(shape)


def stage_load(nc, g, consts, vecs):
    with ExitStack() as stack:
        k = Kit(nc, stack, "load")
        landed = k.sem("landed")
        lam_rows = k.sb("lam_rows", [P, 4, 64])
        prod = k.sb("prod", [P, 2, 64])
        dots = k.sb("dots", [P, 2])
        exps = k.sb("exps", [P, 2])
        ch, ex = k.sem("dve"), k.sem("exp")
        block = stack.enter_context(nc.Block())

        @block.sync
        def _(sp):
            sp.dma_start(g.const[:], consts).then_inc(landed, 16)
            sp.dma_start(g.vec[:], vecs).then_inc(landed, 16)
            for i, v in enumerate(g.lam_in):
                sp.dma_start(lam_rows[:, i, :], v.to_broadcast([P, 64])).then_inc(landed, 16)

        @block.vector
        def _(dve):
            nc.vector.memset(g.ones[:], 1.0)
            nc.vector.memset(g.eps[:], EPS)
            dve.wait_ge(landed, 96)
            chain = Seq(dve, ch)
            for i in range(2):
                chain.link(nc.vector.tensor_tensor(prod[:, i, :], lam_rows[:, 2 * i, :], lam_rows[:, 2 * i + 1, :],
                                                   ALU.mult))
            chain.link(nc.vector.tensor_reduce(out=dots[:], in_=prod[:], axis=AX.X, op=ALU.add))
            gd = g.vcol("g_diff")
            chain.link(nc.vector.tensor_scalar(gd, gd, 1.0 - LAM_INIT, None, ALU.mult))
            dve.wait_ge(ex, 1)
            chain.link(nc.vector.tensor_tensor(g.lam[:, 0:1], exps[:, 0:1], exps[:, 1:2], ALU.subtract))
            chain.link(nc.vector.tensor_scalar(g.lam[:, 1:2], g.lam[:, 0:1], LAM_INIT, -1.0, ALU.add, ALU.mult))

        @block.scalar
        def _(act):
            act.wait_ge(ch, 3)
            nc.scalar.activation(exps[:], dots[:], ACT.Exp).then_inc(ex, 1)


def stage_ada(nc, g, w_ada, cT_dram):
    NC_ = 12
    with ExitStack() as stack:
        k = Kit(nc, stack, "ada")
        cT = k.sb("cT", [P, KB, C9])
        sT = k.sb("sT", [P, KB, C9])
        w = [k.sb(f"w{i}", [P, KB, 512]) for i in range(4)]
        rows = [k.sb(f"rows{i}", [C9, 512]) for i in range(2)]
        acc = [k.ps(f"acc{i}", [C9, 512]) for i in range(2)]
        modp = k.ps("modp", [P, 2, 512])
        c_in = k.sem("c_in")
        silu = k.sem("silu")
        w_in = [k.sem(f"w_in{i}") for i in range(4)]
        mm, ev, tr, dv = k.sem("mm"), k.sem("ev"), k.sem("tr"), k.sem("dv")
        block = stack.enter_context(nc.Block())
        n_all = 2 * NC_

        @block.sync
        def _(sp):
            sp.dma_start(cT[:], cT_dram).then_inc(c_in, 16)
            for i in range(4):
                sp.dma_start(w[i][:], w_ada[i]).then_inc(w_in[i], 16)
            with sp.Fori(1, n_all // 4) as j:
                for i in range(4):
                    sp.wait_ge(mm, j * 4 + (i - 3))
                    sp.dma_start(w[i][:], w_ada[j * 4 + i]).then_inc(w_in[i], 16)

        @block.scalar
        def _(act):
            act.wait_ge(c_in, 16)
            nc.scalar.activation(sT[:], cT[:], ACT.Silu).then_inc(silu, 1)
            for n in range(n_all):
                act.wait_ge(mm, n + 1)
                if n >= 2:
                    act.wait_ge(tr, n - 1)
                nc.scalar.activation(rows[n % 2][:], acc[n % 2][:], ACT.Copy).then_inc(ev, 1)

        @block.tensor
        def _(pe):
            pe.wait_ge(silu, 1)

            def turn(n):
                pe.wait_ge(ev, n + 1)
                for j in range(4):
                    l, b = divmod(n * 4 + j, NMOD)
                    last = nc.tensor.transpose(modp[:, l, b * C9:(b + 1) * C9], rows[n % 2][:, j * P:(j + 1) * P],
                                               g.ident()[0:C9, 0:C9])
                last.then_inc(tr, 1)

            for n in range(n_all):
                pe.wait_ge(w_in[n % 4], 16 * (n // 4 + 1))
                if n >= 2:
                    pe.wait_ge(ev, n - 1)
                for kk in range(KB):
                    last = nc.tensor.matmul(acc[n % 2][:], sT[:, kk, :], w[n % 4][:, kk, :],
                                            start=(kk == 0), stop=(kk == KB - 1))
                last.then_inc(mm, 1)
                if n >= 1:
                    turn(n - 1)
            turn(n_all - 1)

        @block.vector
        def _(dve):
            chain = Seq(dve, dv)
            dve.wait_ge(tr, n_all)
            for l in range(2):
                a = VEC["b_ada"][0] + l * NMOD
                chain.link(nc.vector.tensor_tensor(
                    g.mod[:, l], modp[:, l, 0:NMOD * C9].rearrange("p (b c) -> p b c", c=C9),
                    bc(g.vec[:, a:a + NMOD].rearrange("p (b c) -> p b c", c=1), [P, NMOD, C9]), ALU.add))
            for l in range(2):
                for part, name in ((1, "g_pre_mix"), (4, "g_pre_ffn")):
                    m = g.mod[:, l, part * KB:(part + 1) * KB, :]
                    chain.link(nc.vector.tensor_scalar(m, m, 1.0, None, ALU.add))
                for part, name in ((1, "g_pre_mix"), (2, "g_post_mix"), (4, "g_pre_ffn"), (5, "g_post_ffn")):
                    m = g.mod[:, l, part * KB:(part + 1) * KB, :]
                    a = VEC[name][0] + l * KB
                    chain.link(nc.vector.tensor_tensor(
                        m, m, bc(g.vec[:, a:a + KB].rearrange("p (b c) -> p b c", c=1), [P, KB, C9]), ALU.mult))


def stage_norm(nc, g, tag, spare, y, post, pre, x_in, x_out):
    with ExitStack() as stack:
        k = Kit(nc, stack, tag, spare)
        x = [k.sb(f"x{i}", [P, KB, TT]) for i in range(2)]
        sq = k.sb("sq", [P, KB, TT])
        hf = k.sb("hf", [P, KB, TT])
        root = k.sb("root", [P, TT])
        rstd = k.sb("rstd", [P, TT])
        ss = k.ps("ss", [P, 512])
        x_landed = [k.sem(f"x_landed{i}") for i in range(2)]
        x_stored = [k.sem(f"x_stored{i}") for i in range(2)]
        squared, summed, logged, rooted, dv, hfd, hid = (
            k.sem(s) for s in ("squared", "summed", "logged", "rooted", "dve", "hf", "hi"))
        block = stack.enter_context(nc.Block())
        per = (1 if y is not None else 0) + (1 if pre is not None else 0)

        def mod(spec, off):
            l, part = spec
            return g.mod[:, l, (part + off) * KB:(part + off + 1) * KB, :]

        done = {}

        @block.vector
        def _(dve):
            chain = Seq(dve, dv)

            def normalise(n, out, in_):
                dve.wait_ge(rooted, n + 1)
                chain.link(nc.vector.tensor_tensor(out, in_, bc(rstd[:, None, :], [P, KB, TT]), ALU.mult))
                done[("r", n)] = chain.n

            norm = 0
            for n in range(NT):
                xs = x[n % 2]
                pc = TT if n < NT - 1 else PT
                if y is not None:
                    ys = third(y, n)
                    normalise(norm, ys, ys)
                    norm += 1
                    dve.wait_ge(x_landed[n % 2], 16 * (n // 2 + 1))
                    for b in range(KB):
                        last = nc.vector.scalar_tensor_tensor(
                            out=xs[:, b, 0:pc], in0=ys[:, b, 0:pc], scalar=mod(post, 0)[:, b, 0:1],
                            in1=xs[:, b, 0:pc], op0=ALU.mult, op1=ALU.add)
                    if n == NT - 1:
                        sy = ys[:, :, PT:TT].rearrange("p b (c t) -> p b c t", t=NS)
                        sx = xs[:, :, PT:TT].rearrange("p b (c t) -> p b c t", t=NS)
                        gate = bc(mod(post, 0)[:, :, 1:C9].rearrange("p b (c t) -> p b c t", t=1), [P, KB, NB, NS])
                        chain.link(nc.vector.tensor_tensor(sy, sy, gate, ALU.mult))
                        last = nc.vector.tensor_tensor(sx, sx, sy, ALU.add)
                    chain.link(last)
                    done[("x", n)] = chain.n
                if pre is not None:
                    if y is None:
                        dve.wait_ge(x_landed[n % 2], 16 * (n // 2 + 1))
                    if n >= 1:
                        dve.wait_ge(hid, n)
                    normalise(norm, hf[:], xs[:])
                    norm += 1
                    done[("t", n)] = chain.n
                    if n == NT - 1:
                        sh = hf[:, :, PT:TT].rearrange("p b (c t) -> p b c t", t=NS)
                        for off, op in ((1, ALU.mult), (0, ALU.add)):
                            v = bc(mod(pre, off)[:, :, 1:C9].rearrange("p b (c t) -> p b c t", t=1), [P, KB, NB, NS])
                            chain.link(nc.vector.tensor_tensor(sh, sh, v, op))
                    done[("s", n)] = chain.n
                    dve.wait_ge(hid, n + 1)
                    chain.link(nc.vector.tensor_tensor(third(g.alo, n), hf[:], third(g.ahi, n).bitcast(F32),
                                                       ALU.subtract))
                    done[("lo", n)] = chain.n

        def store(sp, n):
            sp.wait_ge(dv, done[("x", n)])
            sp.dma_start(x_out[:, :, n * TT:(n + 1) * TT], x[n % 2][:]).then_inc(x_stored[n % 2], 16)

        @block.sync
        def _(sp):
            for n in range(NT):
                if n >= 2:
                    if y is not None:
                        sp.wait_ge(x_stored[n % 2], 16 * (n // 2))
                    if pre is not None:
                        sp.wait_ge(dv, done[("t", n - 2)])
                sp.dma_start(x[n % 2][:], x_in[:, :, n * TT:(n + 1) * TT]).then_inc(x_landed[n % 2], 16)
                if y is not None and n >= 1:
                    store(sp, n - 1)
            if y is not None:
                store(sp, NT - 1)
                for i in range(2):
                    sp.wait_ge(x_stored[i], 16 * ((NT - i + 1) // 2))

        @block.scalar
        def _(act):
            norm = 0

            def square(src):
                nonlocal norm
                if norm:
                    act.wait_ge(summed, norm)
                nc.scalar.activation(sq[:], src, ACT.Square).then_inc(squared, 1)
                act.wait_ge(summed, norm + 1)
                nc.scalar.activation(root[:], ss[:, 0:TT], ACT.Ln, scale=1.0 / D, bias=g.eps[:, 0:1]).then_inc(logged, 1)
                act.wait_ge(logged, norm + 1)
                if norm:
                    act.wait_ge(dv, done[("r", norm - 1)])
                nc.scalar.activation(rstd[:], root[:], ACT.Exp, scale=-0.5).then_inc(rooted, 1)
                norm += 1

            for n in range(NT):
                pc = TT if n < NT - 1 else PT
                if y is not None:
                    square(third(y, n))
                    act.wait_ge(dv, done[("x", n)])
                else:
                    act.wait_ge(x_landed[n % 2], 16 * (n // 2 + 1))
                if pre is not None:
                    square(x[n % 2][:])
                    act.wait_ge(dv, done[("s", n)])
                    for b in range(KB):
                        last = nc.scalar.activation(hf[:, b, 0:pc], hf[:, b, 0:pc], ACT.Identity,
                                                    scale=mod(pre, 1)[:, b, 0:1], bias=mod(pre, 0)[:, b, 0:1])
                    last.then_inc(hfd, 1)
                    act.wait_ge(hfd, n + 1)
                    nc.scalar.activation(third(g.ahi, n), hf[:], ACT.Copy).then_inc(hid, 1)

        @block.tensor
        def _(pe):
            for n in range(NT * per):
                pe.wait_ge(squared, n + 1)
                if n:
                    pe.wait_ge(rooted, n)
                for b in range(KB):
                    last = nc.tensor.matmul(ss[:, 0:TT], g.ones[:], sq[:, b, :], start=(b == 0), stop=(b == KB - 1))
                last.then_inc(summed, 1)


def split_units(nc, pool, g, n_pairs, st, hi, lo, landed, made, freed, free_at, pool_chain):
    with pool.Fori(0, n_pairs) as i:
        for u in range(2):
            pool.wait_ge(landed[u], i * 16 + 16)
            pool.wait_ge(freed, free_at(i, u))
            shape = [P, st[u].shape[1]]
            nc.gpsimd.tensor_tensor(hi[u][:], st[u][:], bc(g.ones[:, 0:1], shape), ALU.mult).then_inc(pool_chain, 1)
            pool.wait_ge(pool_chain, i * 2 + (u + 1))
            nc.gpsimd.tensor_tensor(lo[u][:], st[u][:], hi[u][:].bitcast(F32), ALU.subtract).then_inc(made, 1)


def three_passes(nc, out, whi, wlo, xhi, xlo, nk):
    n = 0
    for kk in range(nk):
        for a, b in ((whi, xhi), (whi, xlo), (wlo, xhi)):
            last = nc.tensor.matmul(out, a(kk), b(kk), start=(n == 0), stop=(n == 3 * nk - 1))
            n += 1
    return last


def stage_linear(nc, g, tag, w, sections):
    n_units = sum(s[0] for s in sections)
    with ExitStack() as stack:
        k = Kit(nc, stack, tag)
        st = [k.sb(f"st{i}", [P, UW]) for i in range(2)]
        hi = [k.sb(f"hi{i}", [P, UW], F32R) for i in range(2)]
        lo = [k.sb(f"lo{i}", [P, UW], F32R) for i in range(2)]
        acc = [k.ps(f"acc{i}", [P, NT, 512]) for i in range(2)]
        landed = [k.sem(f"landed{i}") for i in range(2)]
        made, used, taken, pc = k.sem("made"), k.sem("used"), k.sem("taken"), k.sem("pool")
        block = stack.enter_context(nc.Block())

        @block.sync
        def _(sp):
            for u in range(2):
                sp.dma_start(st[u][:], w[u]).then_inc(landed[u], 16)
            with sp.Fori(1, n_units // 2) as i:
                for u in range(2):
                    sp.wait_ge(made, i * 2 + (u - 1))
                    sp.dma_start(st[u][:], w[i * 2 + u]).then_inc(landed[u], 16)

        @block.gpsimd
        def _(pool):
            split_units(nc, pool, g, n_units // 2, st, hi, lo, landed, made, used,
                        lambda i, u: i * 2 + (u + 1), pc)

        @block.tensor
        def _(pe):
            pe.sem_inc(used, 2)
            with pe.Fori(0, n_units // 2) as i:
                for u in range(2):
                    pe.wait_ge(made, i * 2 + (u + 1))
                    pe.wait_ge(taken, i * 2 + (u + 1))
                    for n in range(NT):
                        last = three_passes(nc, acc[u][:, n, 0:TT],
                                            lambda kk: hi[u][:, kk * P:(kk + 1) * P],
                                            lambda kk: lo[u][:, kk * P:(kk + 1) * P],
                                            lambda kk: third(g.ahi, n)[:, kk, :],
                                            lambda kk: third(g.alo, n)[:, kk, :], KB)
                    last.then_inc(used, 1)

        @block.scalar
        def _(act):
            act.sem_inc(taken, 2)
            at = 0
            for count, evacuate in sections:
                with act.Fori(at // 2, (at + count) // 2) as i:
                    for u in range(2):
                        act.wait_ge(used, i * 2 + (u + 3))
                        evacuate(i * 2 + (u - at), acc[u][:, :, 0:TT]).then_inc(taken, 1)
                at += count


class State:

    def __init__(self, nc, stack):
        def sb(name, shape, dt=F32):
            return stack.enter_context(nc.sbuf_tensor(name, shape, dt))

        self.const = sb("const", [P, NCONST])
        self.vec = sb("vec", [P, NVEC])
        self.ones = sb("ones", [P, P])
        self.eps = sb("eps", [P, 1])
        self.lam = sb("lam", [P, 2])
        self.mod = sb("mod", [P, 2, NMOD, C9])



    def col(self, name):
        return cols(self.const, name)

    def ident(self):
        return cols(self.const, "ident")

    def vcol(self, name):
        return cols(self.vec, name, VEC)

    def conv(self, l, c):
        cw, cb = VEC["conv_w"][0] + l * 2 * FB * 3, VEC["conv_b"][0] + l * 2 * FB
        return (lambda tap: self.vec[:, bass.ds(c * 3 + (cw + tap), 1)]), self.vec[:, bass.ds(c + cb, 1)]


def by_thirds(ap):
    return ap.rearrange("p o (n t) -> p (o n) t", n=NT)


def stage_project(nc, g, tag, spare, w, n_groups, rotate, dst, out):
    with ExitStack() as stack:
        k = Kit(nc, stack, tag, spare)
        GU = KB * GW
        st = [k.sb(f"st{i}", [P, GU]) for i in range(2)]
        hi = [k.sb(f"hi{i}", [P, GU], F32R) for i in range(2)]
        lo = [k.sb(f"lo{i}", [P, GU], F32R) for i in range(2)]
        NR = 3
        res = [k.sb(f"res{i}", [P, GW]) for i in range(NR)]
        acc = [k.ps(f"acc{i}", [P, 512]) for i in range(NR)]
        landed = [k.sem(f"landed{i}") for i in range(2)]
        stored = [k.sem(f"stored{i}") for i in range(NR)]
        made, used, summed, pc = k.sem("made"), k.sem("used"), k.sem("summed"), k.sem("pool")
        ready, turned, copied = k.sem("ready"), k.sem("turned"), k.sem("copied")
        if rotate:
            xc = k.sb("xc", [P, GW])
            xs = k.sb("xs", [P, GW])
            turn = [k.ps(f"turn{i}", [P, 2, P]) for i in range(2)]
            rc = k.sem("rc")
        block = stack.enter_context(nc.Block())
        rows = [P] * NCH + [TS]
        DEPTH = 2 * TILES

        @block.sync
        def _(sp):
            for u in range(2):
                sp.dma_start(st[u][:], w[u]).then_inc(landed[u], 16)
            if n_groups > 2:
                with sp.Fori(1, n_groups // 2) as i:
                    for u in range(2):
                        sp.wait_ge(made, i * 2 + (u - 1))
                        sp.dma_start(st[u][:], w[i * 2 + u]).then_inc(landed[u], 16)

        @block.gpsimd
        def _(pool):
            split_units(nc, pool, g, n_groups // 2, st, hi, lo, landed, made, summed,
                        lambda i, u: i * DEPTH + (u + 1) * TILES, pc)

        @block.tensor
        def _(pe):
            pe.sem_inc(summed, DEPTH)

            def transposes(i, q):
                pe.wait_ge(ready, i * DEPTH + (q + 1 + NR))
                pe.wait_ge(copied, i * DEPTH + (q + 1))
                for j in range(2):
                    last = nc.tensor.transpose(turn[q % 2][:, j, :], res[q % NR][:, j * P:(j + 1) * P], g.ident())
                last.then_inc(turned, 1)

            with pe.Fori(0, n_groups // 2) as i:
                for q in range(DEPTH):
                    u, t = divmod(q, TILES)
                    r = rows[t]
                    if t == 0:
                        pe.wait_ge(made, i * 2 + (u + 1))
                    pe.wait_ge(ready, i * DEPTH + (q + 1))
                    last = three_passes(nc, acc[q % NR][0:r, 0:GW],
                                        lambda kk: g.ahi[:, kk, t * P:t * P + r],
                                        lambda kk: g.alo[:, kk, t * P:t * P + r],
                                        lambda kk: hi[u][:, kk * GW:(kk + 1) * GW],
                                        lambda kk: lo[u][:, kk * GW:(kk + 1) * GW], KB)
                    last.then_inc(summed, 1)
                    if rotate and q >= 1:
                        transposes(i, q - 1)
                if rotate:
                    transposes(i, DEPTH - 1)

        if rotate:
            @block.vector
            def _(dve):
                dve.sem_inc(ready, NR)
                with dve.Fori(0, n_groups // 2) as i:
                    for q in range(DEPTH):
                        t = q % TILES
                        r = rows[t]
                        x = acc[q % NR][0:r, 0:GW].rearrange("p (h m d) -> p h m d", h=4, m=2)
                        c4 = xc[0:r].rearrange("p (h m d) -> p h m d", h=4, m=2)
                        s4 = xs[0:r].rearrange("p (h m d) -> p h m d", h=4, m=2)
                        cos = g.col("cos")[0:r, t * 32:(t + 1) * 32]
                        sin = g.col("sin")[0:r, t * 64:(t + 1) * 64].rearrange("p (m d) -> p m d", m=2)
                        dve.wait_ge(summed, i * DEPTH + (q + 1 + DEPTH))
                        dve.wait_ge(ready, i * DEPTH + (q + NR))
                        nc.vector.tensor_tensor(c4, x, bc(cos[:, None, None, :], [r, 4, 2, 32]), ALU.mult)
                        for m in range(2):
                            last = nc.vector.tensor_tensor(s4[:, :, m, :], x[:, :, 1 - m, :],
                                                           bc(sin[:, None, m, :], [r, 4, 32]), ALU.mult)
                        last.then_inc(rc, 1)
                        dve.wait_ge(rc, i * DEPTH + (q + 1))
                        dve.wait_ge(stored[q % NR], (i * (DEPTH // NR) + (q // NR + 1)) * 16)
                        dve.wait_ge(turned, i * DEPTH + (q + 1))
                        nc.vector.tensor_tensor(res[q % NR][0:r], xc[0:r], xs[0:r], ALU.add).then_inc(ready, 1)

        @block.scalar
        def _(act):
            for s in range(NR):
                act.sem_inc(stored[s], 16)
            act.sem_inc(copied, 2)
            if rotate:
                act.sem_inc(turned, NR)
            else:
                act.sem_inc(ready, NR)
            with act.Fori(0, n_groups // 2) as i:
                for q in range(DEPTH):
                    u, t = divmod(q, TILES)
                    r = rows[t]
                    if not rotate:
                        act.wait_ge(summed, i * DEPTH + (q + 1 + DEPTH))
                        act.wait_ge(stored[q % NR], (i * (DEPTH // NR) + (q // NR + 1)) * 16)
                        nc.scalar.activation(res[q % NR][0:r], acc[q % NR][0:r, 0:GW], ACT.Copy).then_inc(ready, 1)
                    act.wait_ge(ready, i * DEPTH + (q + 1 + NR))
                    act.dma_start(out[bass.ds(i * 2 + u, 1), t * P:t * P + r, :].rearrange("o p n -> p o n"),
                                  res[q % NR][0:r, None, :]).then_inc(stored[q % NR], 16)
                    if rotate:
                        act.wait_ge(turned, i * DEPTH + (q + 1 + NR))
                        nc.scalar.activation(dst[:, bass.ds(i * 4 + 2 * u, 2), t * P:t * P + r],
                                             turn[q % 2][:, :, 0:r], ACT.Copy).then_inc(copied, 1)
            for s in range(NR):
                act.wait_ge(stored[s], (n_groups // 2 * (DEPTH // NR) + 1) * 16)


def stage_ffn(nc, g, tag, l, w, y, conv_in, conv_out):
    PAIRS = FB // 2
    with ExitStack() as stack:
        k = Kit(nc, stack, tag)
        NSL = 3
        st = [k.sb(f"st{i}", [P, UW]) for i in range(2)]
        hi = [k.sb(f"hi{i}", [P, UW], F32R) for i in range(NSL)]
        lo = [k.sb(f"lo{i}", [P, UW], F32R) for i in range(NSL)]
        HIST = SEQ + 2
        UC = HIST + NB * (NS + 2)
        up = [k.sb(f"up{i}", [P, UC]) for i in range(2)]
        cv = [k.sb(f"cv{i}", [P, UC]) for i in range(2)]
        ghi = [k.sb(f"ghi{j}", [P, T], F32R) for j in range(2)]
        glo = [k.sb(f"glo{j}", [P, T], F32R) for j in range(2)]
        cin = k.sb("cin", [P, 2 * FB, NB, 2])
        cout = k.sb("cout", [P, 2 * FB, 2 * C9])
        acc = [k.ps(f"acc{i}", [P, NT, 512]) for i in range(2)]
        landed = [k.sem(f"landed{i}") for i in range(2)]
        made, used, pc = k.sem("made"), k.sem("used"), k.sem("pool")
        up_taken, down_taken, down_summed = k.sem("up_taken"), k.sem("down_taken"), k.sem("down_summed")
        cin_in, cout_out, affine, gelued, hid = (k.sem(x) for x in ("cin", "cout", "affine", "gelu", "hi"))
        conv = [k.sem(f"conv{i}") for i in range(2)]
        tap, prod, lod, zeroed = k.sem("tap"), k.sem("prod"), k.sem("lo"), k.sem("zeroed")
        block = stack.enter_context(nc.Block())

        def samples(t):
            return t[:, HIST:UC].rearrange("p (b c) -> p b c", c=NS + 2)

        @block.sync
        def _(sp):
            sp.dma_start(cin[:], conv_in).then_inc(cin_in, 16)
            for u in range(2):
                sp.dma_start(st[u][:], w[u]).then_inc(landed[u], 16)
            with sp.Fori(1, PAIRS * 3) as i:
                for u in range(2):
                    sp.wait_ge(made, i * 2 + (u - 1))
                    sp.dma_start(st[u][:], w[i * 2 + u]).then_inc(landed[u], 16)
            sp.wait_ge(up_taken, 2 * FB)
            sp.wait_ge(affine, 2 * FB)
            sp.dma_start(conv_out, cout[:]).then_inc(cout_out, 16)
            sp.wait_ge(cout_out, 16)

        @block.gpsimd
        def _(pool):
            with pool.Fori(0, PAIRS) as i:
                for u in range(6):
                    pool.wait_ge(landed[u % 2], i * 48 + 16 * (u // 2 + 1))
                    pool.wait_ge(used, i * 6 + (u + 1))
                    nc.gpsimd.tensor_tensor(hi[u % NSL][:], st[u % 2][:], bc(g.ones[:, 0:1], [P, UW]),
                                            ALU.mult).then_inc(pc, 1)
                    pool.wait_ge(pc, i * 6 + (u + 1))
                    nc.gpsimd.tensor_tensor(lo[u % NSL][:], st[u % 2][:], hi[u % NSL][:].bitcast(F32),
                                            ALU.subtract).then_inc(made, 1)

        @block.tensor
        def _(pe):
            pe.sem_inc(used, NSL)

            def up_unit(s, a, made_at, wait_sem, wait_at):
                pe.wait_ge(made, made_at)
                if wait_sem is not None:
                    pe.wait_ge(wait_sem, wait_at)
                for n in range(NT):
                    last = three_passes(nc, acc[a][:, n, 0:TT],
                                        lambda kk: hi[s][:, kk * P:(kk + 1) * P],
                                        lambda kk: lo[s][:, kk * P:(kk + 1) * P],
                                        lambda kk: third(g.ahi, n)[:, kk, :],
                                        lambda kk: third(g.alo, n)[:, kk, :], KB)
                last.then_inc(used, 1)

            def down(i, s0, s1, made_at, up_at, down_at):
                pe.wait_ge(made, made_at)
                pe.wait_ge(lod, i * 2)
                for m in range(KB):
                    if m < 2:
                        pe.wait_ge(up_taken, up_at + (m - 1))
                    else:
                        pe.wait_ge(down_taken, down_at + (m - 1))
                    for n in range(NT):
                        last = three_passes(nc, acc[m % 2][:, n, 0:TT],
                                            lambda j: hi[(s0, s1)[j]][:, m * P:(m + 1) * P],
                                            lambda j: lo[(s0, s1)[j]][:, m * P:(m + 1) * P],
                                            lambda j: ghi[j][:, n * TT:(n + 1) * TT],
                                            lambda j: glo[j][:, n * TT:(n + 1) * TT], 2)
                    if m < KB - 1:
                        last.then_inc(down_summed, 1)
                    else:
                        last.then_inc(used, 2)

            up_unit(0, 0, 1, None, 0)
            up_unit(1, 1, 2, None, 0)
            up_unit(2, 0, 3, up_taken, 1)
            up_unit(0, 1, 4, up_taken, 2)
            with pe.Fori(1, PAIRS) as i:
                up_unit(1, 0, i * 6 - 1, up_taken, i * 4 - 1)
                up_unit(2, 1, i * 6, up_taken, i * 4)
                down(i, 0, 1, i * 6 + 2, i * 4 + 2, i * 8 - 8)
                up_unit(2, 0, i * 6 + 3, down_taken, i * 8 - 1)
                up_unit(0, 1, i * 6 + 4, down_taken, i * 8)
            down(PAIRS, 1, 2, PAIRS * 6, PAIRS * 4, PAIRS * 8 - 8)

        @block.scalar
        def _(act):
            act.wait_ge(cin_in, 16)

            def hidden(n, j, first, used_a, used_b, down_used):
                for x in range(2):
                    c = n * 2 + x
                    act.wait_ge(used, (used_a, used_b)[x])
                    if not first:
                        act.wait_ge(conv[x], n)
                    nc.scalar.activation(up[x][:, 2:2 + 2 * TT].rearrange("p (n t) -> p n t", n=2),
                                         acc[x][:, 0:2, 0:TT], ACT.Copy)
                    nc.scalar.activation(up[x][:, 2 + 2 * TT:HIST], acc[x][:, 2, 0:PT], ACT.Copy)
                    nc.scalar.activation(samples(up[x])[:, :, 2:], acc[x][:, 2, PT:TT].rearrange(
                        "p (b t) -> p b t", t=NS), ACT.Copy)
                    nc.scalar.activation(samples(up[x])[:, None, :, 0:2], cin[:, bass.ds(c, 1), :, :],
                                         ACT.Copy).then_inc(up_taken, 1)
                    act.wait_ge(up_taken, c + 1)
                    nc.scalar.activation(cout[:, bass.ds(c, 1), 0:2], up[x][:, None, SEQ:HIST], ACT.Copy)
                    nc.scalar.activation(cout[:, bass.ds(c, 1), 2:].rearrange("p o (b t) -> p o b t", t=2),
                                         samples(up[x])[:, None, :, NS:], ACT.Copy)
                    if not first:
                        act.wait_ge(lod if x == 0 else prod, n)
                    wv, bv = g.conv(l, c)
                    nc.scalar.activation(cv[x][:, 2:], up[x][:, 2:], ACT.Identity, scale=wv(2), bias=bv)\
                        .then_inc(affine, 1)
                act.wait_ge(conv[0], n + 1)
                nc.scalar.activation(cv[0][:, 2:], cv[0][:, 2:], ACT.Gelu_apprx_tanh).then_inc(gelued, 1)
                act.wait_ge(prod, n + 1)
                if down_used is not None:
                    act.wait_ge(used, down_used)
                nc.scalar.activation(ghi[j][:, 0:SEQ], cv[0][:, 2:HIST], ACT.Copy)
                nc.scalar.activation(ghi[j][:, SEQ:T].rearrange("p (b t) -> p b t", t=NS),
                                     samples(cv[0])[:, :, 2:], ACT.Copy).then_inc(hid, 1)

            hidden(0, 0, True, 1 + NSL, 2 + NSL, None)
            hidden(1, 1, False, 3 + NSL, 4 + NSL, None)
            with act.Fori(1, PAIRS) as i:
                hidden(i * 2, 0, False, i * 6 + (NSL - 1), i * 6 + NSL, i * 6 + (NSL + 2))
                hidden(i * 2 + 1, 1, False, i * 6 + (NSL + 3), i * 6 + (NSL + 4), None)

        @block.vector
        def _(dve):
            for x in range(2):
                nc.vector.memset(up[x][:, 0:2], 0.0)
            nc.vector.memset(y[:], 0.0).then_inc(zeroed, 1)
            dve.wait_ge(zeroed, 1)

            def taps(n, x):
                wv, _ = g.conv(l, n * 2 + x)
                dve.wait_ge(affine, n * 2 + (x + 1))
                nc.vector.scalar_tensor_tensor(out=cv[x][:, 2:], in0=up[x][:, 1:UC - 1], scalar=wv(1),
                                               in1=cv[x][:, 2:], op0=ALU.mult, op1=ALU.add).then_inc(tap, 1)
                dve.wait_ge(tap, n * 2 + (x + 1))
                nc.vector.scalar_tensor_tensor(out=cv[x][:, 2:], in0=up[x][:, 0:UC - 2], scalar=wv(0),
                                               in1=cv[x][:, 2:], op0=ALU.mult, op1=ALU.add).then_inc(conv[x], 1)

            def gate(n):
                dve.wait_ge(gelued, n + 1)
                dve.wait_ge(conv[1], n + 1)
                nc.vector.tensor_tensor(cv[0][:, 2:], cv[0][:, 2:], cv[1][:, 2:], ALU.mult).then_inc(prod, 1)

            def low(n, j):
                dve.wait_ge(hid, n + 1)
                nc.vector.tensor_tensor(glo[j][:, 0:SEQ], cv[0][:, 2:HIST], ghi[j][:, 0:SEQ].bitcast(F32),
                                        ALU.subtract)
                nc.vector.tensor_tensor(glo[j][:, SEQ:T].rearrange("p (b t) -> p b t", t=NS),
                                        samples(cv[0])[:, :, 2:],
                                        ghi[j][:, SEQ:T].bitcast(F32).rearrange("p (b t) -> p b t", t=NS),
                                        ALU.subtract).then_inc(lod, 1)

            def add(i, m, first_used):
                if m < KB - 1:
                    dve.wait_ge(down_summed, i * 7 + (m - 6))
                else:
                    dve.wait_ge(used, first_used)
                ym = by_thirds(y[:, m:m + 1, :])
                nc.vector.tensor_tensor(ym, ym, acc[m % 2][:, :, 0:TT], ALU.add).then_inc(down_taken, 1)

            for n in range(2):
                taps(n, 0)
                taps(n, 1)
                gate(n)
                low(n, n)
            with dve.Fori(1, PAIRS) as i:
                u = i * 6 + (NSL + 2)
                add(i, 0, u)
                taps(i * 2, 0)
                add(i, 1, u)
                taps(i * 2, 1)
                add(i, 2, u)
                add(i, 3, u)
                gate(i * 2)
                for m in range(4, KB):
                    add(i, m, u)
                low(i * 2, 0)
                taps(i * 2 + 1, 0)
                taps(i * 2 + 1, 1)
                gate(i * 2 + 1)
                low(i * 2 + 1, 1)
            for m in range(KB):
                add(PAIRS, m, PAIRS * 6 + NSL)


QA, QB, KA, KBK = 0, 2, 6, 8
KA_GROUP, VA_GROUP, VB_GROUP = 3, 0, 2


def stage_retention(nc, g, qkT, rot, val, o, state_in, state_out, sstate_out):
    with ExitStack() as stack:
        k = Kit(nc, stack, "ret")
        v = [k.sb(f"v{z}", [P, H, DV]) for z in range(2)]
        kn = [k.sb(f"kn{z}", [P, 256]) for z in range(2)]
        kc = [k.sb(f"kc{z}", [P, 2, CH]) for z in range(2)]
        qz = [k.sb(f"qz{z}", [P, H, CH]) for z in range(2)]
        qd = [k.sb(f"qd{z}", [P, H, CH]) for z in range(2)]
        ks = [k.sb(f"ks{z}", [P, 256]) for z in range(2)]
        sm = [k.sb(f"sm{z}", [P, H, CH]) for z in range(2)]
        S = k.sb("S", [P, 2, DV])
        ps_s = [k.ps(f"ps_s{z}", [P, H, CH]) for z in range(2)]
        ps_o = [k.ps(f"ps_o{z}", [P, H, CH]) for z in range(2)]
        ps_d = k.ps("ps_d", [P, 2, 4 * DV])
        v_in = [k.sem(f"v_in{z}") for z in range(2)]
        zeroed, kcopied, qready, scored, masked = (k.sem(x) for x in ("zeroed", "kcopied", "qready", "scored", "masked"))
        summed, deltaed, stated, copied = (k.sem(x) for x in ("summed", "deltaed", "stated", "copied"))
        state_stored = k.sem("state_stored")
        block = stack.enter_context(nc.Block())

        def v_src(at, n):
            return val[VA_GROUP:VA_GROUP + 2, at, :].rearrange("g p f -> p g f")

        @block.sync
        def _(sp):
            def load(z, at):
                sp.dma_start(v[z][:].rearrange("p (g h) e -> p g (h e)", g=2), v_src(at, CH)).then_inc(v_in[z], 16)
                sp.dma_start(kn[z][:], rot[KA_GROUP, at, :]).then_inc(v_in[z], 16)

            for z in range(2):
                load(z, slice(z * CH, (z + 1) * CH))
            with sp.Fori(1, NCH // 2) as i:
                for z in range(2):
                    sp.wait_ge(deltaed, i * 2 + (z + 1))
                    load(z, bass.ds(i * 2 * CH + z * CH, CH))
            sp.wait_ge(stated, NCH + 1)
            sp.dma_start(state_out, S[:]).then_inc(state_stored, 16)
            sp.wait_ge(state_stored, 16)

        @block.scalar
        def _(act):
            act.sem_inc(copied, 2)
            with act.Fori(0, NCH // 2) as i:
                for z in range(2):
                    act.wait_ge(scored, i * 2 + (z + 1))
                    nc.scalar.activation(kc[z][:], qkT[:, KA:KA + 2, bass.ds(i * 2 * CH + z * CH, CH)],
                                         ACT.Copy).then_inc(kcopied, 1)
                for z in range(2):
                    act.wait_ge(summed, i * 2 + (z + 1))
                    nc.scalar.activation(o[:, 0:H, bass.ds(i * 2 * CH + z * CH, CH)], ps_o[z][:],
                                         ACT.Copy).then_inc(copied, 1)

        @block.tensor
        def _(pe):
            pe.sem_inc(scored, 2)
            pe.sem_inc(deltaed, 2)

            def score(i, z):
                pe.wait_ge(kcopied, i * 2 + (z + 1))
                pe.wait_ge(qready, i * 2 + (z + 1))
                for h in range(H):
                    last = nc.tensor.matmul(ps_s[z][:, h, :], kc[z][:, h // 2, :], qz[z][:, h, :],
                                            start=True, stop=True)
                last.then_inc(scored, 1)

            with pe.Fori(0, NCH // 2) as i:
                for z in range(2):
                    score(i, z)
                for z in range(2):
                    pe.wait_ge(v_in[z], i * 32 + 32)
                    pe.wait_ge(masked, i * 2 + (z + 1))
                    pe.wait_ge(stated, i * 2 + (z + 1))
                    pe.wait_ge(copied, i * 2 + (z + 1))
                    for h in range(H):
                        nc.tensor.matmul(ps_o[z][:, h, :], v[z][:, h, :], sm[z][:, h, :], start=True, stop=False)
                        last = nc.tensor.matmul(ps_o[z][:, h, :], S[:, h // 2, :], qd[z][:, h, :],
                                                start=False, stop=True)
                    last.then_inc(summed, 1)
                    for h in range(H):
                        last = nc.tensor.matmul(ps_d[64 * (h % 2):64 * (h % 2) + 64, 0, (h // 2) * DV:(h // 2 + 1) * DV],
                                                ks[z][:, h * 64:(h + 1) * 64], v[z][:, h, :], start=True, stop=True)
                    last.then_inc(deltaed, 1)

        @block.vector
        def _(dve):
            for z in range(2):
                nc.vector.memset(qz[z][:], 0.0)
            nc.vector.memset(S[:], 0.0).then_inc(zeroed, 1)
            dve.wait_ge(zeroed, 1)
            dve.sem_inc(stated, 1)
            with dve.Fori(0, NCH // 2) as i:
                for z in range(2):
                    at = bass.ds(i * 2 * CH + z * CH, CH)
                    dve.wait_ge(deltaed, i * 2 + (z + 1))
                    for s in range(2):
                        last = nc.vector.tensor_copy(qz[z][64 * s:64 * s + 64, s::2, :],
                                                     qkT[64 * s:64 * s + 64, QA:QA + 2, at])
                    last.then_inc(qready, 1)
                    dve.wait_ge(qready, i * 2 + (z + 1))
                    nc.vector.tensor_tensor(qd[z][:], qz[z][:], g.col("decq").rearrange("p (h i) -> p h i", h=H), ALU.mult)
                    dve.wait_ge(v_in[z], i * 32 + 32)
                    nc.vector.tensor_tensor(ks[z][:].rearrange("p (h d) -> p h d", h=H),
                                            kn[z][:].rearrange("p (h d) -> p h d", h=H),
                                            bc(g.col("deck")[:, :, None], [P, H, 64]), ALU.mult)
                    dve.wait_ge(scored, i * 2 + (z + 3))
                    nc.vector.tensor_tensor(sm[z][:], ps_s[z][:], g.col("decay").rearrange("p (h i) -> p h i", h=H),
                                            ALU.mult).then_inc(masked, 1)
                for z in range(2):
                    dve.wait_ge(deltaed, i * 2 + (z + 3))
                    for b in range(2):
                        last = nc.vector.scalar_tensor_tensor(
                            out=S[:, b, :], in0=S[:, b, :], scalar=g.col("decc")[:, b:b + 1],
                            in1=ps_d[:, 0, b * DV:(b + 1) * DV], op0=ALU.mult, op1=ALU.add)
                    last.then_inc(stated, 1)

    with ExitStack() as stack:
        k = Kit(nc, stack, "rets")
        v = k.sb("v", [TS, H, DV])
        vm = k.sb("vm", [TS, H, NB, DV])
        kn = k.sb("kn", [TS, 256])
        ks = k.sb("ks", [TS, 256])
        qz = k.sb("qz", [P, H, TS])
        qd = k.sb("qd", [P, H, TS])
        sm = k.sb("sm", [TS, H, TS])
        ss = k.sb("ss", [P, NB, 2, DV])
        ps_s = k.ps("ps_s", [TS, H, TS])
        ps_o = k.ps("ps_o", [P, H, TS])
        ps_d = k.ps("ps_d", [P, 2, NB, DV])
        landed, out_done = k.sem("landed"), k.sem("out_done")
        qready, scored, masked, summed, deltaed, stated, dv = (
            k.sem(x) for x in ("qready", "scored", "masked", "summed", "deltaed", "stated", "dv"))
        block = stack.enter_context(nc.Block())

        @block.sync
        def _(sp):
            sp.dma_start(v[:].rearrange("p (g h) e -> p g (h e)", g=2),
                         val[VA_GROUP:VA_GROUP + 2, SEQ:T, :].rearrange("g p f -> p g f")).then_inc(landed, 16)
            sp.dma_start(kn[:], rot[KA_GROUP, SEQ:T, :]).then_inc(landed, 16)
            sp.dma_start(ss[:], state_in).then_inc(landed, 16)
            sp.wait_ge(stated, 1)
            sp.dma_start(sstate_out, ss[:]).then_inc(out_done, 16)
            sp.wait_ge(out_done, 16)

        @block.tensor
        def _(pe):
            pe.wait_ge(qready, 1)
            for h in range(H):
                last = nc.tensor.matmul(ps_s[:, h, :], qkT[:, KA + h // 2, SEQ:T], qz[:, h, :], start=True, stop=True)
            last.then_inc(scored, 1)
            pe.wait_ge(landed, 48)
            pe.wait_ge(masked, 1)
            for h in range(H):
                nc.tensor.matmul(ps_o[:, h, :], v[:, h, :], sm[:, h, :], start=True, stop=False)
                for b in range(NB):
                    last = nc.tensor.matmul(ps_o[:, h, b * NS:(b + 1) * NS], ss[:, b, h // 2, :],
                                            qd[:, h, b * NS:(b + 1) * NS], start=False, stop=(b == NB - 1))
            last.then_inc(summed, 1)
            for h in range(H):
                for n in range(2):
                    last = nc.tensor.matmul(ps_d[64 * (h % 2):64 * (h % 2) + 64, h // 2, n * 4:n * 4 + 4, :],
                                            ks[:, h * 64:(h + 1) * 64], vm[:, h, n * 4:n * 4 + 4, :],
                                            start=True, stop=True)
            last.then_inc(deltaed, 1)

        @block.vector
        def _(dve):
            chain = Seq(dve, dv)
            chain.link(nc.vector.memset(qz[:], 0.0))
            for s in range(2):
                last = nc.vector.tensor_copy(qz[64 * s:64 * s + 64, s::2, :], qkT[64 * s:64 * s + 64, QA:QA + 2, SEQ:T])
            last.then_inc(qready, 1)
            dve.wait_ge(qready, 1)
            nc.vector.tensor_tensor(qd[:], qz[:], g.col("sdecq").rearrange("p (h i) -> p h i", h=H), ALU.mult)
            dve.wait_ge(landed, 48)
            nc.vector.tensor_tensor(ks[:].rearrange("p (h d) -> p h d", h=H), kn[:].rearrange("p (h d) -> p h d", h=H),
                                    bc(g.col("sdeck")[0:TS, :, None], [TS, H, 64]), ALU.mult)
            for b in range(NB):
                nc.vector.tensor_scalar(vm[:, :, b, :], v[:], g.col("bmask")[0:TS, b:b + 1], None, ALU.mult)
            dve.wait_ge(scored, 1)
            nc.vector.tensor_tensor(sm[:], ps_s[:], g.col("sdecay")[0:TS].rearrange("p (h i) -> p h i", h=H),
                                    ALU.mult).then_inc(masked, 1)
            dve.wait_ge(deltaed, 1)
            for b in range(2):
                last = nc.vector.scalar_tensor_tensor(out=ss[:, :, b, :], in0=ss[:, :, b, :],
                                                      scalar=g.col("sdecc")[:, b:b + 1], in1=ps_d[:, b, :, :],
                                                      op0=ALU.mult, op1=ALU.add)
            last.then_inc(stated, 1)

        @block.scalar
        def _(act):
            act.wait_ge(summed, 1)
            nc.scalar.activation(o[:, 0:H, SEQ:T], ps_o[:], ACT.Copy)


def stage_store(nc, tag, pairs):
    with ExitStack() as stack:
        stored = Kit(nc, stack, tag).sem("stored")
        block = stack.enter_context(nc.Block())

        @block.sync
        def _(sp):
            for dst, src in pairs:
                sp.dma_start(dst, src).then_inc(stored, 16)
            sp.wait_ge(stored, 16 * len(pairs))


def stage_attention(nc, g, qkT, val, o):
    SC = 64 ** -0.5
    STEPS = 2 * NCH
    with ExitStack() as stack:
        k = Kit(nc, stack, "att")
        v = [k.sb(f"v{u}", [P, NCH, DV]) for u in range(2)]
        qz = [k.sb(f"qz{z}", [P, 2, CH]) for z in range(2)]
        p = [k.sb(f"p{z}", [P, 2, SEQ]) for z in range(2)]
        aT = [k.sb(f"aT{z}", [P, NCH, CH]) for z in range(2)]
        mx, nm, sums, rs = (k.sb(x, [P, 2]) for x in ("mx", "nm", "sums", "rs"))
        ps_s = k.ps("ps_s", [P, 2, SEQ])
        ps_t = k.ps("ps_t", [P, NCH, CH])
        ps_o = [k.ps(f"ps_o{z}", [P, CH]) for z in range(2)]
        v_in = [k.sem(f"v_in{u}") for u in range(2)]
        zeroed, qready, scored, maxed, exped = (k.sem(x) for x in ("zeroed", "qready", "scored", "maxed", "exped"))
        mixed, turned, aready, summed, copied, dv = (k.sem(x) for x in ("mixed", "turned", "aready", "summed", "copied", "dv"))
        block = stack.enter_context(nc.Block())

        @block.sync
        def _(sp):
            with sp.Fori(0, H // 2) as i:
                for u in range(2):
                    sp.wait_ge(summed, i * STEPS + (u + 1) * NCH)
                    sp.dma_start(v[u][:], val[bass.ds(i + VB_GROUP, 1), 0:SEQ, u * DV:(u + 1) * DV].rearrange(
                        "o (c p) e -> p (o c) e", p=P)).then_inc(v_in[u], 16)

        @block.gpsimd
        def _(pool):
            for z in range(2):
                last = nc.gpsimd.memset(qz[z][:], 0.0)
            last.then_inc(zeroed, 1)
            pool.wait_ge(zeroed, 1)
            with pool.Fori(0, H // 2) as i:
                for s in range(STEPS):
                    u, qb = divmod(s, NCH)
                    pool.wait_ge(scored, i * STEPS + (s + 1))
                    for m in range(2):
                        last = nc.gpsimd.tensor_copy(
                            qz[s % 2][64 * m:64 * m + 64, m:m + 1, :],
                            qkT[64 * m:64 * m + 64, bass.ds(i * 2 + (QB + u), 1), qb * CH:(qb + 1) * CH])
                    last.then_inc(qready, 1)

        @block.tensor
        def _(pe):
            pe.sem_inc(scored, 2)
            pe.sem_inc(summed, STEPS)

            def score(i, s):
                u, qb = divmod(s, NCH)
                pe.wait_ge(qready, i * STEPS + (s + 1))
                pe.wait_ge(exped, i * STEPS + (s + 1))
                for m in range(2):
                    for a in range(0, (qb + 1) * CH, 512):
                        b = min(a + 512, (qb + 1) * CH)
                        last = nc.tensor.matmul(ps_s[:, m, a:b], qz[s % 2][:, m, :],
                                                qkT[:, bass.ds(i * 2 + (KBK + u), 1), a:b].rearrange("p o k -> p (o k)"),
                                                start=True, stop=True)
                last.then_inc(scored, 1)

            def turn(i, s):
                pe.wait_ge(mixed, i * STEPS + (s + 1))
                pe.wait_ge(aready, i * STEPS + (s + 1))
                for j in range(s % NCH + 1):
                    last = nc.tensor.transpose(ps_t[:, j, :], p[s % 2][:, 0, j * CH:(j + 1) * CH], g.ident())
                last.then_inc(turned, 1)

            def product(i, s):
                u, qb = divmod(s, NCH)
                if qb == 0:
                    pe.wait_ge(v_in[u], i * 16 + 16)
                pe.wait_ge(aready, i * STEPS + (s + 2))
                pe.wait_ge(copied, i * STEPS + (s + 1))
                for j in range(qb + 1):
                    last = nc.tensor.matmul(ps_o[s % 2][:], v[u][:, j, :], aT[s % 2][:, j, :],
                                            start=(j == 0), stop=(j == qb))
                last.then_inc(summed, 1)

            with pe.Fori(0, H // 2) as i:
                for s in range(STEPS + 2):
                    if s < STEPS:
                        score(i, s)
                    if 1 <= s <= STEPS:
                        turn(i, s - 1)
                    if s >= 2:
                        product(i, s - 2)

        @block.vector
        def _(dve):
            def masked_max(i, s):
                qb = s % NCH
                L = (qb + 1) * CH
                diag = ps_s[:, :, qb * CH:L]
                dve.wait_ge(scored, i * STEPS + (s + 3))
                nc.vector.tensor_tensor(diag, diag, bc(g.col("causal")[:, None, :], [P, 2, CH]), ALU.add).then_inc(dv, 1)
                dve.wait_ge(dv, i * (5 * STEPS) + 5 * s + 1)
                nc.vector.tensor_reduce(out=mx[:], in_=ps_s[:, :, 0:L], axis=AX.X, op=ALU.max).then_inc(dv, 1)
                dve.wait_ge(dv, i * (5 * STEPS) + 5 * s + 2)
                dve.wait_ge(exped, i * STEPS + (s + 1))
                nc.vector.tensor_scalar(nm[:], mx[:], -SC, None, ALU.mult).then_inc(maxed, 1)

            def mix(i, s):
                L = (s % NCH + 1) * CH
                dve.wait_ge(exped, i * STEPS + (s + 2))
                nc.vector.reciprocal(rs[:], sums[:]).then_inc(dv, 1)
                dve.wait_ge(dv, i * (5 * STEPS) + 5 * s + 3)
                nc.vector.tensor_tensor(rs[:, 1:2], rs[:, 1:2], g.lam[:, 1:2], ALU.mult).then_inc(dv, 1)
                nc.vector.tensor_scalar(p[s % 2][:, 0, 0:L], p[s % 2][:, 0, 0:L], rs[:, 0:1], None, ALU.mult).then_inc(dv, 1)
                dve.wait_ge(dv, i * (5 * STEPS) + 5 * s + 5)
                nc.vector.scalar_tensor_tensor(out=p[s % 2][:, 0, 0:L], in0=p[s % 2][:, 1, 0:L], scalar=rs[:, 1:2],
                                               in1=p[s % 2][:, 0, 0:L], op0=ALU.mult, op1=ALU.add).then_inc(mixed, 1)

            with dve.Fori(0, H // 2) as i:
                for s in range(STEPS):
                    masked_max(i, s)
                    mix(i, s)

        @block.scalar
        def _(act):
            act.sem_inc(exped, 1)
            act.sem_inc(aready, 1)
            act.sem_inc(copied, 2)

            def exps(i, s):
                L = (s % NCH + 1) * CH
                act.wait_ge(maxed, i * STEPS + (s + 1))
                act.wait_ge(turned, i * STEPS + (s + 1))
                if s:
                    act.wait_ge(mixed, i * STEPS + s)
                for m in range(2):
                    last = nc.scalar.activation(p[s % 2][:, m, 0:L], ps_s[:, m, 0:L], ACT.Exp, scale=SC,
                                                bias=nm[:, m:m + 1], accum_out=sums[:, m:m + 1])
                last.then_inc(exped, 1)

            def take_turned(i, s):
                act.wait_ge(turned, i * STEPS + (s + 3))
                act.wait_ge(summed, i * STEPS + (s + 1 + STEPS - 2))
                n = s % NCH + 1
                nc.scalar.activation(aT[s % 2][:, 0:n, :], ps_t[:, 0:n, :], ACT.Copy).then_inc(aready, 1)

            def take_product(i, s):
                u, qb = divmod(s, NCH)
                act.wait_ge(summed, i * STEPS + (s + 1 + STEPS))
                nc.scalar.activation(o[:, bass.ds(i * 2 + (H + u), 1), qb * CH:(qb + 1) * CH], ps_o[s % 2][:, None, :],
                                     ACT.Copy).then_inc(copied, 1)

            act.sem_inc(turned, 2)
            with act.Fori(0, H // 2) as i:
                for s in range(STEPS + 2):
                    if s < STEPS:
                        exps(i, s)
                    if 1 <= s <= STEPS:
                        take_turned(i, s - 1)
                    if s >= 2:
                        take_product(i, s - 2)


def stage_cached(nc, g, qkT, cache_k, cache_v, pages, val, o):
    SC = 64 ** -0.5
    G = 4
    GP = NPG // G
    ROWS = 2 * H * NS
    with ExitStack() as stack:
        k = Kit(nc, stack, "dec")
        kt = [k.sb(f"kt{n}", [P, GP, H, PAGE]) for n in range(G)]
        vt = [k.sb(f"vt{n}", [P, GP, H * DV]) for n in range(G)]
        vn = k.sb("vn", [NS, H * DV])
        ids = k.sb("ids", [1, NB * NPG], I32)
        qz = k.sb("qz", [P, H * (ROWS + 8)])
        pm = k.sb("pm", [ROWS, PAST])
        pn = k.sb("pn", [ROWS, NS])
        pT = k.sb("pT", [P, NPG, ROWS])
        pnT = k.sb("pnT", [NS, ROWS])
        os_ = k.sb("os", [ROWS, H * DV])
        mx, sums, coef = (k.sb(x, [ROWS, 2]) for x in ("mx", "sums", "coef"))
        nm, rs = (k.sb(x, [ROWS, 1]) for x in ("nm", "rs"))
        ps_s = k.ps("ps_s", [ROWS, PAST])
        ps_n = k.ps("ps_n", [P, 512])
        ps_t = k.ps("ps_t", [P, NPG, ROWS])
        ps_o = k.ps("ps_o", [ROWS, H * DV])
        ps_x = k.ps("ps_x", [P, 512])
        ids_in, vn_in = k.sem("ids_in"), k.sem("vn_in")
        k_in = [k.sem(f"k_in{n}") for n in range(G)]
        v_in = [k.sem(f"v_in{n}") for n in range(G)]
        zeroed, qready, scored, maxed, exped, turned, pready = (
            k.sem(x) for x in ("zeroed", "qready", "scored", "maxed", "exped", "turned", "pready"))
        summed, scaled, picked, weighted, copied, dv = (
            k.sem(x) for x in ("summed", "scaled", "picked", "weighted", "copied", "dv"))
        grouped = k.sem("grouped")
        block = stack.enter_context(nc.Block())
        new = ps_n[0:ROWS, 0:NS]
        newT = ps_n[0:NS, 256:256 + ROWS]

        @block.sync
        def _(sp):
            sp.dma_start(ids[:], pages.rearrange("b p -> (b p)")[None, :]).then_inc(ids_in, 16)
            sp.wait_ge(ids_in, 16)
            with sp.Fori(0, NB) as i:
                def load(n, cache, order, dst, sem):
                    for j in range(GP):
                        page = sp.value_load(ids[0:1, bass.ds(i * NPG + (n * GP + j), 1)], min_val=0,
                                             max_val=cache.shape[0] - 1)
                        sp.dma_start(dst[:, j:j + 1], cache[bass.ds(page, 1)].rearrange(order)).then_inc(sem, 16)

                for n in range(G):
                    sp.wait_ge(grouped, i * G + (n + 1))
                    load(n, cache_k, "o p h k -> p o h k", kt[n], k_in[n])
                sp.wait_ge(summed, i + 1)
                sp.dma_start(vn[:].rearrange("t (g f) -> t g f", g=2), val[VB_GROUP:VB_GROUP + 2,
                             bass.ds(i * NS + SEQ, NS), :].rearrange("g t f -> t g f")).then_inc(vn_in, 16)
                for n in range(G):
                    load(n, cache_v, "o p f -> p o f", vt[n], v_in[n])

        @block.tensor
        def _(pe):
            pe.sem_inc(grouped, G)
            pe.sem_inc(summed, 1)
            with pe.Fori(0, NB) as i:
                pe.wait_ge(qready, i + 1)
                pe.wait_ge(exped, i + 1)
                for h in range(H):
                    nc.tensor.matmul(new, qz[:, h * ROWS:(h + 1) * ROWS],
                                     qkT[:, KBK + h, bass.ds(i * NS + SEQ, NS)], start=(h == 0), stop=(h == H - 1))
                for n in range(G):
                    pe.wait_ge(k_in[n], (i + 1) * (16 * GP))
                    for h in range(H):
                        last = nc.tensor.matmul(ps_s[:, n * GP * PAGE:(n + 1) * GP * PAGE],
                                                qz[:, h * ROWS:(h + 1) * ROWS], kt[n][:, :, h, :],
                                                start=(h == 0), stop=(h == H - 1))
                    last.then_inc(grouped, 1)
                pe.wait_ge(exped, i + 2)
                pe.wait_ge(pready, i + 1)
                nc.tensor.matmul(ps_t[:, 0, :], pm[:, 0:PAGE], g.ident()[0:ROWS, 0:ROWS], start=True, stop=True)
                for j in range(1, NPG):
                    nc.tensor.transpose(ps_t[:, j, :], pm[:, j * PAGE:(j + 1) * PAGE], g.ident()[0:ROWS, 0:ROWS])
                nc.tensor.transpose(newT, pn[:], g.ident()[0:ROWS, 0:ROWS]).then_inc(turned, 1)
                pe.wait_ge(pready, i + 2)
                pe.wait_ge(scaled, i + 1)
                pe.wait_ge(vn_in, i * 16 + 16)
                for n in range(G):
                    pe.wait_ge(v_in[n], (i + 1) * (16 * GP))
                    for j in range(GP):
                        nc.tensor.matmul(ps_o[:], pT[:, n * GP + j, :], vt[n][:, j, :], start=(n + j == 0), stop=False)
                nc.tensor.matmul(ps_o[:], pnT[:], vn[:], start=False, stop=True).then_inc(summed, 1)
                pe.wait_ge(scaled, i + 2)
                pe.wait_ge(copied, i + 1)
                for h in range(H):
                    last = nc.tensor.matmul(ps_x[:, h * NS:(h + 1) * NS], os_[:, h * DV:(h + 1) * DV],
                                            g.col("sel")[0:ROWS, h * NS:(h + 1) * NS], start=True, stop=True)
                last.then_inc(picked, 1)

        @block.vector
        def _(dve):
            chain = Seq(dve, zeroed)
            chain.link(nc.vector.memset(qz[:], 0.0))
            chain.link(nc.vector.scalar_tensor_tensor(out=coef[:, 0:1], in0=g.col("maps")[0:ROWS, 1:2],
                                                      scalar=g.lam[0:ROWS, 1:2], in1=g.col("maps")[0:ROWS, 0:1],
                                                      op0=ALU.mult, op1=ALU.add))
            with dve.Fori(0, NB) as i:
                dve.wait_ge(grouped, i * G + G)
                for m in range(2):
                    last = nc.vector.tensor_copy(
                        qz[64 * m:64 * m + 64, :].rearrange("p (h c) -> p h c", h=H)[:, :, m * NS:(m + 1) * NS],
                        qkT[64 * m:64 * m + 64, QB:QB + H, bass.ds(i * NS + SEQ, NS)])
                last.then_inc(qready, 1)
                chain = Seq(dve, dv)
                chain.base = i * 5
                dve.wait_ge(grouped, i * G + 2 * G)
                chain.link(nc.vector.tensor_tensor(new, new, g.col("smask")[0:ROWS], ALU.add))
                nc.vector.tensor_reduce(out=mx[:, 0:1], in_=ps_s[:], axis=AX.X, op=ALU.max)
                chain.link(nc.vector.tensor_reduce(out=mx[:, 1:2], in_=new, axis=AX.X, op=ALU.max))
                dve.wait_ge(exped, i + 1)
                chain.link(nc.vector.tensor_reduce(out=nm[:], in_=mx[:], axis=AX.X, op=ALU.max))
                nc.vector.tensor_scalar(nm[:], nm[:], -SC, None, ALU.mult).then_inc(maxed, 1)
                dve.wait_ge(exped, i + 2)
                chain.link(nc.vector.tensor_reduce(out=rs[:], in_=sums[:], axis=AX.X, op=ALU.add))
                chain.link(nc.vector.reciprocal(rs[:], rs[:]))
                nc.vector.tensor_tensor(rs[:], rs[:], coef[:, 0:1], ALU.mult).then_inc(weighted, 1)

        @block.scalar
        def _(act):
            for s in (exped, pready, scaled, copied):
                act.sem_inc(s, 1)
            with act.Fori(0, NB) as i:
                act.wait_ge(maxed, i + 1)
                nc.scalar.activation(pm[:], ps_s[:], ACT.Exp, scale=SC, bias=nm[:], accum_out=sums[:, 0:1])
                nc.scalar.activation(pn[:], new, ACT.Exp, scale=SC, bias=nm[:], accum_out=sums[:, 1:2]).then_inc(exped, 1)
                act.wait_ge(turned, i + 1)
                nc.scalar.activation(pT[:], ps_t[:], ACT.Copy)
                nc.scalar.activation(pnT[:], newT, ACT.Copy).then_inc(pready, 1)
                act.wait_ge(weighted, i + 1)
                act.wait_ge(summed, i + 2)
                nc.scalar.activation(os_[:], ps_o[:], ACT.Copy, scale=rs[:, 0:1]).then_inc(scaled, 1)
                act.wait_ge(picked, i + 1)
                nc.scalar.activation(o[:, H:2 * H, bass.ds(i * NS + SEQ, NS)],
                                     ps_x[:, 0:H * NS].rearrange("p (h t) -> p h t", h=H), ACT.Copy).then_inc(copied, 1)


def stage_heads(nc, g, tag, o, gate, plan):
    NBLK = max(len(b) for b, _, _ in plan)
    with ExitStack() as stack:
        k = Kit(nc, stack, tag)
        gb = [k.sb(f"g{z}", [P, NBLK, T]) for z in range(2)]
        sq = k.sb("sq", [P, NBLK, T])
        ln = k.sb("ln", [P, T])
        rstd = [k.sb(f"rstd{z}", [P, T]) for z in range(2)]
        ss = [k.ps(f"ss{z}", [P, NT, 512]) for z in range(2)]
        gated = [k.sem(f"gated{z}") for z in range(2)]
        squared, summed, logged, rooted, mixed, hid, dv = (
            k.sem(x) for x in ("squared", "summed", "logged", "rooted", "mixed", "hid", "dv"))
        block = stack.enter_context(nc.Block())
        at = {}

        def head(n):
            blocks = plan[n][0]
            return slice(blocks[0], blocks[0] + len(blocks))

        @block.sync
        def _(sp):
            gates = [0, 0]
            for n, (blocks, gate_at, _) in enumerate(plan):
                z, w = n % 2, len(blocks)
                if gate_at is not None:
                    if n >= 2:
                        sp.wait_ge(mixed, n - 1)
                    sp.dma_start(gb[z][:, 0:w, :], gate[:, gate_at:gate_at + w, :]).then_inc(gated[z], 16)
                    gates[z] += 16
                    at[("gate", n)] = gates[z]

        @block.scalar
        def _(act):
            def hi(n):
                act.wait_ge(mixed, n + 1)
                nc.scalar.activation(g.ahi[:, head(n), :], o[:, head(n), :], ACT.Copy).then_inc(hid, 1)

            for n, (blocks, _, _) in enumerate(plan):
                z, w = n % 2, len(blocks)
                if n:
                    act.wait_ge(summed, n)
                nc.scalar.activation(sq[:, 0:w, :], o[:, head(n), :], ACT.Square).then_inc(squared, 1)
                act.wait_ge(summed, n + 1)
                if n:
                    act.wait_ge(rooted, n)
                nc.scalar.activation(by_thirds(ln[:, None, :]), ss[z][:, :, 0:TT], ACT.Ln, scale=1.0 / (w * P),
                                     bias=g.eps[:, 0:1]).then_inc(logged, 1)
                act.wait_ge(logged, n + 1)
                if n >= 2:
                    act.wait_ge(mixed, n - 1)
                nc.scalar.activation(rstd[z][:], ln[:], ACT.Exp, scale=-0.5).then_inc(rooted, 1)
                if n:
                    hi(n - 1)
            hi(len(plan) - 1)

        @block.tensor
        def _(pe):
            for n, (blocks, _, _) in enumerate(plan):
                pe.wait_ge(squared, n + 1)
                if n >= 2:
                    pe.wait_ge(logged, n - 1)
                w = len(blocks)
                for t in range(NT):
                    for b in range(w):
                        last = nc.tensor.matmul(ss[n % 2][:, t, 0:TT], g.ones[:], sq[:, b, t * TT:(t + 1) * TT],
                                                start=(b == 0), stop=(b == w - 1))
                last.then_inc(summed, 1)

        @block.vector
        def _(dve):
            chain = Seq(dve, dv)

            def low(n):
                dve.wait_ge(hid, n + 1)
                nc.vector.tensor_tensor(g.alo[:, head(n), :], o[:, head(n), :], g.ahi[:, head(n), :].bitcast(F32),
                                        ALU.subtract)

            for n, (blocks, gate_at, weights) in enumerate(plan):
                z = n % 2
                dve.wait_ge(rooted, n + 1)
                for i, b in enumerate(blocks):
                    x = o[:, b, :]
                    last = nc.vector.scalar_tensor_tensor(out=x, in0=x, scalar=weights[i] if weights else 1.0,
                                                          in1=rstd[z][:], op0=ALU.mult, op1=ALU.mult)
                if gate_at is None:
                    last.then_inc(mixed, 1)
                else:
                    chain.link(last)
                    dve.wait_ge(gated[z], at[("gate", n)])
                    nc.vector.tensor_tensor(o[:, head(n), :], o[:, head(n), :], gb[z][:, 0:len(blocks), :],
                                            ALU.mult).then_inc(mixed, 1)
                if n:
                    low(n - 1)
            low(len(plan) - 1)


def stage_gate(nc, g, w_a, w_gate, scan_mask, b):
    RANK = 16
    with ExitStack() as stack:
        k = Kit(nc, stack, "gate")
        w = k.sb("w", [P, KB * RANK])
        whi = k.sb("whi", [P, KB * RANK], F32R)
        wlo = k.sb("wlo", [P, KB * RANK], F32R)
        wg = k.sb("wg", [RANK, H * P])
        mask = k.sb("mask", [P, T])
        aT = k.sb("aT", [RANK, T])
        ab, low = k.sb("ab", [P, T]), k.sb("low", [P, T])
        acc = k.ps("acc", [RANK, NT, 512])
        z = k.ps("z", [P, NT, 512])
        landed, split, summed, taken, gated, expd, lowed, used = (
            k.sem(x) for x in ("landed", "split", "summed", "taken", "gated", "expd", "lowed", "used"))
        block = stack.enter_context(nc.Block())

        @block.sync
        def _(sp):
            for dst, src in ((w, w_a), (wg, w_gate), (mask, scan_mask)):
                sp.dma_start(dst[:], src).then_inc(landed, 16)

        @block.tensor
        def _(pe):
            pe.wait_ge(split, 2)
            for n in range(NT):
                last = three_passes(nc, acc[:, n, 0:TT], lambda kk: whi[:, kk * RANK:(kk + 1) * RANK],
                                    lambda kk: wlo[:, kk * RANK:(kk + 1) * RANK],
                                    lambda kk: third(g.ahi, n)[:, kk, :], lambda kk: third(g.alo, n)[:, kk, :], KB)
            last.then_inc(summed, 1)
            pe.wait_ge(taken, 1)
            for h in range(H):
                if h:
                    pe.wait_ge(used, 2 * h)
                for n in range(NT):
                    last = nc.tensor.matmul(z[:, n, 0:TT], wg[:, h * P:(h + 1) * P], aT[:, n * TT:(n + 1) * TT],
                                            start=True, stop=True)
                last.then_inc(gated, 1)

        @block.scalar
        def _(act):
            act.wait_ge(summed, 1)
            nc.scalar.activation(by_thirds(aT[:, None, :]), acc[:, :, 0:TT], ACT.Copy).then_inc(taken, 1)
            for h in range(H):
                act.wait_ge(lowed, 3 * h + 1)
                nc.scalar.activation(by_thirds(ab[:, None, :]), z[:, :, 0:TT], ACT.Abs,
                                     bias=g.vcol("b_gate")[:, h:h + 1]).then_inc(expd, 1)
                act.wait_ge(expd, 3 * h + 1)
                nc.scalar.activation(ab[:], ab[:], ACT.Exp, scale=-1.0).then_inc(expd, 1)
                act.wait_ge(expd, 3 * h + 2)
                nc.scalar.activation(ab[:], ab[:], ACT.Ln, bias=1.0).then_inc(expd, 1)

        @block.vector
        def _(dve):
            dve.wait_ge(landed, 48)
            nc.vector.tensor_copy(whi[:], w[:]).then_inc(split, 1)
            dve.wait_ge(split, 1)
            nc.vector.tensor_tensor(wlo[:], w[:], whi[:].bitcast(F32), ALU.subtract).then_inc(split, 1)
            for h in range(H):
                dve.wait_ge(gated, h + 1)
                if h:
                    dve.wait_ge(lowed, 3 * h)
                nc.vector.tensor_scalar(by_thirds(low[:, None, :]), z[:, :, 0:TT], g.vcol("b_gate")[:, h:h + 1], 0.0,
                                        ALU.add, ALU.min).then_inc(lowed, 1)
                dve.wait_ge(lowed, 3 * h + 1)
                dve.wait_ge(expd, 3 * h + 3)
                nc.vector.tensor_tensor(low[:], low[:], ab[:], ALU.subtract).then_inc(lowed, 1)
                dve.wait_ge(lowed, 3 * h + 2)
                dve.sem_inc(used, 2)
                nc.vector.tensor_tensor_scan(b[:, h, :], mask[:], low[:], 0.0, ALU.mult, ALU.add).then_inc(lowed, 1)


def stage_gla(nc, g, qk, b, levels, v_dram, o, state_out):
    NL = len(LEVELS)
    IT = 1.0 / TAU
    DG = 256
    with ExitStack() as stack:
        k = Kit(nc, stack, "gla")
        lv = k.sb("lv", [P, NL + 1, P], I32)
        v = k.sb("v", [P, H, DG])
        E = [k.sb(f"E{l}", [P, H, CH]) for l in range(NL)]
        X = [k.sb(f"X{l}", [P, H, CH]) for l in range(NL)]
        bs, ek, eq, kd, qe, kc, kdT, attT = (
            k.sb(x, [P, H, CH]) for x in ("bs", "ek", "eq", "kd", "qe", "kc", "kdT", "attT"))
        bcopied = k.sem("bcopied")
        el = k.sb("el", [P, H])
        S = k.sb("S", [P, H, DG])
        gram = [k.ps(f"gram{z}", [P, H, CH]) for z in range(2)]
        ps_t = k.ps("ps_t", [P, H, CH])
        ps_o = k.ps("ps_o", [P, 2 * H, CH])
        ps_d = k.ps("ps_d", [P, H, DG])
        v_in, lv_in, zeroed, out_done = k.sem("v_in"), k.sem("lv_in"), k.sem("zeroed"), k.sem("out_done")
        subbed, exped, multed, grammed, selected, kcopied = (
            k.sem(x) for x in ("subbed", "exped", "multed", "grammed", "selected", "kcopied"))
        turned, kd_taken, summed, deltaed, stated, copied = (
            k.sem(x) for x in ("turned", "kd_taken", "summed", "deltaed", "stated", "copied"))
        block = stack.enter_context(nc.Block())
        NE, NM, NG = NL + 3, NL + 2, NL + 1

        def chunk(t, c):
            return t[:, :, bass.ds(c * CH, CH)]

        def halves(t, s):
            return t.rearrange("p h (n two s) -> p h n two s", two=2, s=s)

        @block.sync
        def _(sp):
            sp.dma_start(lv[:], levels).then_inc(lv_in, 16)
            with sp.Fori(0, NCH) as i:
                sp.wait_ge(deltaed, i + 1)
                sp.dma_start(v[:], v_dram[:, bass.ds(i * CH, CH), :].rearrange("h p e -> p h e")).then_inc(v_in, 16)
            sp.wait_ge(stated, NCH + 1)
            sp.dma_start(state_out, S[:]).then_inc(out_done, 16)
            sp.wait_ge(out_done, 16)

        @block.gpsimd
        def _(pool):
            with pool.Fori(0, NCH) as i:
                bt = bs[:]
                pool.wait_ge(bcopied, i + 1)
                for l, s in enumerate(LEVELS):
                    n = CH // (2 * s)
                    bh, eh = halves(bt, s), halves(E[l][:], s)
                    ref = bc(bh[:, :, :, 0, s - 1:s], [P, H, n, s])
                    pool.wait_ge(multed, i * NM + (l + 1))
                    nc.gpsimd.tensor_tensor(eh[:, :, :, 0, :], ref, bh[:, :, :, 0, :], ALU.subtract)
                    nc.gpsimd.tensor_tensor(eh[:, :, :, 1, :], bh[:, :, :, 1, :], ref, ALU.subtract).then_inc(subbed, 1)
                pool.wait_ge(multed, i * NM + (NL + 1))
                nc.gpsimd.tensor_tensor(ek[:], bc(bt[:, :, CH - 1:CH], [P, H, CH]), bt, ALU.subtract).then_inc(subbed, 1)

        @block.scalar
        def _(act):
            act.sem_inc(kd_taken, 1)
            act.sem_inc(copied, 1)

            def exponentials(i, first=False):
                if not first:
                    act.wait_ge(subbed, i * (NL + 1))
                    act.wait_ge(exped, i * NE)
                nc.scalar.activation(bs[:], chunk(b, i), ACT.Copy).then_inc(bcopied, 1)
                for l in range(NL + 1):
                    e = E[l] if l < NL else ek
                    act.wait_ge(subbed, i * (NL + 1) + (l + 1))
                    nc.scalar.activation(e[:], e[:], ACT.Exp, scale=IT).then_inc(exped, 1)
                act.wait_ge(multed, i * NM + NM)
                nc.scalar.activation(eq[:], bs[:], ACT.Exp, scale=IT).then_inc(exped, 1)

            def decay(i):
                act.wait_ge(stated, i + 1)
                nc.scalar.activation(el[:], bs[:, :, CH - 1], ACT.Exp, scale=IT).then_inc(exped, 1)

            def keys(i):
                act.wait_ge(grammed, i * NG + NG)
                nc.scalar.activation(kc[:], chunk(qk, i)[:, H:2 * H], ACT.Copy).then_inc(kcopied, 1)

            def take(i):
                act.wait_ge(turned, i + 2)
                act.wait_ge(deltaed, i + 1)
                nc.scalar.activation(kdT[:], ps_t[:], ACT.Copy).then_inc(kd_taken, 1)
                act.wait_ge(summed, i + 2)
                nc.scalar.activation(chunk(o, i), ps_o[:], ACT.Copy).then_inc(copied, 1)

            keys(0)
            exponentials(0, True)
            decay(0)
            with act.Fori(0, NCH - 1) as i:
                exponentials(i + 1)
                take(i)
                keys(i + 1)
                decay(i + 1)
            take(NCH - 1)

        @block.tensor
        def _(pe):
            pe.sem_inc(grammed, NG)
            pe.sem_inc(turned, 1)
            pe.sem_inc(summed, 1)
            pe.sem_inc(deltaed, 1)
            with pe.Fori(0, NCH) as i:
                for l in range(NL + 1):
                    pe.wait_ge(selected, i * NG + (l + 1))
                    if l < NL:
                        pe.wait_ge(multed, i * NM + (NM + l + 1))
                    else:
                        pe.wait_ge(kcopied, i + 1)
                    for h in range(H):
                        rhs = X[l][:, h, :] if l < NL else chunk(qk, i)[:, h, :]
                        last = nc.tensor.matmul(gram[l % 2][:, h, :], (X[l] if l < NL else kc)[:, h, :], rhs,
                                                start=True, stop=True)
                    last.then_inc(grammed, 1)
                pe.wait_ge(multed, i * NM + (NM + NL + 1))
                pe.wait_ge(kd_taken, i + 1)
                for h in range(H):
                    last = nc.tensor.transpose(ps_t[:, h, :], kd[:, h, :], g.ident())
                last.then_inc(turned, 1)
                pe.wait_ge(multed, i * NM + 2 * NM)
                pe.wait_ge(selected, i * NG + (NG + 2))
                pe.wait_ge(v_in, i * 16 + 16)
                pe.wait_ge(stated, i + 1)
                pe.wait_ge(copied, i + 1)
                for h in range(H):
                    for e in range(2):
                        nc.tensor.matmul(ps_o[:, 2 * h + e, :], v[:, h, e * P:(e + 1) * P], attT[:, h, :],
                                         start=True, stop=False)
                        last = nc.tensor.matmul(ps_o[:, 2 * h + e, :], S[:, h, e * P:(e + 1) * P], qe[:, h, :],
                                                start=False, stop=True)
                last.then_inc(summed, 1)
                pe.wait_ge(kd_taken, i + 2)
                for h in range(H):
                    last = nc.tensor.matmul(ps_d[:, h, :], kdT[:, h, :], v[:, h, :], start=True, stop=True)
                last.then_inc(deltaed, 1)

        @block.vector
        def _(dve):
            nc.vector.memset(S[:], 0.0)
            nc.vector.memset(attT[:], 0.0).then_inc(zeroed, 1)
            dve.wait_ge(zeroed, 1)
            dve.wait_ge(lv_in, 16)
            dve.sem_inc(stated, 1)
            dve.sem_inc(selected, 2)
            dve.sem_inc(multed, NM)

            def scale_level(i, l):
                s = LEVELS[l]
                dve.wait_ge(exped, i * NE + (l + 1))
                dve.wait_ge(grammed, i * NG + (l + 1))
                xh, eh, th = halves(X[l][:], s), halves(E[l][:], s), halves(chunk(qk, i), s)
                nc.vector.tensor_tensor(xh[:, :, :, 0, :], th[:, H:2 * H, :, 0, :], eh[:, :, :, 0, :], ALU.mult)
                nc.vector.tensor_tensor(xh[:, :, :, 1, :], th[:, 0:H, :, 1, :], eh[:, :, :, 1, :],
                                        ALU.mult).then_inc(multed, 1)

            def scale_kd(i):
                dve.wait_ge(exped, i * NE + (NL + 1))
                dve.wait_ge(turned, i + 1)
                nc.vector.tensor_tensor(kd[:], chunk(qk, i)[:, H:2 * H], ek[:], ALU.mult).then_inc(multed, 1)

            def scale_qe(i):
                dve.wait_ge(exped, i * NE + (NL + 2))
                dve.wait_ge(summed, i + 1)
                nc.vector.tensor_tensor(qe[:], chunk(qk, i)[:, 0:H], eq[:], ALU.mult).then_inc(multed, 1)

            def before_select(i, l):
                dve.wait_ge(grammed, i * NG + (NG + l + 1))
                dve.wait_ge(selected, i * NG + (l + 2))
                if l == 0:
                    dve.wait_ge(summed, i + 1)

            def select(i, l):
                nc.vector.copy_predicated(attT[:], bc(lv[:, l, None, :], [P, H, CH]), gram[l % 2][:]).then_inc(selected, 1)

            def state(i):
                dve.wait_ge(deltaed, i + 2)
                dve.wait_ge(exped, i * NE + NE)
                for h in range(H):
                    last = nc.vector.scalar_tensor_tensor(out=S[:, h, :], in0=S[:, h, :], scalar=el[:, h:h + 1],
                                                          in1=ps_d[:, h, :], op0=ALU.mult, op1=ALU.add)
                last.then_inc(stated, 1)

            for l in range(NL):
                scale_level(0, l)
            scale_kd(0)
            scale_qe(0)
            with dve.Fori(0, NCH - 1) as i:
                for l in range(NL):
                    before_select(i, l)
                    scale_level(i + 1, l)
                    select(i, l)
                before_select(i, NL)
                scale_kd(i + 1)
                select(i, NL)
                state(i)
                scale_qe(i + 1)
            for l in range(NL + 1):
                before_select(NCH - 1, l)
                select(NCH - 1, l)
            state(NCH - 1)


def stage_gla_samples(nc, g, qk, b, levels, v_dram, o, state_in, state_out):
    IT = 1.0 / TAU
    DG = 256
    LV = [l for l, s in enumerate(LEVELS) if 2 * s <= NS]
    with ExitStack() as stack:
        k = Kit(nc, stack, "glas")
        lv = k.sb("lv", [P, len(LEVELS) + 1, P], I32)
        v = k.sb("v", [TS, H, DG])
        vm = [k.sb(f"vm{z}", [TS, NB, DG]) for z in range(2)]
        ss = k.sb("ss", [P, NB, H, DG])
        E = [k.sb(f"E{l}", [P, H, TS]) for l in range(len(LV))]
        X = [k.sb(f"X{l}", [P, H, TS]) for l in range(len(LV))]
        ek, eq, kd, qe = (k.sb(x, [P, H, TS]) for x in ("ek", "eq", "kd", "qe"))
        kdT = k.sb("kdT", [TS, H, P])
        attT = k.sb("attT", [TS, H, TS])
        el = k.sb("el", [P, H, NB])
        ps_g = k.ps("ps_g", [TS, len(LV) + 1, H, TS])
        ps_t = k.ps("ps_t", [TS, H, P])
        ps_o = k.ps("ps_o", [P, 2 * H, TS])
        ps_d = k.ps("ps_d", [P, NB, DG])
        landed, dv, exped, grammed, turned, taken, summed, deltaed, done, decayed, out_done = (
            k.sem(x) for x in ("landed", "dv", "exped", "grammed", "turned", "taken", "summed", "deltaed", "done",
                               "decayed", "out_done"))
        block = stack.enter_context(nc.Block())
        at = {}

        def halves(t, s):
            return t.rearrange("p h (n two s) -> p h n two s", two=2, s=s)

        def seqs(t):
            return t.rearrange("p h (b t) -> p h b t", t=NS)

        bt, qt, kt = b[:, :, SEQ:T], qk[:, 0:H, SEQ:T], qk[:, H:2 * H, SEQ:T]

        @block.sync
        def _(sp):
            sp.dma_start(lv[:], levels).then_inc(landed, 16)
            sp.dma_start(v[:], v_dram[:, SEQ:T, :].rearrange("h p e -> p h e")).then_inc(landed, 16)
            sp.dma_start(ss[:], state_in).then_inc(landed, 16)
            sp.wait_ge(done, H)
            sp.dma_start(state_out, ss[:]).then_inc(out_done, 16)
            sp.wait_ge(out_done, 16)

        def state(dve, h):
            dve.wait_ge(summed, 1)
            nc.vector.tensor_tensor(ss[:, :, h, :], ss[:, :, h, :], bc(el[:, h, :, None], [P, NB, DG]),
                                    ALU.mult).then_inc(decayed, 1)
            dve.wait_ge(decayed, h + 1)
            dve.wait_ge(deltaed, h + 1)
            nc.vector.tensor_tensor(ss[:, :, h, :], ss[:, :, h, :], ps_d[:], ALU.add).then_inc(done, 1)

        @block.vector
        def _(dve):
            chain = Seq(dve, dv)
            for l, i in enumerate(LV):
                s = LEVELS[i]
                bh, eh = halves(bt, s), halves(E[l][:], s)
                ref = bc(bh[:, :, :, 0, s - 1:s], [P, H, TS // (2 * s), s])
                nc.vector.tensor_tensor(eh[:, :, :, 0, :], ref, bh[:, :, :, 0, :], ALU.subtract)
                nc.vector.tensor_tensor(eh[:, :, :, 1, :], bh[:, :, :, 1, :], ref, ALU.subtract)
            nc.vector.memset(attT[:], 0.0)
            for h in range(H):
                bh = bt[:, h, :].rearrange("p (b t) -> p b t", t=NS)
                last = nc.vector.tensor_tensor(ek[:, h, :].rearrange("p (b t) -> p b t", t=NS),
                                               bc(bh[:, :, NS - 1:NS], [P, NB, NS]), bh, ALU.subtract)
            chain.link(last)
            at["sub"] = chain.n
            dve.wait_ge(exped, 1)
            for l, i in enumerate(LV):
                s = LEVELS[i]
                xh, eh = halves(X[l][:], s), halves(E[l][:], s)
                nc.vector.tensor_tensor(xh[:, :, :, 0, :], halves(kt, s)[:, :, :, 0, :], eh[:, :, :, 0, :], ALU.mult)
                nc.vector.tensor_tensor(xh[:, :, :, 1, :], halves(qt, s)[:, :, :, 1, :], eh[:, :, :, 1, :], ALU.mult)
            nc.vector.tensor_tensor(kd[:], kt, ek[:], ALU.mult)
            chain.link(nc.vector.tensor_tensor(qe[:], qt, eq[:], ALU.mult))
            at["mult"] = chain.n
            dve.wait_ge(landed, 48)
            dve.wait_ge(grammed, 1)
            for l in range(len(LV) + 1):
                i = LV[l] if l < len(LV) else len(LEVELS)
                chain.link(nc.vector.copy_predicated(attT[:], bc(lv[0:TS, i, None, 0:TS], [TS, H, TS]), ps_g[:, l]))
            at["select"] = chain.n
            for h in range(H):
                if h >= 2:
                    dve.wait_ge(deltaed, h - 1)
                chain.link(nc.vector.tensor_tensor(vm[h % 2][:], bc(v[:, h, None, :], [TS, NB, DG]),
                                                   bc(g.col("bmask")[0:TS, :, None], [TS, NB, DG]), ALU.mult))
                at[("vm", h)] = chain.n
                if h:
                    state(dve, h - 1)
            state(dve, H - 1)

        @block.scalar
        def _(act):
            act.wait_ge(dv, at["sub"])
            for e in [*E, ek]:
                nc.scalar.activation(e[:], e[:], ACT.Exp, scale=IT)
            nc.scalar.activation(el[:], seqs(bt)[:, :, :, NS - 1], ACT.Exp, scale=IT)
            nc.scalar.activation(eq[:], bt, ACT.Exp, scale=IT).then_inc(exped, 1)
            act.wait_ge(turned, 1)
            nc.scalar.activation(kdT[:], ps_t[:], ACT.Copy).then_inc(taken, 1)
            act.wait_ge(summed, 1)
            nc.scalar.activation(o[:, :, SEQ:T], ps_o[:], ACT.Copy)

        @block.tensor
        def _(pe):
            pe.wait_ge(dv, at["mult"])
            for l in range(len(LV) + 1):
                for h in range(H):
                    a, c = (X[l][:, h, :], X[l][:, h, :]) if l < len(LV) else (kt[:, h, :], qt[:, h, :])
                    last = nc.tensor.matmul(ps_g[:, l, h, :], a, c, start=True, stop=True)
            last.then_inc(grammed, 1)
            for h in range(H):
                last = nc.tensor.transpose(ps_t[:, h, :], kd[:, h, :], g.ident())
            last.then_inc(turned, 1)
            pe.wait_ge(dv, at["select"])
            for h in range(H):
                for e in range(2):
                    nc.tensor.matmul(ps_o[:, 2 * h + e, :], v[:, h, e * P:(e + 1) * P], attT[:, h, :],
                                     start=True, stop=False)
                    for i in range(NB):
                        last = nc.tensor.matmul(ps_o[:, 2 * h + e, i * NS:(i + 1) * NS], ss[:, i, h, e * P:(e + 1) * P],
                                                qe[:, h, i * NS:(i + 1) * NS], start=False, stop=(i == NB - 1))
            last.then_inc(summed, 1)
            pe.wait_ge(taken, 1)
            for h in range(H):
                pe.wait_ge(dv, at[("vm", h)])
                if h:
                    pe.wait_ge(done, h)
                for n in range(NB // 2):
                    last = nc.tensor.matmul(ps_d[:, 2 * n:2 * n + 2, :], kdT[:, h, :], vm[h % 2][:, 2 * n:2 * n + 2, :],
                                            start=True, stop=True)
                last.then_inc(deltaed, 1)


def decoder_step(nc, a, outs):
    def scratch(name, shape):
        return nc.dram_tensor(name, shape, F32, kind="Internal").ap()

    Kit.taken = []
    x_0, x_1, x_2 = (scratch(f"x_{i}", [P, KB, T]) for i in range(3))
    v_gla = scratch("v_gla", [4, T, GW])
    gates = scratch("gates", [P, KB, T])
    with ExitStack() as life:
        g = State(nc, life)
        g.lam_in = [a[n] for n in ("lam_q1", "lam_k1", "lam_q2", "lam_k2")]

        def sb(stack, name, shape, dt=F32):
            return stack.enter_context(nc.sbuf_tensor(name, shape, dt))

        def operand(stack, tag):
            g.ahi, g.alo = (stack.enter_context(nc.sbuf_tensor(f"{tag}_{x}", [P, KB, T], F32R, side="right"))
                            for x in ("hi", "lo"))

        def copy_to(dst, scale=1.0):
            return lambda u, s: nc.scalar.activation(by_thirds(dst[:, bass.ds(u, 1), :]), s, ACT.Copy, scale=scale)

        def silu_to(dst):
            return lambda u, s: nc.scalar.activation(by_thirds(dst[:, bass.ds(u, 1), :]), s, ACT.Silu)

        stage_load(nc, g, a["consts"], a["vecs"])
        stage_ada(nc, g, a["w_ada"], a["cT"])
        y_flat = sb(life, "y", [P, KB * T])
        y = y_flat[:].rearrange("p (k t) -> p k t", k=KB)

        with ExitStack() as first:
            qkT = sb(first, "qkT", [P, 12, T])
            with ExitStack() as projections:
                operand(projections, "h0")
                stage_norm(nc, g, "n0", y_flat[:], None, None, (0, 0), a["x"], None)
                stage_linear(nc, g, "ga", a["w_ga"], [(H, silu_to(y))])
                stage_store(nc, "gate_ab", [(gates[:, 0:H, :], y[:, 0:H, :])])
                stage_project(nc, g, "qk", y_flat[:], a["w_qk"], 6, True, qkT, outs["rotated"])
                stage_project(nc, g, "v", y_flat[:], a["w_v"], 4, False, None, outs["values"])
            stage_retention(nc, g, qkT, outs["rotated"], outs["values"], y, a["state_ret"],
                            outs["ret_prompt"], outs["ret_sample"])
            stage_attention(nc, g, qkT, outs["values"], y)
            stage_cached(nc, g, qkT, a["cache_k"], a["cache_v"], a["pages"], outs["values"], y)
        recycle_semaphores(nc)
        h = life.enter_context(ExitStack())
        operand(h, "h")
        stage_heads(nc, g, "hd0", y, gates,
                    [([h], h, None) for h in range(H)] + [([H + h], None, [g.vcol("g_diff")]) for h in range(H)])
        stage_linear(nc, g, "oab", a["w_out_ab"], [(KB, copy_to(y))])
        stage_norm(nc, g, "n1", None, y, (0, 2), (0, 3), a["x"], x_0)
        stage_ffn(nc, g, "f0", 0, a["w_ffn0"], y, a["conv_in0"], outs["conv0"])
        stage_norm(nc, g, "n2", None, y, (0, 5), (1, 0), x_0, x_1)

        recycle_semaphores(nc)
        stage_project(nc, g, "vc", y_flat[:], a["w_vc"], 4, False, None, v_gla)
        stage_linear(nc, g, "r", a["w_qkr"][2 * H:4 * H], [(2 * H, silu_to(y))])
        stage_store(nc, "gate_c", [(gates, y)])
        with ExitStack() as second:
            qk = sb(second, "qk", [P, 2 * H, T])
            b = sb(second, "b", [P, H, T])
            stage_linear(nc, g, "qkc", a["w_qkr"][0:2 * H],
                         [(H, copy_to(qk, DV ** -0.5)), (H, copy_to(qk[:, H:2 * H, :]))])
            stage_gate(nc, g, a["w_a"], a["w_gate"], a["scan"], b)
            h.close()
            stage_gla(nc, g, qk, b, a["levels"], v_gla, y, outs["gla_prompt"])
            stage_gla_samples(nc, g, qk, b, a["levels"], v_gla, y, a["state_gla"], outs["gla_sample"])
        operand(life, "m")
        g_gla = g.vcol("g_gla")
        stage_heads(nc, g, "hd1", y, gates,
                    [([2 * h, 2 * h + 1], 2 * h, [g_gla[:, 0:1], g_gla[:, 1:2]]) for h in range(H)])
        stage_linear(nc, g, "oc", a["w_out_c"], [(KB, copy_to(y))])
        stage_norm(nc, g, "n3", None, y, (1, 2), (1, 3), x_1, x_2)
        stage_ffn(nc, g, "f1", 1, a["w_ffn1"], y, a["conv_in1"], outs["conv1"])
        stage_norm(nc, g, "n4", None, y, (1, 5), None, x_2, outs["x_out"])


def _constants():
    c = np.zeros((P, NCONST), np.float32)

    def put(name, a):
        a = np.asarray(a, np.float64).astype(np.float32)
        c[:a.shape[0], CONST[name][0]:CONST[name][1]] = a.reshape(a.shape[0], -1)

    i = np.arange(P)
    put("ident", np.eye(P))
    put("causal", np.where(i[None, :] <= i[:, None], 0.0, NEG))
    gamma = 1.0 - np.exp2(-5.0 - np.arange(H))
    scale = 64 ** -0.5
    rel = i[None, :] - i[:, None]
    put("decay", np.stack([np.where(rel >= 0, gm ** np.maximum(rel, 0), 0) for gm in gamma], 1) * scale)
    put("decq", np.broadcast_to(np.stack([gm ** (i + 1) for gm in gamma]), (P, H, P)))
    put("deck", np.stack([gm ** (P - 1 - i) for gm in gamma], 1) * scale)
    half = (i // 64)[:, None]
    pair = 2 * np.arange(2)[None, :] + half
    put("decc", gamma[pair] ** P)
    inv = (np.float32(10000.0) ** (-np.arange(0, 64, 2, dtype=np.float32) / np.float32(64))).astype(np.float32)
    pos = np.concatenate([np.arange(SEQ), PAST + np.tile(np.arange(NS), NB)]).astype(np.float32)
    ang = (pos[:, None] * inv[None, :]).astype(np.float32).astype(np.float64)
    ang = np.concatenate([ang, np.zeros((TILES * P - T, 32))]).reshape(TILES, P, 32).transpose(1, 0, 2)
    put("cos", np.cos(ang))
    put("sin", np.stack([-np.sin(ang), np.sin(ang)], 2))
    s = np.arange(TS)
    same = (s[:, None] // NS == s[None, :] // NS)
    srel = s[None, :] - s[:, None]
    put("sdecay", np.stack([np.where(same & (srel >= 0), gm ** np.maximum(srel, 0), 0) for gm in gamma], 1) * scale)
    put("sdecq", np.broadcast_to(np.stack([gm ** (s % NS + 1) for gm in gamma]), (P, H, TS)))
    put("sdeck", np.stack([gm ** (NS - 1 - s % NS) for gm in gamma], 1) * scale)
    put("sdecc", gamma[pair] ** NS)
    row = np.arange(TS)
    put("smask", np.where(np.arange(NS)[None, :] <= row[:, None] % NS, 0.0, NEG))
    put("sel", np.stack([(row[:, None] // 8 == h) & (row[:, None] % NS == np.arange(NS)[None, :])
                         for h in range(H)], 1))
    put("bmask", s[:, None] // NS == np.arange(NB)[None, :])
    put("maps", np.stack([row % 8 < NS, row % 8 >= NS], 1))
    t = np.arange(T)
    first = np.where(t < SEQ, t % CH == 0, (t - SEQ) % NS == 0)
    return c, np.broadcast_to(np.where(first, 0.0, 1.0), (P, T)).astype(np.float32)


def _level_masks():
    i = np.arange(P)
    m = [((i[:, None] // (2 * s) == i[None, :] // (2 * s)) & (i[:, None] % (2 * s) < s) & (i[None, :] % (2 * s) >= s))
         for s in LEVELS]
    m.append(i[:, None] == i[None, :])
    return np.stack(m, 1).astype(np.int32)


def _units(w, width=P):
    n = w.shape[1] // width
    return np.ascontiguousarray(w.reshape(KB, P, n, width).transpose(2, 1, 0, 3).reshape(n, P, KB * width))


def _columns(v):
    return np.ascontiguousarray(v.reshape(-1, P).T)


def _hidden_order(v):
    v = v.reshape(v.shape[:-1] + (2, FB, P))
    return np.moveaxis(v, -3, -2).reshape(v.shape[:-3] + (2 * FB, P))


def _ffn_units(w_up, w_down):
    up = _units(w_up).reshape(2, FB, P, UW)
    down = w_down.reshape(FB, P, D)
    out = [up[0, 0], up[1, 0], up[0, 1], up[1, 1]]
    for p in range(1, FB // 2):
        out += [up[0, 2 * p], up[1, 2 * p], down[2 * p - 2], down[2 * p - 1], up[0, 2 * p + 1], up[1, 2 * p + 1]]
    out += [down[FB - 2], down[FB - 1]]
    return np.stack(out)


def _feature_major(prompt, sample):
    a = np.concatenate([prompt, sample.reshape(TS, -1)])
    return np.ascontiguousarray(a.reshape(T, -1, P).transpose(2, 1, 0))


def lay_out(i):
    a = {}
    a["consts"], a["scan"] = _constants()
    a["levels"] = _level_masks()
    v = [_columns(i["b_ada"])] + [_columns(i[n]) for n in ("g_pre_mix", "g_post_mix", "g_pre_ffn", "g_post_ffn")]
    v += [_columns(i["g_diff"]), _columns(i["g_gla"]), _columns(i["b_gate_c"])]
    v += [_hidden_order(i["conv_b"]).reshape(-1, P).T]
    cw = _hidden_order(i["conv_w"])
    v += [cw.transpose(3, 0, 2, 1).reshape(P, -1)]
    a["vecs"] = np.ascontiguousarray(np.concatenate(v, 1))
    for n in ("lam_q1", "lam_k1", "lam_q2", "lam_k2"):
        a[n] = i[n].reshape(1, 64)
    a["x"] = _feature_major(i["x_prompt"][0], i["x_sample"])
    a["cT"] = np.ascontiguousarray(np.concatenate([i["c_prompt"], i["c_sample"]]).reshape(C9, KB, P).transpose(2, 1, 0))
    a["w_ada"] = np.concatenate([_units(i["w_ada"][l], 512) for l in range(2)]).reshape(24, P, KB, 512)
    w = i["w_in_ab"][0]
    qa, ka, va, ga, qb, kb, vb = np.split(w, [256, 512, 1024, 1536, 2048, 2560], axis=1)
    a["w_qk"] = _units(np.concatenate([qa, qb, ka, kb], 1), GW)
    a["w_v"] = _units(np.concatenate([va, vb], 1), GW)
    a["w_ga"] = _units(ga)
    a["w_out_ab"] = _units(i["w_out_ab"][0])
    w = i["w_in_c"][0]
    q, k, vv, r, ga_ = np.split(w, [512, 1024, 2048, 3072], axis=1)
    a["w_qkr"] = _units(np.concatenate([q, k, r], 1))
    a["w_vc"] = _units(vv, GW)
    a["w_a"] = _units(ga_, 16)[0]
    a["w_gate"] = i["w_gate_c"][0]
    a["w_out_c"] = _units(i["w_out_c"][0])
    for l in range(2):
        a[f"w_ffn{l}"] = _ffn_units(i["w_up"][l], i["w_down"][l])
        sc = _hidden_order(i["state_conv"][l])
        a[f"conv_in{l}"] = np.ascontiguousarray(sc.transpose(3, 2, 0, 1))
    a["cache_k"] = np.ascontiguousarray(i["cache_k"][0].transpose(0, 3, 2, 1))
    a["cache_v"] = i["cache_v"][0].reshape(-1, PAGE, H * DV)
    a["pages"] = np.ascontiguousarray(i["page_table"].astype(np.int32))
    a["state_ret"] = np.ascontiguousarray(i["state_ret"][0].reshape(NB, 2, P, DV).transpose(2, 0, 1, 3))
    a["state_gla"] = np.ascontiguousarray(i["state_gla"][0].transpose(2, 0, 1, 3))
    return a


OUTPUTS = {"rotated": [6, T, GW], "values": [4, T, GW], "ret_prompt": [P, 2, DV], "ret_sample": [P, NB, 2, DV],
           "x_out": [P, KB, T], "gla_prompt": [P, H, 256], "gla_sample": [P, NB, H, 256],
           "conv0": [P, 2 * FB, 2 * C9], "conv1": [P, 2 * FB, 2 * C9]}


def kernel(**inputs):
    import concourse.bacc as _bacc
    from concourse.bass_utils import run_bass_kernel_spmd

    arrays = lay_out({n: np.asarray(v) for n, v in inputs.items()})
    nc = _bacc.Bacc("TRN2", target_bir_lowering=False, num_devices=1)
    a = {n: nc.dram_tensor(n, list(v.shape), mybir.dt.from_np(v.dtype), kind="ExternalInput").ap()
         for n, v in arrays.items()}
    outs = {n: nc.dram_tensor(n, s, F32, kind="ExternalOutput").ap() for n, s in OUTPUTS.items()}
    decoder_step(nc, a, outs)
    nc.finalize()
    r = run_bass_kernel_spmd(nc, [arrays], core_ids=[0]).results[0]
    r = {n: np.asarray(r[n]).reshape(s) for n, s in OUTPUTS.items()}

    x = r["x_out"].transpose(2, 1, 0).reshape(T, D)
    kb = r["rotated"][4:6].transpose(1, 0, 2).reshape(T, H, DV)
    vb = r["values"][VB_GROUP:].transpose(1, 0, 2).reshape(T, H, DV)
    conv = np.stack([r[n].reshape(P, FB, 2, 2 * C9).transpose(3, 2, 1, 0).reshape(C9, 2, 2 * FB * P)
                     for n in ("conv0", "conv1")])
    out = (x[None, :SEQ], x[SEQ:].reshape(NB, NS, D),
           kb[None, None, :SEQ], vb[None, None, :SEQ],
           kb[SEQ:].reshape(1, NB, NS, H, DV), vb[SEQ:].reshape(1, NB, NS, H, DV),
           r["ret_prompt"].reshape(2, 64, 2, DV).transpose(2, 0, 1, 3).reshape(1, 1, H, 64, DV),
           r["ret_sample"].reshape(2, 64, NB, 2, DV).transpose(2, 3, 0, 1, 4).reshape(1, NB, H, 64, DV),
           r["gla_prompt"].transpose(1, 0, 2)[None, None], r["gla_sample"].transpose(1, 2, 0, 3)[None],
           conv[:, 0:1], conv[:, 1:])
    return tuple(np.ascontiguousarray(o) for o in out)
```

```python
from contextlib import ExitStack

import numpy as np
import concourse.bass as bass
from concourse import mybir

F32 = mybir.dt.float32
F32R = mybir.dt.float32r
I32 = mybir.dt.int32
ALU = mybir.AluOpType
ACT = mybir.ActivationFunctionType
AX = mybir.AxisListType

P = 128
D = 1024
KB = D // P
SEQ = 1024
NB = 8
NS = 4
TS = NB * NS
T = SEQ + TS
NT = 3
TT = T // NT
PT = SEQ - 2 * TT
CH = 128
NCH = SEQ // CH
TILES = NCH + 1
H = 4
DV = 128
PAST = 2048
PAGE = 128
NPG = PAST // PAGE
FB = 22
UW = KB * P
GW = 256
EPS = 1e-6
TAU = 16.0
LAM_INIT = 0.2
NEG = -1e30
C9 = 1 + NB
NMOD = 6 * KB
LEVELS = [64, 32, 16, 8, 4, 2, 1]

def const_columns():
    at, n = {}, 0
    for name, w in (("ident", P), ("causal", P), ("decay", H * P), ("decq", H * P), ("deck", H),
                    ("decc", 2), ("cos", TILES * 32), ("sin", TILES * 64), ("sdecay", H * TS),
                    ("sdecq", H * TS), ("sdeck", H), ("sdecc", 2), ("smask", NS), ("sel", H * NS),
                    ("bmask", NB), ("maps", 2 * TS)):
        at[name] = (n, n + w)
        n += w
    return at, n


CONST, NCONST = const_columns()
VEC = {}
NVEC = 0
for _n, _w in (("b_ada", 2 * NMOD), ("g_pre_mix", 2 * KB), ("g_post_mix", 2 * KB), ("g_pre_ffn", 2 * KB),
               ("g_post_ffn", 2 * KB), ("g_diff", 1), ("g_gla", 2), ("b_gate", 4), ("conv_b", 4 * FB),
               ("conv_w", 12 * FB)):
    VEC[_n] = (NVEC, NVEC + _w)
    NVEC += _w


class Kit:

    def __init__(self, nc, stack, tag, spare=None):
        self.nc, self.stack, self.tag, self.spare, self.used = nc, stack, tag, spare, 0

    def sb(self, name, shape, dt=F32):
        n = int(np.prod(shape[1:]))
        if self.spare is not None and dt != F32R and self.used + n <= self.spare.shape[1]:
            view = self.spare[0:shape[0], self.used:self.used + n]
            self.used += n
            if dt != F32:
                view = view.bitcast(dt)
            names = "abcd"[:len(shape) - 1]
            return view.rearrange(f"p ({' '.join(names)}) -> p {' '.join(names)}",
                                  **dict(zip(names[1:], shape[2:]))) if len(shape) > 2 else view
        return self.stack.enter_context(self.nc.sbuf_tensor(f"{self.tag}_{name}", shape, dt))

    def ps(self, name, shape, dt=F32):
        return self.stack.enter_context(self.nc.psum_tensor(f"{self.tag}_{name}", shape, dt))

    taken = []

    def sem(self, name):
        Kit.taken.append(self.nc.alloc_semaphore(f"{self.tag}_{name}"))
        return Kit.taken[-1]


def recycle_semaphores(nc):
    nc.clear_and_free_semaphores(Kit.taken)
    Kit.taken = []
    with nc.Block():
        pass


class Seq:

    def __init__(self, eng, sem):
        self.eng, self.sem, self.n, self.base = eng, sem, 0, 0

    def link(self, ins):
        ins.then_inc(self.sem, 1)
        self.n += 1
        self.eng.wait_ge(self.sem, self.base + self.n)
        return ins


def cols(t, name, table=CONST):
    a, b = table[name]
    return t[:, a:b]


def third(ap, n):
    return ap[:, :, n * TT:(n + 1) * TT]


def bc(ap, shape):
    return ap.to_broadcast(shape)


def stage_load(nc, g, consts, vecs):
    with ExitStack() as stack:
        k = Kit(nc, stack, "load")
        landed = k.sem("landed")
        lam_rows = k.sb("lam_rows", [P, 4, 64])
        prod = k.sb("prod", [P, 2, 64])
        dots = k.sb("dots", [P, 2])
        exps = k.sb("exps", [P, 2])
        ch, ex = k.sem("dve"), k.sem("exp")
        block = stack.enter_context(nc.Block())

        @block.sync
        def _(sp):
            sp.dma_start(g.const[:], consts).then_inc(landed, 16)
            sp.dma_start(g.vec[:], vecs).then_inc(landed, 16)
            for i, v in enumerate(g.lam_in):
                sp.dma_start(lam_rows[:, i, :], v.to_broadcast([P, 64])).then_inc(landed, 16)

        @block.vector
        def _(dve):
            nc.vector.memset(g.ones[:], 1.0)
            nc.vector.memset(g.eps[:], EPS)
            dve.wait_ge(landed, 96)
            chain = Seq(dve, ch)
            for i in range(2):
                chain.link(nc.vector.tensor_tensor(prod[:, i, :], lam_rows[:, 2 * i, :], lam_rows[:, 2 * i + 1, :],
                                                   ALU.mult))
            chain.link(nc.vector.tensor_reduce(out=dots[:], in_=prod[:], axis=AX.X, op=ALU.add))
            gd = g.vcol("g_diff")
            chain.link(nc.vector.tensor_scalar(gd, gd, 1.0 - LAM_INIT, None, ALU.mult))
            dve.wait_ge(ex, 1)
            chain.link(nc.vector.tensor_tensor(g.lam[:, 0:1], exps[:, 0:1], exps[:, 1:2], ALU.subtract))
            chain.link(nc.vector.tensor_scalar(g.lam[:, 1:2], g.lam[:, 0:1], LAM_INIT, -1.0, ALU.add, ALU.mult))

        @block.scalar
        def _(act):
            act.wait_ge(ch, 3)
            nc.scalar.activation(exps[:], dots[:], ACT.Exp).then_inc(ex, 1)


def stage_ada(nc, g, w_ada, cT_dram):
    NC_ = 12
    with ExitStack() as stack:
        k = Kit(nc, stack, "ada")
        cT = k.sb("cT", [P, KB, C9])
        sT = k.sb("sT", [P, KB, C9])
        w = [k.sb(f"w{i}", [P, KB, 512]) for i in range(4)]
        rows = [k.sb(f"rows{i}", [C9, 512]) for i in range(2)]
        acc = [k.ps(f"acc{i}", [C9, 512]) for i in range(2)]
        modp = k.ps("modp", [P, 2, 512])
        c_in = k.sem("c_in")
        silu = k.sem("silu")
        w_in = [k.sem(f"w_in{i}") for i in range(4)]
        mm, ev, tr, dv = k.sem("mm"), k.sem("ev"), k.sem("tr"), k.sem("dv")
        block = stack.enter_context(nc.Block())
        n_all = 2 * NC_

        @block.sync
        def _(sp):
            sp.dma_start(cT[:], cT_dram).then_inc(c_in, 16)
            for i in range(4):
                sp.dma_start(w[i][:], w_ada[i]).then_inc(w_in[i], 16)
            with sp.Fori(1, n_all // 4) as j:
                for i in range(4):
                    sp.wait_ge(mm, j * 4 + (i - 3))
                    sp.dma_start(w[i][:], w_ada[j * 4 + i]).then_inc(w_in[i], 16)

        @block.scalar
        def _(act):
            act.wait_ge(c_in, 16)
            nc.scalar.activation(sT[:], cT[:], ACT.Silu).then_inc(silu, 1)
            for n in range(n_all):
                act.wait_ge(mm, n + 1)
                if n >= 2:
                    act.wait_ge(tr, n - 1)
                nc.scalar.activation(rows[n % 2][:], acc[n % 2][:], ACT.Copy).then_inc(ev, 1)

        @block.tensor
        def _(pe):
            pe.wait_ge(silu, 1)

            def turn(n):
                pe.wait_ge(ev, n + 1)
                for j in range(4):
                    l, b = divmod(n * 4 + j, NMOD)
                    last = nc.tensor.transpose(modp[:, l, b * C9:(b + 1) * C9], rows[n % 2][:, j * P:(j + 1) * P],
                                               g.ident()[0:C9, 0:C9])
                last.then_inc(tr, 1)

            for n in range(n_all):
                pe.wait_ge(w_in[n % 4], 16 * (n // 4 + 1))
                if n >= 2:
                    pe.wait_ge(ev, n - 1)
                for kk in range(KB):
                    last = nc.tensor.matmul(acc[n % 2][:], sT[:, kk, :], w[n % 4][:, kk, :],
                                            start=(kk == 0), stop=(kk == KB - 1))
                last.then_inc(mm, 1)
                if n >= 1:
                    turn(n - 1)
            turn(n_all - 1)

        @block.vector
        def _(dve):
            chain = Seq(dve, dv)
            dve.wait_ge(tr, n_all)
            for l in range(2):
                a = VEC["b_ada"][0] + l * NMOD
                chain.link(nc.vector.tensor_tensor(
                    g.mod[:, l], modp[:, l, 0:NMOD * C9].rearrange("p (b c) -> p b c", c=C9),
                    bc(g.vec[:, a:a + NMOD].rearrange("p (b c) -> p b c", c=1), [P, NMOD, C9]), ALU.add))
            for l in range(2):
                for part, name in ((1, "g_pre_mix"), (4, "g_pre_ffn")):
                    m = g.mod[:, l, part * KB:(part + 1) * KB, :]
                    chain.link(nc.vector.tensor_scalar(m, m, 1.0, None, ALU.add))
                for part, name in ((1, "g_pre_mix"), (2, "g_post_mix"), (4, "g_pre_ffn"), (5, "g_post_ffn")):
                    m = g.mod[:, l, part * KB:(part + 1) * KB, :]
                    a = VEC[name][0] + l * KB
                    chain.link(nc.vector.tensor_tensor(
                        m, m, bc(g.vec[:, a:a + KB].rearrange("p (b c) -> p b c", c=1), [P, KB, C9]), ALU.mult))


def stage_norm(nc, g, tag, spare, y, post, pre, x_in, x_out):
    with ExitStack() as stack:
        k = Kit(nc, stack, tag, spare)
        x = [k.sb(f"x{n}", [P, KB, TT]) for n in range(NT)]
        sq = [k.sb(f"sq{z}", [P, KB, TT]) for z in range(2)]
        hf = [k.sb(f"hf{z}", [P, KB, TT]) for z in range(2)]
        root = [k.sb(f"root{z}", [P, TT]) for z in range(2)]
        rstd = [k.sb(f"rstd{z}", [P, TT]) for z in range(2)]
        ss = [k.ps(f"ss{z}", [P, 512]) for z in range(2)]
        x_landed = [k.sem(f"x_landed{n}") for n in range(NT)]
        x_stored, squared, summed, logged, rooted, dv, scaled, hid = (
            k.sem(s) for s in ("x_stored", "squared", "summed", "logged", "rooted", "dve", "scaled", "hi"))
        block = stack.enter_context(nc.Block())
        if y is None:
            jobs = [("x", n) for n in range(NT)]
        elif pre is None:
            jobs = [("y", n) for n in range(NT)]
        else:
            jobs = [("y", 0), ("y", 1), ("x", 0), ("y", 2), ("x", 1), ("x", 2)]
        at = {}

        def mod(spec, off):
            l, part = spec
            return g.mod[:, l, (part + off) * KB:(part + off + 1) * KB, :]

        def sample_mod(spec, off):
            return bc(mod(spec, off)[:, :, 1:C9].rearrange("p b (c t) -> p b c t", t=1), [P, KB, NB, NS])

        def sample_cols(t):
            return t[:, :, PT:TT].rearrange("p b (c t) -> p b c t", t=NS)

        def prompt_cols(n):
            return TT if n < NT - 1 else PT

        @block.vector
        def _(dve):
            chain = Seq(dve, dv)

            def add_to_x(j, n):
                ys, pc = third(y, n), prompt_cols(n)
                dve.wait_ge(rooted, j + 1)
                chain.link(nc.vector.tensor_tensor(ys, ys, bc(rstd[j % 2][:, None, :], [P, KB, TT]), ALU.mult))
                at[("rstd", j)] = chain.n
                dve.wait_ge(x_landed[n], 16)
                for b in range(KB):
                    last = nc.vector.scalar_tensor_tensor(
                        out=x[n][:, b, 0:pc], in0=ys[:, b, 0:pc], scalar=mod(post, 0)[:, b, 0:1],
                        in1=x[n][:, b, 0:pc], op0=ALU.mult, op1=ALU.add)
                if n == NT - 1:
                    sy, sx = sample_cols(ys), sample_cols(x[n])
                    chain.link(nc.vector.tensor_tensor(sy, sy, sample_mod(post, 0), ALU.mult))
                    last = nc.vector.tensor_tensor(sx, sx, sy, ALU.add)
                chain.link(last)
                at[("x", n)] = chain.n

            def normalise_x(j, n):
                h = hf[n % 2]
                dve.wait_ge(rooted, j + 1)
                if n >= 2:
                    dve.wait_ge(hid, n - 1)
                chain.link(nc.vector.tensor_tensor(h[:], x[n][:], bc(rstd[j % 2][:, None, :], [P, KB, TT]), ALU.mult))
                at[("rstd", j)] = chain.n
                if n == NT - 1:
                    sh = sample_cols(h)
                    for off, op in ((1, ALU.mult), (0, ALU.add)):
                        chain.link(nc.vector.tensor_tensor(sh, sh, sample_mod(pre, off), op))
                at[("h", n)] = chain.n

            def low(n):
                dve.wait_ge(hid, n + 1)
                chain.link(nc.vector.tensor_tensor(third(g.alo, n), hf[n % 2][:], third(g.ahi, n).bitcast(F32),
                                                   ALU.subtract))

            for j in range(len(jobs) + 2):
                if j >= 2 and jobs[j - 2][0] == "x":
                    low(jobs[j - 2][1])
                if j < len(jobs):
                    (add_to_x if jobs[j][0] == "y" else normalise_x)(j, jobs[j][1])

        @block.sync
        def _(sp):
            for n in range(NT):
                sp.dma_start(x[n][:], x_in[:, :, n * TT:(n + 1) * TT]).then_inc(x_landed[n], 16)
            if y is not None:
                for n in range(NT):
                    sp.wait_ge(dv, at[("x", n)])
                    sp.dma_start(x_out[:, :, n * TT:(n + 1) * TT], x[n][:]).then_inc(x_stored, 16)
                sp.wait_ge(x_stored, 16 * NT)

        @block.scalar
        def _(act):
            def square(j, kind, n):
                if kind == "y":
                    src = third(y, n)
                else:
                    src = x[n][:]
                    if y is None:
                        act.wait_ge(x_landed[n], 16)
                    else:
                        act.wait_ge(dv, at[("x", n)])
                if j >= 2:
                    act.wait_ge(summed, j - 1)
                nc.scalar.activation(sq[j % 2][:], src, ACT.Square).then_inc(squared, 1)

            def reciprocal_root(j):
                act.wait_ge(summed, j + 1)
                if j >= 2:
                    act.wait_ge(rooted, j - 1)
                nc.scalar.activation(root[j % 2][:], ss[j % 2][:, 0:TT], ACT.Ln, scale=1.0 / D,
                                     bias=g.eps[:, 0:1]).then_inc(logged, 1)
                act.wait_ge(logged, j + 1)
                if j >= 2:
                    act.wait_ge(dv, at[("rstd", j - 2)])
                nc.scalar.activation(rstd[j % 2][:], root[j % 2][:], ACT.Exp, scale=-0.5).then_inc(rooted, 1)

            def scale_and_shift(n):
                pc = prompt_cols(n)
                act.wait_ge(dv, at[("h", n)])
                for b in range(KB):
                    last = nc.scalar.activation(hf[n % 2][:, b, 0:pc], hf[n % 2][:, b, 0:pc], ACT.Identity,
                                                scale=mod(pre, 1)[:, b, 0:1], bias=mod(pre, 0)[:, b, 0:1])
                last.then_inc(scaled, 1)

            for j in range(len(jobs) + 2):
                if j < len(jobs):
                    square(j, *jobs[j])
                if 1 <= j <= len(jobs):
                    reciprocal_root(j - 1)
                if j >= 2 and jobs[j - 2][0] == "x":
                    scale_and_shift(jobs[j - 2][1])

        @block.tensor
        def _(pe):
            for j in range(len(jobs)):
                pe.wait_ge(squared, j + 1)
                if j >= 2:
                    pe.wait_ge(logged, j - 1)
                for b in range(KB):
                    last = nc.tensor.matmul(ss[j % 2][:, 0:TT], g.ones[:], sq[j % 2][:, b, :],
                                            start=(b == 0), stop=(b == KB - 1))
                last.then_inc(summed, 1)

        if pre is not None:
            @block.gpsimd
            def _(pool):
                for n in range(NT):
                    pool.wait_ge(scaled, n + 1)
                    nc.gpsimd.tensor_tensor(third(g.ahi, n), hf[n % 2][:], bc(g.ones[:, 0:1, None], [P, KB, TT]),
                                            ALU.mult).then_inc(hid, 1)


def split_units(nc, pool, g, n_pairs, st, hi, lo, landed, made, freed, free_at, pool_chain):
    with pool.Fori(0, n_pairs) as i:
        for u in range(2):
            pool.wait_ge(landed[u], i * 16 + 16)
            pool.wait_ge(freed, free_at(i, u))
            shape = [P, st[u].shape[1]]
            nc.gpsimd.tensor_tensor(hi[u][:], st[u][:], bc(g.ones[:, 0:1], shape), ALU.mult).then_inc(pool_chain, 1)
            pool.wait_ge(pool_chain, i * 2 + (u + 1))
            nc.gpsimd.tensor_tensor(lo[u][:], st[u][:], hi[u][:].bitcast(F32), ALU.subtract).then_inc(made, 1)


def three_passes(nc, out, whi, wlo, xhi, xlo, nk):
    n = 0
    for kk in range(nk):
        for a, b in ((whi, xhi), (whi, xlo), (wlo, xhi)):
            last = nc.tensor.matmul(out, a(kk), b(kk), start=(n == 0), stop=(n == 3 * nk - 1))
            n += 1
    return last


def stage_linear(nc, g, tag, w, sections):
    n_units = sum(s[0] for s in sections)
    with ExitStack() as stack:
        k = Kit(nc, stack, tag)
        st = [k.sb(f"st{i}", [P, UW]) for i in range(2)]
        hi = [k.sb(f"hi{i}", [P, UW], F32R) for i in range(2)]
        lo = [k.sb(f"lo{i}", [P, UW], F32R) for i in range(2)]
        acc = [k.ps(f"acc{i}", [P, NT, 512]) for i in range(2)]
        landed = [k.sem(f"landed{i}") for i in range(2)]
        made, used, taken, pc = k.sem("made"), k.sem("used"), k.sem("taken"), k.sem("pool")
        block = stack.enter_context(nc.Block())

        @block.sync
        def _(sp):
            for u in range(2):
                sp.dma_start(st[u][:], w[u]).then_inc(landed[u], 16)
            with sp.Fori(1, n_units // 2) as i:
                for u in range(2):
                    sp.wait_ge(made, i * 2 + (u - 1))
                    sp.dma_start(st[u][:], w[i * 2 + u]).then_inc(landed[u], 16)

        @block.gpsimd
        def _(pool):
            split_units(nc, pool, g, n_units // 2, st, hi, lo, landed, made, used,
                        lambda i, u: i * 2 + (u + 1), pc)

        @block.tensor
        def _(pe):
            pe.sem_inc(used, 2)
            with pe.Fori(0, n_units // 2) as i:
                for u in range(2):
                    pe.wait_ge(made, i * 2 + (u + 1))
                    pe.wait_ge(taken, i * 2 + (u + 1))
                    for n in range(NT):
                        last = three_passes(nc, acc[u][:, n, 0:TT],
                                            lambda kk: hi[u][:, kk * P:(kk + 1) * P],
                                            lambda kk: lo[u][:, kk * P:(kk + 1) * P],
                                            lambda kk: third(g.ahi, n)[:, kk, :],
                                            lambda kk: third(g.alo, n)[:, kk, :], KB)
                    last.then_inc(used, 1)

        @block.scalar
        def _(act):
            act.sem_inc(taken, 2)
            at = 0
            for count, evacuate in sections:
                with act.Fori(at // 2, (at + count) // 2) as i:
                    for u in range(2):
                        act.wait_ge(used, i * 2 + (u + 3))
                        evacuate(i * 2 + (u - at), acc[u][:, :, 0:TT]).then_inc(taken, 1)
                at += count


class State:

    def __init__(self, nc, stack):
        def sb(name, shape, dt=F32):
            return stack.enter_context(nc.sbuf_tensor(name, shape, dt))

        self.const = sb("const", [P, NCONST])
        self.vec = sb("vec", [P, NVEC])
        self.ones = sb("ones", [P, P])
        self.eps = sb("eps", [P, 1])
        self.lam = sb("lam", [P, 2])
        self.mod = sb("mod", [P, 2, NMOD, C9])



    def col(self, name):
        return cols(self.const, name)

    def ident(self):
        return cols(self.const, "ident")

    def vcol(self, name):
        return cols(self.vec, name, VEC)

    def conv(self, l, c):
        cw, cb = VEC["conv_w"][0] + l * 2 * FB * 3, VEC["conv_b"][0] + l * 2 * FB
        return (lambda tap: self.vec[:, bass.ds(c * 3 + (cw + tap), 1)]), self.vec[:, bass.ds(c + cb, 1)]


def by_thirds(ap):
    return ap.rearrange("p o (n t) -> p (o n) t", n=NT)


def stage_project(nc, g, tag, spare, w, n_groups, rotate, dst, out):
    with ExitStack() as stack:
        k = Kit(nc, stack, tag, spare)
        GU = KB * GW
        st = [k.sb(f"st{i}", [P, GU]) for i in range(2)]
        hi = [k.sb(f"hi{i}", [P, GU], F32R) for i in range(2)]
        lo = [k.sb(f"lo{i}", [P, GU], F32R) for i in range(2)]
        NR = 3
        res = [k.sb(f"res{i}", [P, GW]) for i in range(NR)]
        acc = [k.ps(f"acc{i}", [P, 512]) for i in range(NR)]
        landed = [k.sem(f"landed{i}") for i in range(2)]
        stored = [k.sem(f"stored{i}") for i in range(NR)]
        made, used, summed, pc = k.sem("made"), k.sem("used"), k.sem("summed"), k.sem("pool")
        ready, turned, copied = k.sem("ready"), k.sem("turned"), k.sem("copied")
        if rotate:
            xc = k.sb("xc", [P, GW])
            xs = k.sb("xs", [P, GW])
            turn = [k.ps(f"turn{i}", [P, 2, P]) for i in range(2)]
            rc = k.sem("rc")
        block = stack.enter_context(nc.Block())
        rows = [P] * NCH + [TS]
        DEPTH = 2 * TILES

        @block.sync
        def _(sp):
            for u in range(2):
                sp.dma_start(st[u][:], w[u]).then_inc(landed[u], 16)
            if n_groups > 2:
                with sp.Fori(1, n_groups // 2) as i:
                    for u in range(2):
                        sp.wait_ge(made, i * 2 + (u - 1))
                        sp.dma_start(st[u][:], w[i * 2 + u]).then_inc(landed[u], 16)

        @block.gpsimd
        def _(pool):
            split_units(nc, pool, g, n_groups // 2, st, hi, lo, landed, made, summed,
                        lambda i, u: i * DEPTH + (u + 1) * TILES, pc)

        @block.tensor
        def _(pe):
            pe.sem_inc(summed, DEPTH)

            def transposes(i, q):
                pe.wait_ge(ready, i * DEPTH + (q + 1 + NR))
                pe.wait_ge(copied, i * DEPTH + (q + 1))
                for j in range(2):
                    last = nc.tensor.transpose(turn[q % 2][:, j, :], res[q % NR][:, j * P:(j + 1) * P], g.ident())
                last.then_inc(turned, 1)

            with pe.Fori(0, n_groups // 2) as i:
                for q in range(DEPTH):
                    u, t = divmod(q, TILES)
                    r = rows[t]
                    if t == 0:
                        pe.wait_ge(made, i * 2 + (u + 1))
                    pe.wait_ge(ready, i * DEPTH + (q + 1))
                    last = three_passes(nc, acc[q % NR][0:r, 0:GW],
                                        lambda kk: g.ahi[:, kk, t * P:t * P + r],
                                        lambda kk: g.alo[:, kk, t * P:t * P + r],
                                        lambda kk: hi[u][:, kk * GW:(kk + 1) * GW],
                                        lambda kk: lo[u][:, kk * GW:(kk + 1) * GW], KB)
                    last.then_inc(summed, 1)
                    if rotate and q >= 1:
                        transposes(i, q - 1)
                if rotate:
                    transposes(i, DEPTH - 1)

        if rotate:
            @block.vector
            def _(dve):
                dve.sem_inc(ready, NR)
                with dve.Fori(0, n_groups // 2) as i:
                    for q in range(DEPTH):
                        t = q % TILES
                        r = rows[t]
                        x = acc[q % NR][0:r, 0:GW].rearrange("p (h m d) -> p h m d", h=4, m=2)
                        c4 = xc[0:r].rearrange("p (h m d) -> p h m d", h=4, m=2)
                        s4 = xs[0:r].rearrange("p (h m d) -> p h m d", h=4, m=2)
                        cos = g.col("cos")[0:r, t * 32:(t + 1) * 32]
                        sin = g.col("sin")[0:r, t * 64:(t + 1) * 64].rearrange("p (m d) -> p m d", m=2)
                        dve.wait_ge(summed, i * DEPTH + (q + 1 + DEPTH))
                        dve.wait_ge(ready, i * DEPTH + (q + NR))
                        nc.vector.tensor_tensor(c4, x, bc(cos[:, None, None, :], [r, 4, 2, 32]), ALU.mult)
                        for m in range(2):
                            last = nc.vector.tensor_tensor(s4[:, :, m, :], x[:, :, 1 - m, :],
                                                           bc(sin[:, None, m, :], [r, 4, 32]), ALU.mult)
                        last.then_inc(rc, 1)
                        dve.wait_ge(rc, i * DEPTH + (q + 1))
                        dve.wait_ge(stored[q % NR], (i * (DEPTH // NR) + (q // NR + 1)) * 16)
                        dve.wait_ge(turned, i * DEPTH + (q + 1))
                        nc.vector.tensor_tensor(res[q % NR][0:r], xc[0:r], xs[0:r], ALU.add).then_inc(ready, 1)

        @block.scalar
        def _(act):
            for s in range(NR):
                act.sem_inc(stored[s], 16)
            act.sem_inc(copied, 2)
            if rotate:
                act.sem_inc(turned, NR)
            else:
                act.sem_inc(ready, NR)
            with act.Fori(0, n_groups // 2) as i:
                for q in range(DEPTH):
                    u, t = divmod(q, TILES)
                    r = rows[t]
                    if not rotate:
                        act.wait_ge(summed, i * DEPTH + (q + 1 + DEPTH))
                        act.wait_ge(stored[q % NR], (i * (DEPTH // NR) + (q // NR + 1)) * 16)
                        nc.scalar.activation(res[q % NR][0:r], acc[q % NR][0:r, 0:GW], ACT.Copy).then_inc(ready, 1)
                    act.wait_ge(ready, i * DEPTH + (q + 1 + NR))
                    act.dma_start(out[bass.ds(i * 2 + u, 1), t * P:t * P + r, :].rearrange("o p n -> p o n"),
                                  res[q % NR][0:r, None, :]).then_inc(stored[q % NR], 16)
                    if rotate:
                        act.wait_ge(turned, i * DEPTH + (q + 1 + NR))
                        nc.scalar.activation(dst[:, bass.ds(i * 4 + 2 * u, 2), t * P:t * P + r],
                                             turn[q % 2][:, :, 0:r], ACT.Copy).then_inc(copied, 1)
            for s in range(NR):
                act.wait_ge(stored[s], (n_groups // 2 * (DEPTH // NR) + 1) * 16)


def stage_ffn(nc, g, tag, l, w, y, conv_in, conv_out):
    PAIRS = FB // 2
    with ExitStack() as stack:
        k = Kit(nc, stack, tag)
        NSL = 3
        st = [k.sb(f"st{i}", [P, UW]) for i in range(2)]
        hi = [k.sb(f"hi{i}", [P, UW], F32R) for i in range(NSL)]
        lo = [k.sb(f"lo{i}", [P, UW], F32R) for i in range(NSL)]
        HIST = SEQ + 2
        UC = HIST + NB * (NS + 2)
        up = [k.sb(f"up{i}", [P, UC]) for i in range(2)]
        cv = [k.sb(f"cv{i}", [P, UC]) for i in range(2)]
        ghi = [k.sb(f"ghi{j}", [P, T], F32R) for j in range(2)]
        glo = [k.sb(f"glo{j}", [P, T], F32R) for j in range(2)]
        cin = k.sb("cin", [P, 2 * FB, NB, 2])
        cout = k.sb("cout", [P, 2 * FB, 2 * C9])
        acc = [k.ps(f"acc{i}", [P, NT, 512]) for i in range(2)]
        landed = [k.sem(f"landed{i}") for i in range(2)]
        made, used, pc = k.sem("made"), k.sem("used"), k.sem("pool")
        up_taken, down_taken, down_summed = k.sem("up_taken"), k.sem("down_taken"), k.sem("down_summed")
        cin_in, cout_out, affine, gelued, hid = (k.sem(x) for x in ("cin", "cout", "affine", "gelu", "hi"))
        conv = [k.sem(f"conv{i}") for i in range(2)]
        tap, prod, lod, zeroed = k.sem("tap"), k.sem("prod"), k.sem("lo"), k.sem("zeroed")
        block = stack.enter_context(nc.Block())

        def samples(t):
            return t[:, HIST:UC].rearrange("p (b c) -> p b c", c=NS + 2)

        @block.sync
        def _(sp):
            sp.dma_start(cin[:], conv_in).then_inc(cin_in, 16)
            for u in range(2):
                sp.dma_start(st[u][:], w[u]).then_inc(landed[u], 16)
            with sp.Fori(1, PAIRS * 3) as i:
                for u in range(2):
                    sp.wait_ge(made, i * 2 + (u - 1))
                    sp.dma_start(st[u][:], w[i * 2 + u]).then_inc(landed[u], 16)
            sp.wait_ge(up_taken, 2 * FB)
            sp.wait_ge(affine, 2 * FB)
            sp.dma_start(conv_out, cout[:]).then_inc(cout_out, 16)
            sp.wait_ge(cout_out, 16)

        @block.gpsimd
        def _(pool):
            with pool.Fori(0, PAIRS) as i:
                for u in range(6):
                    pool.wait_ge(landed[u % 2], i * 48 + 16 * (u // 2 + 1))
                    pool.wait_ge(used, i * 6 + (u + 1))
                    nc.gpsimd.tensor_tensor(hi[u % NSL][:], st[u % 2][:], bc(g.ones[:, 0:1], [P, UW]),
                                            ALU.mult).then_inc(pc, 1)
                    pool.wait_ge(pc, i * 6 + (u + 1))
                    nc.gpsimd.tensor_tensor(lo[u % NSL][:], st[u % 2][:], hi[u % NSL][:].bitcast(F32),
                                            ALU.subtract).then_inc(made, 1)

        @block.tensor
        def _(pe):
            pe.sem_inc(used, NSL)

            def up_unit(s, a, made_at, wait_sem, wait_at):
                pe.wait_ge(made, made_at)
                if wait_sem is not None:
                    pe.wait_ge(wait_sem, wait_at)
                for n in range(NT):
                    last = three_passes(nc, acc[a][:, n, 0:TT],
                                        lambda kk: hi[s][:, kk * P:(kk + 1) * P],
                                        lambda kk: lo[s][:, kk * P:(kk + 1) * P],
                                        lambda kk: third(g.ahi, n)[:, kk, :],
                                        lambda kk: third(g.alo, n)[:, kk, :], KB)
                last.then_inc(used, 1)

            def down(i, s0, s1, made_at, up_at, down_at):
                pe.wait_ge(made, made_at)
                pe.wait_ge(lod, i * 2)
                for m in range(KB):
                    if m < 2:
                        pe.wait_ge(up_taken, up_at + (m - 1))
                    else:
                        pe.wait_ge(down_taken, down_at + (m - 1))
                    for n in range(NT):
                        last = three_passes(nc, acc[m % 2][:, n, 0:TT],
                                            lambda j: hi[(s0, s1)[j]][:, m * P:(m + 1) * P],
                                            lambda j: lo[(s0, s1)[j]][:, m * P:(m + 1) * P],
                                            lambda j: ghi[j][:, n * TT:(n + 1) * TT],
                                            lambda j: glo[j][:, n * TT:(n + 1) * TT], 2)
                    if m < KB - 1:
                        last.then_inc(down_summed, 1)
                    else:
                        last.then_inc(used, 2)

            up_unit(0, 0, 1, None, 0)
            up_unit(1, 1, 2, None, 0)
            up_unit(2, 0, 3, up_taken, 1)
            up_unit(0, 1, 4, up_taken, 2)
            with pe.Fori(1, PAIRS) as i:
                up_unit(1, 0, i * 6 - 1, up_taken, i * 4 - 1)
                up_unit(2, 1, i * 6, up_taken, i * 4)
                down(i, 0, 1, i * 6 + 2, i * 4 + 2, i * 8 - 8)
                up_unit(2, 0, i * 6 + 3, down_taken, i * 8 - 1)
                up_unit(0, 1, i * 6 + 4, down_taken, i * 8)
            down(PAIRS, 1, 2, PAIRS * 6, PAIRS * 4, PAIRS * 8 - 8)

        @block.scalar
        def _(act):
            act.wait_ge(cin_in, 16)

            def hidden(n, j, first, used_a, used_b, down_used):
                for x in range(2):
                    c = n * 2 + x
                    act.wait_ge(used, (used_a, used_b)[x])
                    if not first:
                        act.wait_ge(conv[x], n)
                    nc.scalar.activation(up[x][:, 2:2 + 2 * TT].rearrange("p (n t) -> p n t", n=2),
                                         acc[x][:, 0:2, 0:TT], ACT.Copy)
                    nc.scalar.activation(up[x][:, 2 + 2 * TT:HIST], acc[x][:, 2, 0:PT], ACT.Copy)
                    nc.scalar.activation(samples(up[x])[:, :, 2:], acc[x][:, 2, PT:TT].rearrange(
                        "p (b t) -> p b t", t=NS), ACT.Copy)
                    nc.scalar.activation(samples(up[x])[:, None, :, 0:2], cin[:, bass.ds(c, 1), :, :],
                                         ACT.Copy).then_inc(up_taken, 1)
                    act.wait_ge(up_taken, c + 1)
                    nc.scalar.activation(cout[:, bass.ds(c, 1), 0:2], up[x][:, None, SEQ:HIST], ACT.Copy)
                    nc.scalar.activation(cout[:, bass.ds(c, 1), 2:].rearrange("p o (b t) -> p o b t", t=2),
                                         samples(up[x])[:, None, :, NS:], ACT.Copy)
                    if not first:
                        act.wait_ge(lod if x == 0 else prod, n)
                    wv, bv = g.conv(l, c)
                    nc.scalar.activation(cv[x][:, 2:], up[x][:, 2:], ACT.Identity, scale=wv(2), bias=bv)\
                        .then_inc(affine, 1)
                act.wait_ge(conv[0], n + 1)
                nc.scalar.activation(cv[0][:, 2:], cv[0][:, 2:], ACT.Gelu_apprx_tanh).then_inc(gelued, 1)
                act.wait_ge(prod, n + 1)
                if down_used is not None:
                    act.wait_ge(used, down_used)
                nc.scalar.activation(ghi[j][:, 0:SEQ], cv[0][:, 2:HIST], ACT.Copy)
                nc.scalar.activation(ghi[j][:, SEQ:T].rearrange("p (b t) -> p b t", t=NS),
                                     samples(cv[0])[:, :, 2:], ACT.Copy).then_inc(hid, 1)

            hidden(0, 0, True, 1 + NSL, 2 + NSL, None)
            hidden(1, 1, False, 3 + NSL, 4 + NSL, None)
            with act.Fori(1, PAIRS) as i:
                hidden(i * 2, 0, False, i * 6 + (NSL - 1), i * 6 + NSL, i * 6 + (NSL + 2))
                hidden(i * 2 + 1, 1, False, i * 6 + (NSL + 3), i * 6 + (NSL + 4), None)

        @block.vector
        def _(dve):
            for x in range(2):
                nc.vector.memset(up[x][:, 0:2], 0.0)
            nc.vector.memset(y[:], 0.0).then_inc(zeroed, 1)
            dve.wait_ge(zeroed, 1)

            def taps(n, x):
                wv, _ = g.conv(l, n * 2 + x)
                dve.wait_ge(affine, n * 2 + (x + 1))
                nc.vector.scalar_tensor_tensor(out=cv[x][:, 2:], in0=up[x][:, 1:UC - 1], scalar=wv(1),
                                               in1=cv[x][:, 2:], op0=ALU.mult, op1=ALU.add).then_inc(tap, 1)
                dve.wait_ge(tap, n * 2 + (x + 1))
                nc.vector.scalar_tensor_tensor(out=cv[x][:, 2:], in0=up[x][:, 0:UC - 2], scalar=wv(0),
                                               in1=cv[x][:, 2:], op0=ALU.mult, op1=ALU.add).then_inc(conv[x], 1)

            def gate(n):
                dve.wait_ge(gelued, n + 1)
                dve.wait_ge(conv[1], n + 1)
                nc.vector.tensor_tensor(cv[0][:, 2:], cv[0][:, 2:], cv[1][:, 2:], ALU.mult).then_inc(prod, 1)

            def low(n, j):
                dve.wait_ge(hid, n + 1)
                nc.vector.tensor_tensor(glo[j][:, 0:SEQ], cv[0][:, 2:HIST], ghi[j][:, 0:SEQ].bitcast(F32),
                                        ALU.subtract)
                nc.vector.tensor_tensor(glo[j][:, SEQ:T].rearrange("p (b t) -> p b t", t=NS),
                                        samples(cv[0])[:, :, 2:],
                                        ghi[j][:, SEQ:T].bitcast(F32).rearrange("p (b t) -> p b t", t=NS),
                                        ALU.subtract).then_inc(lod, 1)

            def add(i, m, first_used):
                if m < KB - 1:
                    dve.wait_ge(down_summed, i * 7 + (m - 6))
                else:
                    dve.wait_ge(used, first_used)
                ym = by_thirds(y[:, m:m + 1, :])
                nc.vector.tensor_tensor(ym, ym, acc[m % 2][:, :, 0:TT], ALU.add).then_inc(down_taken, 1)

            for n in range(2):
                taps(n, 0)
                taps(n, 1)
                gate(n)
                low(n, n)
            with dve.Fori(1, PAIRS) as i:
                u = i * 6 + (NSL + 2)
                add(i, 0, u)
                taps(i * 2, 0)
                add(i, 1, u)
                taps(i * 2, 1)
                add(i, 2, u)
                add(i, 3, u)
                gate(i * 2)
                for m in range(4, KB):
                    add(i, m, u)
                low(i * 2, 0)
                taps(i * 2 + 1, 0)
                taps(i * 2 + 1, 1)
                gate(i * 2 + 1)
                low(i * 2 + 1, 1)
            for m in range(KB):
                add(PAIRS, m, PAIRS * 6 + NSL)


QA, QB, KA, KBK = 0, 2, 6, 8
KA_GROUP, VA_GROUP, VB_GROUP = 3, 0, 2


def stage_retention(nc, g, qkT, rot, val, o, state_in, state_out, sstate_out):
    with ExitStack() as stack:
        k = Kit(nc, stack, "ret")
        v = [k.sb(f"v{z}", [P, H, DV]) for z in range(2)]
        kn = [k.sb(f"kn{z}", [P, 256]) for z in range(2)]
        kc = [k.sb(f"kc{z}", [P, 2, CH]) for z in range(2)]
        qz = [k.sb(f"qz{z}", [P, H, CH]) for z in range(2)]
        qd = [k.sb(f"qd{z}", [P, H, CH]) for z in range(2)]
        ks = [k.sb(f"ks{z}", [P, 256]) for z in range(2)]
        sm = [k.sb(f"sm{z}", [P, H, CH]) for z in range(2)]
        S = k.sb("S", [P, 2, DV])
        ps_s = [k.ps(f"ps_s{z}", [P, H, CH]) for z in range(2)]
        ps_o = [k.ps(f"ps_o{z}", [P, H, CH]) for z in range(2)]
        ps_d = k.ps("ps_d", [P, 2, 4 * DV])
        v_in = [k.sem(f"v_in{z}") for z in range(2)]
        zeroed, kcopied, qready, scored, masked = (k.sem(x) for x in ("zeroed", "kcopied", "qready", "scored", "masked"))
        summed, deltaed, stated, copied = (k.sem(x) for x in ("summed", "deltaed", "stated", "copied"))
        state_stored = k.sem("state_stored")
        block = stack.enter_context(nc.Block())

        def v_src(at, n):
            return val[VA_GROUP:VA_GROUP + 2, at, :].rearrange("g p f -> p g f")

        @block.sync
        def _(sp):
            def load(z, at):
                sp.dma_start(v[z][:].rearrange("p (g h) e -> p g (h e)", g=2), v_src(at, CH)).then_inc(v_in[z], 16)
                sp.dma_start(kn[z][:], rot[KA_GROUP, at, :]).then_inc(v_in[z], 16)

            for z in range(2):
                load(z, slice(z * CH, (z + 1) * CH))
            with sp.Fori(1, NCH // 2) as i:
                for z in range(2):
                    sp.wait_ge(deltaed, i * 2 + (z + 1))
                    load(z, bass.ds(i * 2 * CH + z * CH, CH))
            sp.wait_ge(stated, NCH + 1)
            sp.dma_start(state_out, S[:]).then_inc(state_stored, 16)
            sp.wait_ge(state_stored, 16)

        @block.scalar
        def _(act):
            act.sem_inc(copied, 2)
            with act.Fori(0, NCH // 2) as i:
                for z in range(2):
                    act.wait_ge(scored, i * 2 + (z + 1))
                    nc.scalar.activation(kc[z][:], qkT[:, KA:KA + 2, bass.ds(i * 2 * CH + z * CH, CH)],
                                         ACT.Copy).then_inc(kcopied, 1)
                for z in range(2):
                    act.wait_ge(summed, i * 2 + (z + 1))
                    nc.scalar.activation(o[:, 0:H, bass.ds(i * 2 * CH + z * CH, CH)], ps_o[z][:],
                                         ACT.Copy).then_inc(copied, 1)

        @block.tensor
        def _(pe):
            pe.sem_inc(scored, 2)
            pe.sem_inc(deltaed, 2)

            def score(i, z):
                pe.wait_ge(kcopied, i * 2 + (z + 1))
                pe.wait_ge(qready, i * 2 + (z + 1))
                for h in range(H):
                    last = nc.tensor.matmul(ps_s[z][:, h, :], kc[z][:, h // 2, :], qz[z][:, h, :],
                                            start=True, stop=True)
                last.then_inc(scored, 1)

            with pe.Fori(0, NCH // 2) as i:
                for z in range(2):
                    score(i, z)
                for z in range(2):
                    pe.wait_ge(v_in[z], i * 32 + 32)
                    pe.wait_ge(masked, i * 2 + (z + 1))
                    pe.wait_ge(stated, i * 2 + (z + 1))
                    pe.wait_ge(copied, i * 2 + (z + 1))
                    for h in range(H):
                        nc.tensor.matmul(ps_o[z][:, h, :], v[z][:, h, :], sm[z][:, h, :], start=True, stop=False)
                        last = nc.tensor.matmul(ps_o[z][:, h, :], S[:, h // 2, :], qd[z][:, h, :],
                                                start=False, stop=True)
                    last.then_inc(summed, 1)
                    for h in range(H):
                        last = nc.tensor.matmul(ps_d[64 * (h % 2):64 * (h % 2) + 64, 0, (h // 2) * DV:(h // 2 + 1) * DV],
                                                ks[z][:, h * 64:(h + 1) * 64], v[z][:, h, :], start=True, stop=True)
                    last.then_inc(deltaed, 1)

        @block.vector
        def _(dve):
            for z in range(2):
                nc.vector.memset(qz[z][:], 0.0)
            nc.vector.memset(S[:], 0.0).then_inc(zeroed, 1)
            dve.wait_ge(zeroed, 1)
            dve.sem_inc(stated, 1)
            with dve.Fori(0, NCH // 2) as i:
                for z in range(2):
                    at = bass.ds(i * 2 * CH + z * CH, CH)
                    dve.wait_ge(deltaed, i * 2 + (z + 1))
                    for s in range(2):
                        last = nc.vector.tensor_copy(qz[z][64 * s:64 * s + 64, s::2, :],
                                                     qkT[64 * s:64 * s + 64, QA:QA + 2, at])
                    last.then_inc(qready, 1)
                    dve.wait_ge(qready, i * 2 + (z + 1))
                    nc.vector.tensor_tensor(qd[z][:], qz[z][:], g.col("decq").rearrange("p (h i) -> p h i", h=H), ALU.mult)
                    dve.wait_ge(v_in[z], i * 32 + 32)
                    nc.vector.tensor_tensor(ks[z][:].rearrange("p (h d) -> p h d", h=H),
                                            kn[z][:].rearrange("p (h d) -> p h d", h=H),
                                            bc(g.col("deck")[:, :, None], [P, H, 64]), ALU.mult)
                    dve.wait_ge(scored, i * 2 + (z + 3))
                    nc.vector.tensor_tensor(sm[z][:], ps_s[z][:], g.col("decay").rearrange("p (h i) -> p h i", h=H),
                                            ALU.mult).then_inc(masked, 1)
                for z in range(2):
                    dve.wait_ge(deltaed, i * 2 + (z + 3))
                    for b in range(2):
                        last = nc.vector.scalar_tensor_tensor(
                            out=S[:, b, :], in0=S[:, b, :], scalar=g.col("decc")[:, b:b + 1],
                            in1=ps_d[:, 0, b * DV:(b + 1) * DV], op0=ALU.mult, op1=ALU.add)
                    last.then_inc(stated, 1)

    with ExitStack() as stack:
        k = Kit(nc, stack, "rets")
        v = k.sb("v", [TS, H, DV])
        vm = k.sb("vm", [TS, H, NB, DV])
        kn = k.sb("kn", [TS, 256])
        ks = k.sb("ks", [TS, 256])
        qz = k.sb("qz", [P, H, TS])
        qd = k.sb("qd", [P, H, TS])
        sm = k.sb("sm", [TS, H, TS])
        ss = k.sb("ss", [P, NB, 2, DV])
        ps_s = k.ps("ps_s", [TS, H, TS])
        ps_o = k.ps("ps_o", [P, H, TS])
        ps_d = k.ps("ps_d", [P, 2, NB, DV])
        landed, out_done = k.sem("landed"), k.sem("out_done")
        qready, scored, masked, summed, deltaed, stated, dv = (
            k.sem(x) for x in ("qready", "scored", "masked", "summed", "deltaed", "stated", "dv"))
        block = stack.enter_context(nc.Block())

        @block.sync
        def _(sp):
            sp.dma_start(v[:].rearrange("p (g h) e -> p g (h e)", g=2),
                         val[VA_GROUP:VA_GROUP + 2, SEQ:T, :].rearrange("g p f -> p g f")).then_inc(landed, 16)
            sp.dma_start(kn[:], rot[KA_GROUP, SEQ:T, :]).then_inc(landed, 16)
            sp.dma_start(ss[:], state_in).then_inc(landed, 16)
            sp.wait_ge(stated, 1)
            sp.dma_start(sstate_out, ss[:]).then_inc(out_done, 16)
            sp.wait_ge(out_done, 16)

        @block.tensor
        def _(pe):
            pe.wait_ge(qready, 1)
            for h in range(H):
                last = nc.tensor.matmul(ps_s[:, h, :], qkT[:, KA + h // 2, SEQ:T], qz[:, h, :], start=True, stop=True)
            last.then_inc(scored, 1)
            pe.wait_ge(landed, 48)
            pe.wait_ge(masked, 1)
            for h in range(H):
                nc.tensor.matmul(ps_o[:, h, :], v[:, h, :], sm[:, h, :], start=True, stop=False)
                for b in range(NB):
                    last = nc.tensor.matmul(ps_o[:, h, b * NS:(b + 1) * NS], ss[:, b, h // 2, :],
                                            qd[:, h, b * NS:(b + 1) * NS], start=False, stop=(b == NB - 1))
            last.then_inc(summed, 1)
            for h in range(H):
                for n in range(2):
                    last = nc.tensor.matmul(ps_d[64 * (h % 2):64 * (h % 2) + 64, h // 2, n * 4:n * 4 + 4, :],
                                            ks[:, h * 64:(h + 1) * 64], vm[:, h, n * 4:n * 4 + 4, :],
                                            start=True, stop=True)
            last.then_inc(deltaed, 1)

        @block.vector
        def _(dve):
            chain = Seq(dve, dv)
            chain.link(nc.vector.memset(qz[:], 0.0))
            for s in range(2):
                last = nc.vector.tensor_copy(qz[64 * s:64 * s + 64, s::2, :], qkT[64 * s:64 * s + 64, QA:QA + 2, SEQ:T])
            last.then_inc(qready, 1)
            dve.wait_ge(qready, 1)
            nc.vector.tensor_tensor(qd[:], qz[:], g.col("sdecq").rearrange("p (h i) -> p h i", h=H), ALU.mult)
            dve.wait_ge(landed, 48)
            nc.vector.tensor_tensor(ks[:].rearrange("p (h d) -> p h d", h=H), kn[:].rearrange("p (h d) -> p h d", h=H),
                                    bc(g.col("sdeck")[0:TS, :, None], [TS, H, 64]), ALU.mult)
            for b in range(NB):
                nc.vector.tensor_scalar(vm[:, :, b, :], v[:], g.col("bmask")[0:TS, b:b + 1], None, ALU.mult)
            dve.wait_ge(scored, 1)
            nc.vector.tensor_tensor(sm[:], ps_s[:], g.col("sdecay")[0:TS].rearrange("p (h i) -> p h i", h=H),
                                    ALU.mult).then_inc(masked, 1)
            dve.wait_ge(deltaed, 1)
            for b in range(2):
                last = nc.vector.scalar_tensor_tensor(out=ss[:, :, b, :], in0=ss[:, :, b, :],
                                                      scalar=g.col("sdecc")[:, b:b + 1], in1=ps_d[:, b, :, :],
                                                      op0=ALU.mult, op1=ALU.add)
            last.then_inc(stated, 1)

        @block.scalar
        def _(act):
            act.wait_ge(summed, 1)
            nc.scalar.activation(o[:, 0:H, SEQ:T], ps_o[:], ACT.Copy)


def stage_store(nc, tag, pairs):
    with ExitStack() as stack:
        stored = Kit(nc, stack, tag).sem("stored")
        block = stack.enter_context(nc.Block())

        @block.sync
        def _(sp):
            for dst, src in pairs:
                sp.dma_start(dst, src).then_inc(stored, 16)
            sp.wait_ge(stored, 16 * len(pairs))


def stage_attention(nc, g, qkT, cache_k, cache_v, pages, val, o):
    SC = 64 ** -0.5
    STEPS = 2 * NCH
    G = 4
    GP = NPG // G
    ROWS = 2 * H * NS
    SPP = NB * NCH // (H * NCH)
    SEQS = 2 * SPP
    WIN = STEPS // SEQS
    BT = 4
    with ExitStack() as stack:
        k = Kit(nc, stack, "att")
        v = [k.sb(f"v{u}", [P, NCH, DV]) for u in range(2)]
        qz = [k.sb(f"qz{z}", [P, 2, CH]) for z in range(2)]
        p = [k.sb(f"p{z}", [P, SEQ]) for z in range(3)]
        p2 = k.sb("second", [P, SEQ])
        aT = [k.sb(f"aT{z}", [P, NCH, CH]) for z in range(2)]
        mx, nm, sums, rs = (k.sb(x, [P, 2]) for x in ("mx", "nm", "sums", "rs"))
        ps_s = k.ps("ps_s", [P, 2, SEQ])
        ps_t = k.ps("ps_t", [P, BT, CH])
        ps_o = k.ps("ps_o", [P, 512])
        v_in = [k.sem(f"v_in{u}") for u in range(2)]
        zeroed, qready, scored, maxed, exped = (k.sem(x) for x in ("zeroed", "qready", "scored", "maxed", "exped"))
        mixed, turned, aready, summed, copied, dv = (
            k.sem(x) for x in ("mixed", "turned", "aready", "summed", "copied", "dv"))

        kt = [k.sb(f"kt{n}", [P, GP, H, PAGE]) for n in range(G)]
        vt = [k.sb(f"vt{n}", [P, GP, H * DV]) for n in range(G)]
        vn = k.sb("vn", [NS, H * DV])
        ids = k.sb("ids", [1, NB * NPG], I32)
        cqz = k.sb("cqz", [P, H * (ROWS + 2 * NS)])
        ckn = k.sb("ckn", [P, H, NS])
        cp = k.sb("cp", [P, GP * PAGE])
        cpn = k.sb("cpn", [P, NS])
        cpT = k.sb("cpT", [P, GP, P])
        cpnT = k.sb("cpnT", [NS, P])
        os_ = k.sb("os", [P, H * DV])
        cmx, csums = k.sb("cmx", [P, 2]), k.sb("csums", [P, 2])
        cm, cnm, cs, cw = (k.sb(x, [P, 1]) for x in ("cm", "cnm", "cs", "cw"))
        erow, wrow = k.sb("erow", [1, G, ROWS]), k.sb("wrow", [1, G, ROWS])
        top, total, coef = (k.sb(x, [1, ROWS]) for x in ("top", "total", "coef"))
        bank_a = k.ps("bank_a", [P, 512])
        bank_b = k.ps("bank_b", [P, 512])
        ids_in, vn_in = k.sem("ids_in"), k.sem("vn_in")
        k_in = [k.sem(f"k_in{n}") for n in range(G)]
        cv_in = [k.sem(f"cv_in{n}") for n in range(G)]
        c_zeroed, c_qready, c_scored, c_maxed, c_exped, c_sums, c_turned, c_pready = (
            k.sem(f"c_{x}") for x in ("zeroed", "qready", "scored", "maxed", "exped", "sums", "turned", "pready"))
        c_diff, c_rexp, c_weighted, c_summed, c_wcol, c_scaled, c_picked, c_copied, c_dv = (
            k.sem(f"c_{x}") for x in ("diff", "rexp", "weighted", "summed", "wcol", "scaled", "picked", "copied", "dv"))
        block = stack.enter_context(nc.Block())
        W_COL, PICK = slice(0, 1), 16
        NEW_T, M_ROW, S_ROW, NEW = slice(0, P), slice(P, 2 * P), slice(2 * P, 3 * P), slice(3 * P, 3 * P + NS)

        def batches(s):
            return s % NCH // BT + 1

        PASS_BT = sum(batches(s) for s in range(STEPS))

        def batch_at(s):
            return sum(batches(x) for x in range(s))

        def new_cols(i, r):
            return bass.ds(i * (SEQS * NS) + (SEQ + r * NS), NS)

        @block.sync
        def _(sp):
            sp.dma_start(ids[:], pages.rearrange("b p -> (b p)")[None, :]).then_inc(ids_in, 16)
            sp.wait_ge(ids_in, 16)
            with sp.Fori(0, NB) as q:
                page = [sp.value_load(ids[0:1, bass.ds(q * NPG + j, 1)], min_val=0, max_val=cache_k.shape[0] - 1)
                        for j in range(NPG)]

                def load(n, cache, order, dst, sem):
                    for j in range(GP):
                        sp.dma_start(dst[:, j:j + 1], cache[bass.ds(page[n * GP + j], 1)].rearrange(order)).then_inc(sem, 16)

                sp.wait_ge(c_scored, q + 1)
                for n in range(G):
                    load(n, cache_k, "o p h k -> p o h k", kt[n], k_in[n])
                sp.wait_ge(c_summed, q + 1)
                sp.dma_start(vn[:].rearrange("t (g f) -> t g f", g=2), val[VB_GROUP:VB_GROUP + 2,
                             bass.ds(q * NS + SEQ, NS), :].rearrange("g t f -> t g f")).then_inc(vn_in, 16)
                for n in range(G):
                    load(n, cache_v, "o p f -> p o f", vt[n], cv_in[n])

        @block.gpsimd
        def _(pool):
            for z in range(2):
                last = nc.gpsimd.memset(qz[z][:], 0.0)
            last.then_inc(zeroed, 1)
            pool.wait_ge(zeroed, 1)
            with pool.Fori(0, H // 2) as i:
                for s in range(STEPS):
                    u, qb = divmod(s, NCH)
                    pool.wait_ge(scored, i * (2 * STEPS) + (2 * s + 2))
                    for m in range(2):
                        last = nc.gpsimd.tensor_copy(
                            qz[s % 2][64 * m:64 * m + 64, m:m + 1, :],
                            qkT[64 * m:64 * m + 64, bass.ds(i * 2 + (QB + u), 1), qb * CH:(qb + 1) * CH])
                    last.then_inc(qready, 1)

        @block.tensor
        def _(pe):
            pe.sem_inc(scored, 4)
            pe.sem_inc(turned, PASS_BT)
            pe.sem_inc(summed, STEPS)
            pe.sem_inc(c_scored, 1)
            pe.sem_inc(c_summed, 1)

            def score(i, s):
                u, qb = divmod(s, NCH)
                pe.wait_ge(qready, i * STEPS + (s + 1))
                for m in range(2):
                    pe.wait_ge(exped, i * (2 * STEPS) + (2 * s + m + 1))
                    for a in range(0, (qb + 1) * CH, 512):
                        b = min(a + 512, (qb + 1) * CH)
                        last = nc.tensor.matmul(ps_s[:, m, a:b], qz[s % 2][:, m, :],
                                                qkT[:, bass.ds(i * 2 + (KBK + u), 1), a:b].rearrange("p o k -> p (o k)"),
                                                start=True, stop=True)
                    last.then_inc(scored, 1)

            def turn(i, s, c):
                if c == 0:
                    pe.wait_ge(mixed, i * STEPS + (s + 1))
                pe.wait_ge(aready, i * PASS_BT + (batch_at(s) + c + 1))
                for j in range(c * BT, min(c * BT + BT, s % NCH + 1)):
                    last = nc.tensor.transpose(ps_t[:, j % BT, :], p[s % 3][:, j * CH:(j + 1) * CH], g.ident())
                last.then_inc(turned, 1)

            def product(i, s):
                u, qb = divmod(s, NCH)
                if qb == 0:
                    pe.wait_ge(v_in[u], i * 16 + 16)
                pe.wait_ge(aready, i * PASS_BT + (batch_at(s + 1) + 1))
                pe.wait_ge(copied, i * STEPS + (s + 1))
                for j in range(qb + 1):
                    last = nc.tensor.matmul(ps_o[:, 0:CH], v[u][:, j, :], aT[s % 2][:, j, :],
                                            start=(j == 0), stop=(j == qb))
                last.then_inc(summed, 1)

            def cached_scores(i, r):
                pe.wait_ge(c_qready, i * SEQS + (r + 1))
                pe.wait_ge(c_scaled, i * SEQS + (r + 1))
                for h in range(H):
                    for n in range(G):
                        nc.tensor.matmul(bank_b[n * ROWS:(n + 1) * ROWS, NEW], cqz[:, h * ROWS:(h + 1) * ROWS],
                                         ckn[:, h, :], start=(h == 0), stop=(h == H - 1))
                pe.wait_ge(c_copied, i * SEQS + (r + 1))
                for n in range(G):
                    pe.wait_ge(k_in[n], i * (SEQS * 16 * GP) + (r + 1) * (16 * GP))
                for h in range(H):
                    for n in range(G):
                        last = nc.tensor.matmul(bank_a[n * ROWS:(n + 1) * ROWS, :], cqz[:, h * ROWS:(h + 1) * ROWS],
                                                kt[n][:, :, h, :], start=(h == 0), stop=(h == H - 1))
                last.then_inc(c_scored, 1)

            def cached_turns(i, r):
                pe.wait_ge(c_sums, i * SEQS + (r + 1))
                for j in range(GP):
                    nc.tensor.transpose(bank_a[:, j * P:(j + 1) * P], cp[:, j * PAGE:(j + 1) * PAGE], g.ident())
                nc.tensor.matmul(bank_b[0:NS, NEW_T], cpn[:], g.ident(), start=True, stop=True)
                nc.tensor.matmul(bank_b[0:1, M_ROW], cm[:], g.ident(), start=True, stop=True)
                nc.tensor.matmul(bank_b[0:1, S_ROW], cs[:], g.ident(), start=True, stop=True).then_inc(c_turned, 1)

            def cached_products(i, r):
                pe.wait_ge(c_pready, i * SEQS + (r + 1))
                pe.wait_ge(c_weighted, i * SEQS + (r + 1))
                nc.tensor.matmul(bank_a[:, W_COL], wrow[:].rearrange("o g r -> o (g r)"), g.ones[0:1, 0:1],
                                 start=True, stop=True)
                pe.wait_ge(vn_in, i * (SEQS * 16) + (r + 1) * 16)
                for n in range(G):
                    pe.wait_ge(cv_in[n], i * (SEQS * 16 * GP) + (r + 1) * (16 * GP))
                for j in range(GP):
                    for n in range(G):
                        nc.tensor.matmul(bank_b[n * ROWS:(n + 1) * ROWS, :], cpT[:, j, n * ROWS:(n + 1) * ROWS],
                                         vt[n][:, j, :], start=(j == 0), stop=(j == GP - 1 and n < G - 1))
                n = G - 1
                nc.tensor.matmul(bank_b[n * ROWS:(n + 1) * ROWS, :], cpnT[:, n * ROWS:(n + 1) * ROWS], vn[:],
                                 start=False, stop=True).then_inc(c_summed, 1)

            def cached_picks(i, r):
                pe.wait_ge(c_scaled, i * SEQS + (r + 2))
                for h in range(H):
                    last = nc.tensor.matmul(bank_a[:, PICK + h * NS:PICK + (h + 1) * NS], os_[:, h * DV:(h + 1) * DV],
                                            g.col("sel")[:, h * NS:(h + 1) * NS], start=True, stop=True)
                last.then_inc(c_picked, 1)

            with pe.Fori(0, H // 2) as i:
                for s in range(STEPS + 3):
                    if s < STEPS:
                        score(i, s)
                    if 2 <= s < STEPS + 2:
                        for c in range(batches(s - 2)):
                            turn(i, s - 2, c)
                    if s < STEPS:
                        (cached_scores, cached_turns, cached_products, cached_picks)[s % WIN](i, s // WIN)
                    if s >= 3:
                        product(i, s - 3)

        @block.vector
        def _(dve):
            start = Seq(dve, c_zeroed)
            start.link(nc.vector.memset(cqz[:], 0.0))
            maps = g.col("maps")[0:1]
            start.link(nc.vector.scalar_tensor_tensor(out=coef[:], in0=maps[:, ROWS:2 * ROWS], scalar=g.lam[0:1, 1:2],
                                                      in1=maps[:, 0:ROWS], op0=ALU.mult, op1=ALU.add))

            LINKS = 7

            def masked_max(i, s):
                qb = s % NCH
                L = (qb + 1) * CH
                for m in range(2):
                    link = i * (LINKS * STEPS) + (LINKS * s + 2 * m)
                    diag = ps_s[:, m, qb * CH:L]
                    dve.wait_ge(scored, i * (2 * STEPS) + (2 * s + m + 5))
                    nc.vector.tensor_tensor(diag, diag, g.col("causal"), ALU.add).then_inc(dv, 1)
                    dve.wait_ge(dv, link + 1)
                    nc.vector.tensor_reduce(out=mx[:, m:m + 1], in_=ps_s[:, m, 0:L], axis=AX.X, op=ALU.max)\
                        .then_inc(dv, 1)
                    dve.wait_ge(dv, link + 2)
                    dve.wait_ge(exped, i * (2 * STEPS) + (2 * s + m + 1))
                    nc.vector.tensor_scalar(nm[:, m:m + 1], mx[:, m:m + 1], -SC, None, ALU.mult).then_inc(maxed, 1)

            def mix(i, s):
                L = (s % NCH + 1) * CH
                link = i * (LINKS * STEPS) + (LINKS * s + 4)
                dve.wait_ge(exped, i * (2 * STEPS) + (2 * s + 4))
                nc.vector.reciprocal(rs[:], sums[:]).then_inc(dv, 1)
                dve.wait_ge(dv, link + 1)
                nc.vector.tensor_tensor(rs[:, 1:2], rs[:, 1:2], g.lam[:, 1:2], ALU.mult).then_inc(dv, 1)
                mine = p[s % 3][:, 0:L]
                nc.vector.tensor_scalar(mine, mine, rs[:, 0:1], None, ALU.mult).then_inc(dv, 1)
                dve.wait_ge(dv, link + 3)
                nc.vector.scalar_tensor_tensor(out=mine, in0=p2[:, 0:L], scalar=rs[:, 1:2], in1=mine, op0=ALU.mult, op1=ALU.add).then_inc(mixed, 1)

            C_LINKS = 8

            def cached_chain(i, r, n):
                chain = Seq(dve, c_dv)
                chain.base = i * (SEQS * C_LINKS) + (r * C_LINKS + n)
                return chain

            def cached_queries(i, r):
                dve.wait_ge(c_scored, i * SEQS + (r + 1))
                nc.vector.tensor_copy(ckn[:], qkT[:, KBK:KBK + H, new_cols(i, r)])
                for m in range(2):
                    last = nc.vector.tensor_copy(
                        cqz[64 * m:64 * m + 64, :].rearrange("p (h c) -> p h c", h=H)[:, :, m * NS:(m + 1) * NS],
                        qkT[64 * m:64 * m + 64, QB:QB + H, new_cols(i, r)])
                last.then_inc(c_qready, 1)

            def cached_max(i, r):
                chain = cached_chain(i, r, 0)
                dve.wait_ge(c_scored, i * SEQS + (r + 2))
                chain.link(nc.vector.tensor_tensor(bank_b[:, NEW], bank_b[:, NEW], g.col("smask"), ALU.add))
                nc.vector.tensor_reduce(out=cmx[:, 0:1], in_=bank_a[:], axis=AX.X, op=ALU.max)
                chain.link(nc.vector.tensor_reduce(out=cmx[:, 1:2], in_=bank_b[:, NEW], axis=AX.X, op=ALU.max))
                dve.wait_ge(c_turned, i * SEQS + (r + 1))
                chain.link(nc.vector.tensor_reduce(out=cm[:], in_=cmx[:], axis=AX.X, op=ALU.max))
                dve.wait_ge(c_exped, i * SEQS + (r + 1))
                nc.vector.tensor_scalar(cnm[:], cm[:], -SC, None, ALU.mult).then_inc(c_maxed, 1)

            def cached_sums(i, r):
                dve.wait_ge(c_exped, i * SEQS + (r + 2))
                nc.vector.tensor_reduce(out=cs[:], in_=csums[:], axis=AX.X, op=ALU.add).then_inc(c_sums, 1)

            def rows(cols_):
                return bank_b[0:1, cols_].rearrange("o (g r) -> o g r", g=G)

            def cached_top(i, r):
                chain = cached_chain(i, r, 3)
                dve.wait_ge(c_turned, i * SEQS + (r + 2))
                dve.wait_ge(c_pready, i * SEQS + (r + 1))
                chain.link(nc.vector.tensor_reduce(out=top[:], in_=bank_b[0:1, M_ROW].rearrange("o (g r) -> o r g", g=G),
                                                   axis=AX.X, op=ALU.max))
                nc.vector.tensor_tensor(erow[:], rows(M_ROW), bc(top[:, None, :], [1, G, ROWS]),
                                        ALU.subtract).then_inc(c_diff, 1)

            def cached_weights(i, r):
                chain = cached_chain(i, r, 4)
                dve.wait_ge(c_rexp, i * SEQS + (r + 1))
                dve.wait_ge(c_wcol, i * SEQS + (r + 1))
                chain.link(nc.vector.tensor_tensor(wrow[:], erow[:], rows(S_ROW), ALU.mult))
                chain.link(nc.vector.tensor_reduce(out=total[:], in_=wrow[:].rearrange("o g r -> o r g"), axis=AX.X,
                                                   op=ALU.add))
                chain.link(nc.vector.reciprocal(total[:], total[:]))
                chain.link(nc.vector.tensor_tensor(total[:], total[:], coef[:], ALU.mult))
                nc.vector.tensor_tensor(wrow[:], erow[:], bc(total[:, None, :], [1, G, ROWS]),
                                        ALU.mult).then_inc(c_weighted, 1)

            def cached_column(i, r):
                dve.wait_ge(c_summed, i * SEQS + (r + 2))
                nc.vector.tensor_copy(cw[:], bank_a[:, W_COL]).then_inc(c_wcol, 1)

            def cached_output(i, r):
                dve.wait_ge(c_picked, i * SEQS + (r + 1))
                nc.vector.tensor_copy(o[:, H:2 * H, new_cols(i, r)],
                                      bank_a[:, PICK:PICK + H * NS].rearrange("p (h t) -> p h t", h=H)).then_inc(c_copied, 1)

            with dve.Fori(0, H // 2) as i:
                for s in range(STEPS):
                    r, w = divmod(s, WIN)
                    if w == 0:
                        cached_queries(i, r)
                    if w == 1:
                        cached_sums(i, r)
                    if w == 2:
                        cached_weights(i, r)
                    masked_max(i, s)
                    mix(i, s)
                    (cached_max, cached_top, cached_column, cached_output)[w](i, r)

        @block.scalar
        def _(act):
            act.sem_inc(exped, 2)
            act.sem_inc(aready, 1)
            act.sem_inc(copied, 1)
            for x in (c_exped, c_scaled, c_copied, c_turned, c_wcol):
                act.sem_inc(x, 1)

            def exps(i, s):
                L = (s % NCH + 1) * CH
                if s >= 3:
                    act.wait_ge(turned, i * PASS_BT + (PASS_BT + batch_at(s - 2)))
                else:
                    before = max(x for x in range(STEPS) if x % 3 == s)
                    act.wait_ge(turned, i * PASS_BT + batch_at(before + 1))
                if s:
                    act.wait_ge(mixed, i * STEPS + s)
                for m in range(2):
                    act.wait_ge(maxed, i * (2 * STEPS) + (2 * s + m + 1))
                    nc.scalar.activation((p[s % 3], p2)[m][:, 0:L], ps_s[:, m, 0:L], ACT.Exp, scale=SC,
                                         bias=nm[:, m:m + 1], accum_out=sums[:, m:m + 1]).then_inc(exped, 1)

            def take_turned(i, s, c):
                act.wait_ge(turned, i * PASS_BT + (PASS_BT + batch_at(s) + c + 1))
                if c == 0:
                    act.wait_ge(summed, i * STEPS + (s + 1 + STEPS - 2))
                n = min(BT, s % NCH + 1 - c * BT)
                nc.scalar.activation(aT[s % 2][:, c * BT:c * BT + n, :], ps_t[:, 0:n, :], ACT.Copy).then_inc(aready, 1)

            def take_product(i, s):
                u, qb = divmod(s, NCH)
                act.wait_ge(summed, i * STEPS + (s + 1 + STEPS))
                nc.scalar.activation(o[:, bass.ds(i * 2 + (H + u), 1), qb * CH:(qb + 1) * CH], ps_o[:, None, 0:CH],
                                     ACT.Copy).then_inc(copied, 1)

            def cached_exps(i, r):
                act.wait_ge(c_maxed, i * SEQS + (r + 1))
                nc.scalar.activation(cp[:], bank_a[:], ACT.Exp, scale=SC, bias=cnm[:], accum_out=csums[:, 0:1])
                nc.scalar.activation(cpn[:], bank_b[:, NEW], ACT.Exp, scale=SC, bias=cnm[:],
                                     accum_out=csums[:, 1:2]).then_inc(c_exped, 1)

            def cached_take(i, r):
                act.wait_ge(c_turned, i * SEQS + (r + 2))
                nc.scalar.activation(cpT[:].rearrange("p j r -> p (j r)"), bank_a[:], ACT.Copy)
                nc.scalar.activation(cpnT[:], bank_b[0:NS, NEW_T], ACT.Copy).then_inc(c_pready, 1)
                act.wait_ge(c_diff, i * SEQS + (r + 1))
                nc.scalar.activation(erow[:], erow[:], ACT.Exp, scale=SC).then_inc(c_rexp, 1)

            def cached_scale(i, r):
                act.wait_ge(c_wcol, i * SEQS + (r + 2))
                act.wait_ge(c_summed, i * SEQS + (r + 2))
                nc.scalar.activation(os_[:], bank_b[:], ACT.Copy, scale=cw[:]).then_inc(c_scaled, 1)

            with act.Fori(0, H // 2) as i:
                for u in range(2):
                    act.wait_ge(summed, i * STEPS + (u + 1) * NCH)
                    act.dma_start(v[u][:], val[bass.ds(i + VB_GROUP, 1), 0:SEQ, u * DV:(u + 1) * DV].rearrange(
                        "o (c p) e -> p (o c) e", p=P)).then_inc(v_in[u], 16)
                for s in range(STEPS + 4):
                    if s < STEPS and s % WIN == 3:
                        cached_scale(i, s // WIN)
                    if 2 <= s < STEPS + 2:
                        for c in range(batches(s - 2)):
                            take_turned(i, s - 2, c)
                    if s >= 4:
                        take_product(i, s - 4)
                    if s < STEPS:
                        exps(i, s)
                    if s < STEPS and s % WIN == 0:
                        cached_exps(i, s // WIN)
                    if s < STEPS and s % WIN == 1:
                        cached_take(i, s // WIN)


def stage_heads(nc, g, tag, o, gate, plan):
    NBLK = max(len(b) for b, _, _ in plan)
    with ExitStack() as stack:
        k = Kit(nc, stack, tag)
        gb = [k.sb(f"g{z}", [P, NBLK, T]) for z in range(2)]
        sq = k.sb("sq", [P, NBLK, T])
        ln = k.sb("ln", [P, T])
        rstd = [k.sb(f"rstd{z}", [P, T]) for z in range(2)]
        ss = [k.ps(f"ss{z}", [P, NT, 512]) for z in range(2)]
        gated = [k.sem(f"gated{z}") for z in range(2)]
        squared, summed, logged, rooted, mixed, hid, dv = (
            k.sem(x) for x in ("squared", "summed", "logged", "rooted", "mixed", "hid", "dv"))
        block = stack.enter_context(nc.Block())
        at = {}

        def head(n):
            blocks = plan[n][0]
            return slice(blocks[0], blocks[0] + len(blocks))

        @block.sync
        def _(sp):
            gates = [0, 0]
            for n, (blocks, gate_at, _) in enumerate(plan):
                z, w = n % 2, len(blocks)
                if gate_at is not None:
                    if n >= 2:
                        sp.wait_ge(mixed, n - 1)
                    sp.dma_start(gb[z][:, 0:w, :], gate[:, gate_at:gate_at + w, :]).then_inc(gated[z], 16)
                    gates[z] += 16
                    at[("gate", n)] = gates[z]

        @block.scalar
        def _(act):
            def hi(n):
                act.wait_ge(mixed, n + 1)
                nc.scalar.activation(g.ahi[:, head(n), :], o[:, head(n), :], ACT.Copy).then_inc(hid, 1)

            for n, (blocks, _, _) in enumerate(plan):
                z, w = n % 2, len(blocks)
                if n:
                    act.wait_ge(summed, n)
                nc.scalar.activation(sq[:, 0:w, :], o[:, head(n), :], ACT.Square).then_inc(squared, 1)
                act.wait_ge(summed, n + 1)
                if n:
                    act.wait_ge(rooted, n)
                nc.scalar.activation(by_thirds(ln[:, None, :]), ss[z][:, :, 0:TT], ACT.Ln, scale=1.0 / (w * P),
                                     bias=g.eps[:, 0:1]).then_inc(logged, 1)
                act.wait_ge(logged, n + 1)
                if n >= 2:
                    act.wait_ge(mixed, n - 1)
                nc.scalar.activation(rstd[z][:], ln[:], ACT.Exp, scale=-0.5).then_inc(rooted, 1)
                if n:
                    hi(n - 1)
            hi(len(plan) - 1)

        @block.tensor
        def _(pe):
            for n, (blocks, _, _) in enumerate(plan):
                pe.wait_ge(squared, n + 1)
                if n >= 2:
                    pe.wait_ge(logged, n - 1)
                w = len(blocks)
                for t in range(NT):
                    for b in range(w):
                        last = nc.tensor.matmul(ss[n % 2][:, t, 0:TT], g.ones[:], sq[:, b, t * TT:(t + 1) * TT],
                                                start=(b == 0), stop=(b == w - 1))
                last.then_inc(summed, 1)

        @block.vector
        def _(dve):
            chain = Seq(dve, dv)

            def low(n):
                dve.wait_ge(hid, n + 1)
                nc.vector.tensor_tensor(g.alo[:, head(n), :], o[:, head(n), :], g.ahi[:, head(n), :].bitcast(F32),
                                        ALU.subtract)

            for n, (blocks, gate_at, weights) in enumerate(plan):
                z = n % 2
                dve.wait_ge(rooted, n + 1)
                for i, b in enumerate(blocks):
                    x = o[:, b, :]
                    last = nc.vector.scalar_tensor_tensor(out=x, in0=x, scalar=weights[i] if weights else 1.0,
                                                          in1=rstd[z][:], op0=ALU.mult, op1=ALU.mult)
                if gate_at is None:
                    last.then_inc(mixed, 1)
                else:
                    chain.link(last)
                    dve.wait_ge(gated[z], at[("gate", n)])
                    nc.vector.tensor_tensor(o[:, head(n), :], o[:, head(n), :], gb[z][:, 0:len(blocks), :],
                                            ALU.mult).then_inc(mixed, 1)
                if n:
                    low(n - 1)
            low(len(plan) - 1)


def stage_gate(nc, g, w_a, w_gate, scan_mask, b):
    RANK = 16
    with ExitStack() as stack:
        k = Kit(nc, stack, "gate")
        w = k.sb("w", [P, KB * RANK])
        whi = k.sb("whi", [P, KB * RANK], F32R)
        wlo = k.sb("wlo", [P, KB * RANK], F32R)
        wg = k.sb("wg", [RANK, H * P])
        mask = k.sb("mask", [P, T])
        aT = k.sb("aT", [RANK, T])
        ab, low = k.sb("ab", [P, T]), k.sb("low", [P, T])
        acc = k.ps("acc", [RANK, NT, 512])
        z = k.ps("z", [P, NT, 512])
        landed, split, summed, taken, gated, expd, lowed, used = (
            k.sem(x) for x in ("landed", "split", "summed", "taken", "gated", "expd", "lowed", "used"))
        block = stack.enter_context(nc.Block())

        @block.sync
        def _(sp):
            for dst, src in ((w, w_a), (wg, w_gate), (mask, scan_mask)):
                sp.dma_start(dst[:], src).then_inc(landed, 16)

        @block.tensor
        def _(pe):
            pe.wait_ge(split, 2)
            for n in range(NT):
                last = three_passes(nc, acc[:, n, 0:TT], lambda kk: whi[:, kk * RANK:(kk + 1) * RANK],
                                    lambda kk: wlo[:, kk * RANK:(kk + 1) * RANK],
                                    lambda kk: third(g.ahi, n)[:, kk, :], lambda kk: third(g.alo, n)[:, kk, :], KB)
            last.then_inc(summed, 1)
            pe.wait_ge(taken, 1)
            for h in range(H):
                if h:
                    pe.wait_ge(used, 2 * h)
                for n in range(NT):
                    last = nc.tensor.matmul(z[:, n, 0:TT], wg[:, h * P:(h + 1) * P], aT[:, n * TT:(n + 1) * TT],
                                            start=True, stop=True)
                last.then_inc(gated, 1)

        @block.scalar
        def _(act):
            act.wait_ge(summed, 1)
            nc.scalar.activation(by_thirds(aT[:, None, :]), acc[:, :, 0:TT], ACT.Copy).then_inc(taken, 1)
            for h in range(H):
                act.wait_ge(lowed, 3 * h + 1)
                nc.scalar.activation(by_thirds(ab[:, None, :]), z[:, :, 0:TT], ACT.Abs,
                                     bias=g.vcol("b_gate")[:, h:h + 1]).then_inc(expd, 1)
                act.wait_ge(expd, 3 * h + 1)
                nc.scalar.activation(ab[:], ab[:], ACT.Exp, scale=-1.0).then_inc(expd, 1)
                act.wait_ge(expd, 3 * h + 2)
                nc.scalar.activation(ab[:], ab[:], ACT.Ln, bias=1.0).then_inc(expd, 1)

        @block.vector
        def _(dve):
            dve.wait_ge(landed, 48)
            nc.vector.tensor_copy(whi[:], w[:]).then_inc(split, 1)
            dve.wait_ge(split, 1)
            nc.vector.tensor_tensor(wlo[:], w[:], whi[:].bitcast(F32), ALU.subtract).then_inc(split, 1)
            for h in range(H):
                dve.wait_ge(gated, h + 1)
                if h:
                    dve.wait_ge(lowed, 3 * h)
                nc.vector.tensor_scalar(by_thirds(low[:, None, :]), z[:, :, 0:TT], g.vcol("b_gate")[:, h:h + 1], 0.0,
                                        ALU.add, ALU.min).then_inc(lowed, 1)
                dve.wait_ge(lowed, 3 * h + 1)
                dve.wait_ge(expd, 3 * h + 3)
                nc.vector.tensor_tensor(low[:], low[:], ab[:], ALU.subtract).then_inc(lowed, 1)
                dve.wait_ge(lowed, 3 * h + 2)
                dve.sem_inc(used, 2)
                nc.vector.tensor_tensor_scan(b[:, h, :], mask[:], low[:], 0.0, ALU.mult, ALU.add).then_inc(lowed, 1)


def stage_gla(nc, g, qk, b, levels, v_dram, o, state_out):
    NL = len(LEVELS)
    IT = 1.0 / TAU
    DG = 256
    with ExitStack() as stack:
        k = Kit(nc, stack, "gla")
        lv = k.sb("lv", [P, NL + 1, P], I32)
        v = k.sb("v", [P, H, DG])
        E = [k.sb(f"E{l}", [P, H, CH]) for l in range(NL)]
        X = [k.sb(f"X{l}", [P, H, CH]) for l in range(NL)]
        bs, ek, eq, kd, qe, kc, kdT, attT = (
            k.sb(x, [P, H, CH]) for x in ("bs", "ek", "eq", "kd", "qe", "kc", "kdT", "attT"))
        bcopied = k.sem("bcopied")
        el = k.sb("el", [P, H])
        S = k.sb("S", [P, H, DG])
        gram = [k.ps(f"gram{z}", [P, H, CH]) for z in range(2)]
        ps_t = k.ps("ps_t", [P, H, CH])
        ps_o = k.ps("ps_o", [P, 2 * H, CH])
        ps_d = k.ps("ps_d", [P, H, DG])
        v_in, lv_in, zeroed, out_done = k.sem("v_in"), k.sem("lv_in"), k.sem("zeroed"), k.sem("out_done")
        subbed, exped, multed, grammed, selected, kcopied = (
            k.sem(x) for x in ("subbed", "exped", "multed", "grammed", "selected", "kcopied"))
        turned, kd_taken, summed, deltaed, stated, copied = (
            k.sem(x) for x in ("turned", "kd_taken", "summed", "deltaed", "stated", "copied"))
        block = stack.enter_context(nc.Block())
        NE, NM, NG = NL + 3, NL + 2, NL + 1

        def chunk(t, c):
            return t[:, :, bass.ds(c * CH, CH)]

        def halves(t, s):
            return t.rearrange("p h (n two s) -> p h n two s", two=2, s=s)

        @block.sync
        def _(sp):
            sp.dma_start(lv[:], levels).then_inc(lv_in, 16)
            with sp.Fori(0, NCH) as i:
                sp.wait_ge(deltaed, i + 1)
                sp.dma_start(v[:], v_dram[:, bass.ds(i * CH, CH), :].rearrange("h p e -> p h e")).then_inc(v_in, 16)
            sp.wait_ge(stated, NCH + 1)
            sp.dma_start(state_out, S[:]).then_inc(out_done, 16)
            sp.wait_ge(out_done, 16)

        @block.gpsimd
        def _(pool):
            with pool.Fori(0, NCH) as i:
                bt = bs[:]
                pool.wait_ge(bcopied, i + 1)
                for l, s in enumerate(LEVELS):
                    n = CH // (2 * s)
                    bh, eh = halves(bt, s), halves(E[l][:], s)
                    ref = bc(bh[:, :, :, 0, s - 1:s], [P, H, n, s])
                    pool.wait_ge(multed, i * NM + (l + 1))
                    nc.gpsimd.tensor_tensor(eh[:, :, :, 0, :], ref, bh[:, :, :, 0, :], ALU.subtract)
                    nc.gpsimd.tensor_tensor(eh[:, :, :, 1, :], bh[:, :, :, 1, :], ref, ALU.subtract).then_inc(subbed, 1)
                pool.wait_ge(multed, i * NM + (NL + 1))
                nc.gpsimd.tensor_tensor(ek[:], bc(bt[:, :, CH - 1:CH], [P, H, CH]), bt, ALU.subtract).then_inc(subbed, 1)

        @block.scalar
        def _(act):
            act.sem_inc(kd_taken, 1)
            act.sem_inc(copied, 1)

            def exponentials(i, first=False):
                if not first:
                    act.wait_ge(subbed, i * (NL + 1))
                    act.wait_ge(exped, i * NE)
                nc.scalar.activation(bs[:], chunk(b, i), ACT.Copy).then_inc(bcopied, 1)
                for l in range(NL + 1):
                    e = E[l] if l < NL else ek
                    act.wait_ge(subbed, i * (NL + 1) + (l + 1))
                    nc.scalar.activation(e[:], e[:], ACT.Exp, scale=IT).then_inc(exped, 1)
                act.wait_ge(multed, i * NM + NM)
                nc.scalar.activation(eq[:], bs[:], ACT.Exp, scale=IT).then_inc(exped, 1)

            def decay(i):
                act.wait_ge(stated, i + 1)
                nc.scalar.activation(el[:], bs[:, :, CH - 1], ACT.Exp, scale=IT).then_inc(exped, 1)

            def keys(i):
                act.wait_ge(grammed, i * NG + NG)
                nc.scalar.activation(kc[:], chunk(qk, i)[:, H:2 * H], ACT.Copy).then_inc(kcopied, 1)

            def take(i):
                act.wait_ge(turned, i + 2)
                act.wait_ge(deltaed, i + 1)
                nc.scalar.activation(kdT[:], ps_t[:], ACT.Copy).then_inc(kd_taken, 1)
                act.wait_ge(summed, i + 2)
                nc.scalar.activation(chunk(o, i), ps_o[:], ACT.Copy).then_inc(copied, 1)

            keys(0)
            exponentials(0, True)
            decay(0)
            with act.Fori(0, NCH - 1) as i:
                exponentials(i + 1)
                take(i)
                keys(i + 1)
                decay(i + 1)
            take(NCH - 1)

        @block.tensor
        def _(pe):
            pe.sem_inc(grammed, NG)
            pe.sem_inc(turned, 1)
            pe.sem_inc(summed, 1)
            pe.sem_inc(deltaed, 1)
            with pe.Fori(0, NCH) as i:
                for l in range(NL + 1):
                    pe.wait_ge(selected, i * NG + (l + 1))
                    if l < NL:
                        pe.wait_ge(multed, i * NM + (NM + l + 1))
                    else:
                        pe.wait_ge(kcopied, i + 1)
                    for h in range(H):
                        rhs = X[l][:, h, :] if l < NL else chunk(qk, i)[:, h, :]
                        last = nc.tensor.matmul(gram[l % 2][:, h, :], (X[l] if l < NL else kc)[:, h, :], rhs,
                                                start=True, stop=True)
                    last.then_inc(grammed, 1)
                pe.wait_ge(multed, i * NM + (NM + NL + 1))
                pe.wait_ge(kd_taken, i + 1)
                for h in range(H):
                    last = nc.tensor.transpose(ps_t[:, h, :], kd[:, h, :], g.ident())
                last.then_inc(turned, 1)
                pe.wait_ge(multed, i * NM + 2 * NM)
                pe.wait_ge(selected, i * NG + (NG + 2))
                pe.wait_ge(v_in, i * 16 + 16)
                pe.wait_ge(stated, i + 1)
                pe.wait_ge(copied, i + 1)
                for h in range(H):
                    for e in range(2):
                        nc.tensor.matmul(ps_o[:, 2 * h + e, :], v[:, h, e * P:(e + 1) * P], attT[:, h, :],
                                         start=True, stop=False)
                        last = nc.tensor.matmul(ps_o[:, 2 * h + e, :], S[:, h, e * P:(e + 1) * P], qe[:, h, :],
                                                start=False, stop=True)
                last.then_inc(summed, 1)
                pe.wait_ge(kd_taken, i + 2)
                for h in range(H):
                    last = nc.tensor.matmul(ps_d[:, h, :], kdT[:, h, :], v[:, h, :], start=True, stop=True)
                last.then_inc(deltaed, 1)

        @block.vector
        def _(dve):
            nc.vector.memset(S[:], 0.0)
            nc.vector.memset(attT[:], 0.0).then_inc(zeroed, 1)
            dve.wait_ge(zeroed, 1)
            dve.wait_ge(lv_in, 16)
            dve.sem_inc(stated, 1)
            dve.sem_inc(selected, 2)
            dve.sem_inc(multed, NM)

            def scale_level(i, l):
                s = LEVELS[l]
                dve.wait_ge(exped, i * NE + (l + 1))
                dve.wait_ge(grammed, i * NG + (l + 1))
                xh, eh, th = halves(X[l][:], s), halves(E[l][:], s), halves(chunk(qk, i), s)
                nc.vector.tensor_tensor(xh[:, :, :, 0, :], th[:, H:2 * H, :, 0, :], eh[:, :, :, 0, :], ALU.mult)
                nc.vector.tensor_tensor(xh[:, :, :, 1, :], th[:, 0:H, :, 1, :], eh[:, :, :, 1, :],
                                        ALU.mult).then_inc(multed, 1)

            def scale_kd(i):
                dve.wait_ge(exped, i * NE + (NL + 1))
                dve.wait_ge(turned, i + 1)
                nc.vector.tensor_tensor(kd[:], chunk(qk, i)[:, H:2 * H], ek[:], ALU.mult).then_inc(multed, 1)

            def scale_qe(i):
                dve.wait_ge(exped, i * NE + (NL + 2))
                dve.wait_ge(summed, i + 1)
                nc.vector.tensor_tensor(qe[:], chunk(qk, i)[:, 0:H], eq[:], ALU.mult).then_inc(multed, 1)

            def before_select(i, l):
                dve.wait_ge(grammed, i * NG + (NG + l + 1))
                dve.wait_ge(selected, i * NG + (l + 2))
                if l == 0:
                    dve.wait_ge(summed, i + 1)

            def select(i, l):
                nc.vector.copy_predicated(attT[:], bc(lv[:, l, None, :], [P, H, CH]), gram[l % 2][:]).then_inc(selected, 1)

            def state(i):
                dve.wait_ge(deltaed, i + 2)
                dve.wait_ge(exped, i * NE + NE)
                for h in range(H):
                    last = nc.vector.scalar_tensor_tensor(out=S[:, h, :], in0=S[:, h, :], scalar=el[:, h:h + 1],
                                                          in1=ps_d[:, h, :], op0=ALU.mult, op1=ALU.add)
                last.then_inc(stated, 1)

            for l in range(NL):
                scale_level(0, l)
            scale_kd(0)
            scale_qe(0)
            with dve.Fori(0, NCH - 1) as i:
                for l in range(NL):
                    before_select(i, l)
                    scale_level(i + 1, l)
                    select(i, l)
                before_select(i, NL)
                scale_kd(i + 1)
                select(i, NL)
                state(i)
                scale_qe(i + 1)
            for l in range(NL + 1):
                before_select(NCH - 1, l)
                select(NCH - 1, l)
            state(NCH - 1)


def stage_gla_samples(nc, g, qk, b, levels, v_dram, o, state_in, state_out):
    IT = 1.0 / TAU
    DG = 256
    LV = [l for l, s in enumerate(LEVELS) if 2 * s <= NS]
    with ExitStack() as stack:
        k = Kit(nc, stack, "glas")
        lv = k.sb("lv", [P, len(LEVELS) + 1, P], I32)
        v = k.sb("v", [TS, H, DG])
        vm = [k.sb(f"vm{z}", [TS, NB, DG]) for z in range(2)]
        ss = k.sb("ss", [P, NB, H, DG])
        E = [k.sb(f"E{l}", [P, H, TS]) for l in range(len(LV))]
        X = [k.sb(f"X{l}", [P, H, TS]) for l in range(len(LV))]
        ek, eq, kd, qe = (k.sb(x, [P, H, TS]) for x in ("ek", "eq", "kd", "qe"))
        kdT = k.sb("kdT", [TS, H, P])
        attT = k.sb("attT", [TS, H, TS])
        el = k.sb("el", [P, H, NB])
        ps_g = k.ps("ps_g", [TS, len(LV) + 1, H, TS])
        ps_t = k.ps("ps_t", [TS, H, P])
        ps_o = k.ps("ps_o", [P, 2 * H, TS])
        ps_d = k.ps("ps_d", [P, NB, DG])
        landed, dv, exped, grammed, turned, taken, summed, deltaed, done, decayed, out_done = (
            k.sem(x) for x in ("landed", "dv", "exped", "grammed", "turned", "taken", "summed", "deltaed", "done",
                               "decayed", "out_done"))
        block = stack.enter_context(nc.Block())
        at = {}

        def halves(t, s):
            return t.rearrange("p h (n two s) -> p h n two s", two=2, s=s)

        def seqs(t):
            return t.rearrange("p h (b t) -> p h b t", t=NS)

        bt, qt, kt = b[:, :, SEQ:T], qk[:, 0:H, SEQ:T], qk[:, H:2 * H, SEQ:T]

        @block.sync
        def _(sp):
            sp.dma_start(lv[:], levels).then_inc(landed, 16)
            sp.dma_start(v[:], v_dram[:, SEQ:T, :].rearrange("h p e -> p h e")).then_inc(landed, 16)
            sp.dma_start(ss[:], state_in).then_inc(landed, 16)
            sp.wait_ge(done, H)
            sp.dma_start(state_out, ss[:]).then_inc(out_done, 16)
            sp.wait_ge(out_done, 16)

        def state(dve, h):
            dve.wait_ge(summed, 1)
            nc.vector.tensor_tensor(ss[:, :, h, :], ss[:, :, h, :], bc(el[:, h, :, None], [P, NB, DG]),
                                    ALU.mult).then_inc(decayed, 1)
            dve.wait_ge(decayed, h + 1)
            dve.wait_ge(deltaed, h + 1)
            nc.vector.tensor_tensor(ss[:, :, h, :], ss[:, :, h, :], ps_d[:], ALU.add).then_inc(done, 1)

        @block.vector
        def _(dve):
            chain = Seq(dve, dv)
            for l, i in enumerate(LV):
                s = LEVELS[i]
                bh, eh = halves(bt, s), halves(E[l][:], s)
                ref = bc(bh[:, :, :, 0, s - 1:s], [P, H, TS // (2 * s), s])
                nc.vector.tensor_tensor(eh[:, :, :, 0, :], ref, bh[:, :, :, 0, :], ALU.subtract)
                nc.vector.tensor_tensor(eh[:, :, :, 1, :], bh[:, :, :, 1, :], ref, ALU.subtract)
            nc.vector.memset(attT[:], 0.0)
            for h in range(H):
                bh = bt[:, h, :].rearrange("p (b t) -> p b t", t=NS)
                last = nc.vector.tensor_tensor(ek[:, h, :].rearrange("p (b t) -> p b t", t=NS),
                                               bc(bh[:, :, NS - 1:NS], [P, NB, NS]), bh, ALU.subtract)
            chain.link(last)
            at["sub"] = chain.n
            dve.wait_ge(exped, 1)
            for l, i in enumerate(LV):
                s = LEVELS[i]
                xh, eh = halves(X[l][:], s), halves(E[l][:], s)
                nc.vector.tensor_tensor(xh[:, :, :, 0, :], halves(kt, s)[:, :, :, 0, :], eh[:, :, :, 0, :], ALU.mult)
                nc.vector.tensor_tensor(xh[:, :, :, 1, :], halves(qt, s)[:, :, :, 1, :], eh[:, :, :, 1, :], ALU.mult)
            nc.vector.tensor_tensor(kd[:], kt, ek[:], ALU.mult)
            chain.link(nc.vector.tensor_tensor(qe[:], qt, eq[:], ALU.mult))
            at["mult"] = chain.n
            dve.wait_ge(landed, 48)
            dve.wait_ge(grammed, 1)
            for l in range(len(LV) + 1):
                i = LV[l] if l < len(LV) else len(LEVELS)
                chain.link(nc.vector.copy_predicated(attT[:], bc(lv[0:TS, i, None, 0:TS], [TS, H, TS]), ps_g[:, l]))
            at["select"] = chain.n
            for h in range(H):
                if h >= 2:
                    dve.wait_ge(deltaed, h - 1)
                chain.link(nc.vector.tensor_tensor(vm[h % 2][:], bc(v[:, h, None, :], [TS, NB, DG]),
                                                   bc(g.col("bmask")[0:TS, :, None], [TS, NB, DG]), ALU.mult))
                at[("vm", h)] = chain.n
                if h:
                    state(dve, h - 1)
            state(dve, H - 1)

        @block.scalar
        def _(act):
            act.wait_ge(dv, at["sub"])
            for e in [*E, ek]:
                nc.scalar.activation(e[:], e[:], ACT.Exp, scale=IT)
            nc.scalar.activation(el[:], seqs(bt)[:, :, :, NS - 1], ACT.Exp, scale=IT)
            nc.scalar.activation(eq[:], bt, ACT.Exp, scale=IT).then_inc(exped, 1)
            act.wait_ge(turned, 1)
            nc.scalar.activation(kdT[:], ps_t[:], ACT.Copy).then_inc(taken, 1)
            act.wait_ge(summed, 1)
            nc.scalar.activation(o[:, :, SEQ:T], ps_o[:], ACT.Copy)

        @block.tensor
        def _(pe):
            pe.wait_ge(dv, at["mult"])
            for l in range(len(LV) + 1):
                for h in range(H):
                    a, c = (X[l][:, h, :], X[l][:, h, :]) if l < len(LV) else (kt[:, h, :], qt[:, h, :])
                    last = nc.tensor.matmul(ps_g[:, l, h, :], a, c, start=True, stop=True)
            last.then_inc(grammed, 1)
            for h in range(H):
                last = nc.tensor.transpose(ps_t[:, h, :], kd[:, h, :], g.ident())
            last.then_inc(turned, 1)
            pe.wait_ge(dv, at["select"])
            for h in range(H):
                for e in range(2):
                    nc.tensor.matmul(ps_o[:, 2 * h + e, :], v[:, h, e * P:(e + 1) * P], attT[:, h, :],
                                     start=True, stop=False)
                    for i in range(NB):
                        last = nc.tensor.matmul(ps_o[:, 2 * h + e, i * NS:(i + 1) * NS], ss[:, i, h, e * P:(e + 1) * P],
                                                qe[:, h, i * NS:(i + 1) * NS], start=False, stop=(i == NB - 1))
            last.then_inc(summed, 1)
            pe.wait_ge(taken, 1)
            for h in range(H):
                pe.wait_ge(dv, at[("vm", h)])
                if h:
                    pe.wait_ge(done, h)
                for n in range(NB // 2):
                    last = nc.tensor.matmul(ps_d[:, 2 * n:2 * n + 2, :], kdT[:, h, :], vm[h % 2][:, 2 * n:2 * n + 2, :],
                                            start=True, stop=True)
                last.then_inc(deltaed, 1)


def decoder_step(nc, a, outs):
    def scratch(name, shape):
        return nc.dram_tensor(name, shape, F32, kind="Internal").ap()

    Kit.taken = []
    x_0, x_1, x_2 = (scratch(f"x_{i}", [P, KB, T]) for i in range(3))
    v_gla = scratch("v_gla", [4, T, GW])
    gates = scratch("gates", [P, KB, T])
    with ExitStack() as life:
        g = State(nc, life)
        g.lam_in = [a[n] for n in ("lam_q1", "lam_k1", "lam_q2", "lam_k2")]

        def sb(stack, name, shape, dt=F32):
            return stack.enter_context(nc.sbuf_tensor(name, shape, dt))

        def operand(stack, tag):
            g.ahi, g.alo = (stack.enter_context(nc.sbuf_tensor(f"{tag}_{x}", [P, KB, T], F32R, side="right"))
                            for x in ("hi", "lo"))

        def copy_to(dst, scale=1.0):
            return lambda u, s: nc.scalar.activation(by_thirds(dst[:, bass.ds(u, 1), :]), s, ACT.Copy, scale=scale)

        def silu_to(dst):
            return lambda u, s: nc.scalar.activation(by_thirds(dst[:, bass.ds(u, 1), :]), s, ACT.Silu)

        stage_load(nc, g, a["consts"], a["vecs"])
        stage_ada(nc, g, a["w_ada"], a["cT"])
        y_flat = sb(life, "y", [P, KB * T])
        y = y_flat[:].rearrange("p (k t) -> p k t", k=KB)

        with ExitStack() as first:
            with ExitStack() as projections:
                operand(projections, "h0")
                stage_norm(nc, g, "n0", y_flat[:], None, None, (0, 0), a["x"], None)
                stage_linear(nc, g, "ga", a["w_ga"], [(H, silu_to(y))])
                stage_store(nc, "gate_ab", [(gates[:, 0:H, :], y[:, 0:H, :])])
                qkT = sb(first, "qkT", [P, 12, T])
                stage_project(nc, g, "qk", y_flat[:], a["w_qk"], 6, True, qkT, outs["rotated"])
                stage_project(nc, g, "v", y_flat[:], a["w_v"], 4, False, None, outs["values"])
            stage_retention(nc, g, qkT, outs["rotated"], outs["values"], y, a["state_ret"],
                            outs["ret_prompt"], outs["ret_sample"])
            stage_attention(nc, g, qkT, a["cache_k"], a["cache_v"], a["pages"], outs["values"], y)
        recycle_semaphores(nc)
        h = life.enter_context(ExitStack())
        operand(h, "h")
        stage_heads(nc, g, "hd0", y, gates,
                    [([h], h, None) for h in range(H)] + [([H + h], None, [g.vcol("g_diff")]) for h in range(H)])
        stage_linear(nc, g, "oab", a["w_out_ab"], [(KB, copy_to(y))])
        stage_norm(nc, g, "n1", None, y, (0, 2), (0, 3), a["x"], x_0)
        stage_ffn(nc, g, "f0", 0, a["w_ffn0"], y, a["conv_in0"], outs["conv0"])
        stage_norm(nc, g, "n2", None, y, (0, 5), (1, 0), x_0, x_1)

        recycle_semaphores(nc)
        stage_project(nc, g, "vc", y_flat[:], a["w_vc"], 4, False, None, v_gla)
        stage_linear(nc, g, "r", a["w_qkr"][2 * H:4 * H], [(2 * H, silu_to(y))])
        stage_store(nc, "gate_c", [(gates, y)])
        with ExitStack() as second:
            qk = sb(second, "qk", [P, 2 * H, T])
            b = sb(second, "b", [P, H, T])
            stage_linear(nc, g, "qkc", a["w_qkr"][0:2 * H],
                         [(H, copy_to(qk, DV ** -0.5)), (H, copy_to(qk[:, H:2 * H, :]))])
            stage_gate(nc, g, a["w_a"], a["w_gate"], a["scan"], b)
            h.close()
            stage_gla(nc, g, qk, b, a["levels"], v_gla, y, outs["gla_prompt"])
            stage_gla_samples(nc, g, qk, b, a["levels"], v_gla, y, a["state_gla"], outs["gla_sample"])
        operand(life, "m")
        g_gla = g.vcol("g_gla")
        stage_heads(nc, g, "hd1", y, gates,
                    [([2 * h, 2 * h + 1], 2 * h, [g_gla[:, 0:1], g_gla[:, 1:2]]) for h in range(H)])
        stage_linear(nc, g, "oc", a["w_out_c"], [(KB, copy_to(y))])
        stage_norm(nc, g, "n3", None, y, (1, 2), (1, 3), x_1, x_2)
        stage_ffn(nc, g, "f1", 1, a["w_ffn1"], y, a["conv_in1"], outs["conv1"])
        stage_norm(nc, g, "n4", None, y, (1, 5), None, x_2, outs["x_out"])


def _constants():
    c = np.zeros((P, NCONST), np.float32)

    def put(name, a):
        a = np.asarray(a, np.float64).astype(np.float32)
        c[:a.shape[0], CONST[name][0]:CONST[name][1]] = a.reshape(a.shape[0], -1)

    i = np.arange(P)
    put("ident", np.eye(P))
    put("causal", np.where(i[None, :] <= i[:, None], 0.0, NEG))
    gamma = 1.0 - np.exp2(-5.0 - np.arange(H))
    scale = 64 ** -0.5
    rel = i[None, :] - i[:, None]
    put("decay", np.stack([np.where(rel >= 0, gm ** np.maximum(rel, 0), 0) for gm in gamma], 1) * scale)
    put("decq", np.broadcast_to(np.stack([gm ** (i + 1) for gm in gamma]), (P, H, P)))
    put("deck", np.stack([gm ** (P - 1 - i) for gm in gamma], 1) * scale)
    half = (i // 64)[:, None]
    pair = 2 * np.arange(2)[None, :] + half
    put("decc", gamma[pair] ** P)
    inv = (10000.0 ** (-np.arange(0, 64, 2) / 64)).astype(np.float32)
    pos = np.concatenate([np.arange(SEQ), PAST + np.tile(np.arange(NS), NB)]).astype(np.float32)
    ang = (pos[:, None] * inv[None, :]).astype(np.float32).astype(np.float64)
    ang = np.concatenate([ang, np.zeros((TILES * P - T, 32))]).reshape(TILES, P, 32).transpose(1, 0, 2)
    put("cos", np.cos(ang))
    put("sin", np.stack([-np.sin(ang), np.sin(ang)], 2))
    s = np.arange(TS)
    same = (s[:, None] // NS == s[None, :] // NS)
    srel = s[None, :] - s[:, None]
    put("sdecay", np.stack([np.where(same & (srel >= 0), gm ** np.maximum(srel, 0), 0) for gm in gamma], 1) * scale)
    put("sdecq", np.broadcast_to(np.stack([gm ** (s % NS + 1) for gm in gamma]), (P, H, TS)))
    put("sdeck", np.stack([gm ** (NS - 1 - s % NS) for gm in gamma], 1) * scale)
    put("sdecc", gamma[pair] ** NS)
    row = np.arange(P)
    allowed = (row[:, None] >= P - TS) & (np.arange(NS)[None, :] <= row[:, None] % NS)
    put("smask", np.where(allowed, 0.0, NEG))
    put("sel", np.stack([(row[:, None] % TS // 8 == h) & (row[:, None] % NS == np.arange(NS)[None, :])
                         for h in range(H)], 1))
    put("bmask", s[:, None] // NS == np.arange(NB)[None, :])
    put("maps", np.stack([s % 8 < NS, s % 8 >= NS])[None])
    t = np.arange(T)
    first = np.where(t < SEQ, t % CH == 0, (t - SEQ) % NS == 0)
    return c, np.broadcast_to(np.where(first, 0.0, 1.0), (P, T)).astype(np.float32)


def _level_masks():
    i = np.arange(P)
    m = [((i[:, None] // (2 * s) == i[None, :] // (2 * s)) & (i[:, None] % (2 * s) < s) & (i[None, :] % (2 * s) >= s))
         for s in LEVELS]
    m.append(i[:, None] == i[None, :])
    return np.stack(m, 1).astype(np.int32)


def _units(w, width=P):
    n = w.shape[1] // width
    return np.ascontiguousarray(w.reshape(KB, P, n, width).transpose(2, 1, 0, 3).reshape(n, P, KB * width))


def _columns(v):
    return np.ascontiguousarray(v.reshape(-1, P).T)


def _hidden_order(v):
    v = v.reshape(v.shape[:-1] + (2, FB, P))
    return np.moveaxis(v, -3, -2).reshape(v.shape[:-3] + (2 * FB, P))


def _ffn_units(w_up, w_down):
    up = _units(w_up).reshape(2, FB, P, UW)
    down = w_down.reshape(FB, P, D)
    out = [up[0, 0], up[1, 0], up[0, 1], up[1, 1]]
    for p in range(1, FB // 2):
        out += [up[0, 2 * p], up[1, 2 * p], down[2 * p - 2], down[2 * p - 1], up[0, 2 * p + 1], up[1, 2 * p + 1]]
    out += [down[FB - 2], down[FB - 1]]
    return np.stack(out)


def _feature_major(prompt, sample):
    a = np.concatenate([prompt, sample.reshape(TS, -1)])
    return np.ascontiguousarray(a.reshape(T, -1, P).transpose(2, 1, 0))


def lay_out(i):
    a = {}
    a["consts"], a["scan"] = _constants()
    a["levels"] = _level_masks()
    v = [_columns(i["b_ada"])] + [_columns(i[n]) for n in ("g_pre_mix", "g_post_mix", "g_pre_ffn", "g_post_ffn")]
    v += [_columns(i["g_diff"]), _columns(i["g_gla"]), _columns(i["b_gate_c"])]
    v += [_hidden_order(i["conv_b"]).reshape(-1, P).T]
    cw = _hidden_order(i["conv_w"])
    v += [cw.transpose(3, 0, 2, 1).reshape(P, -1)]
    a["vecs"] = np.ascontiguousarray(np.concatenate(v, 1))
    for n in ("lam_q1", "lam_k1", "lam_q2", "lam_k2"):
        a[n] = i[n].reshape(1, 64)
    a["x"] = _feature_major(i["x_prompt"][0], i["x_sample"])
    a["cT"] = np.ascontiguousarray(np.concatenate([i["c_prompt"], i["c_sample"]]).reshape(C9, KB, P).transpose(2, 1, 0))
    a["w_ada"] = np.concatenate([_units(i["w_ada"][l], 512) for l in range(2)]).reshape(24, P, KB, 512)
    w = i["w_in_ab"][0]
    qa, ka, va, ga, qb, kb, vb = np.split(w, [256, 512, 1024, 1536, 2048, 2560], axis=1)
    a["w_qk"] = _units(np.concatenate([qa, qb, ka, kb], 1), GW)
    a["w_v"] = _units(np.concatenate([va, vb], 1), GW)
    a["w_ga"] = _units(ga)
    a["w_out_ab"] = _units(i["w_out_ab"][0])
    w = i["w_in_c"][0]
    q, k, vv, r, ga_ = np.split(w, [512, 1024, 2048, 3072], axis=1)
    a["w_qkr"] = _units(np.concatenate([q, k, r], 1))
    a["w_vc"] = _units(vv, GW)
    a["w_a"] = _units(ga_, 16)[0]
    a["w_gate"] = i["w_gate_c"][0]
    a["w_out_c"] = _units(i["w_out_c"][0])
    for l in range(2):
        a[f"w_ffn{l}"] = _ffn_units(i["w_up"][l], i["w_down"][l])
        sc = _hidden_order(i["state_conv"][l])
        a[f"conv_in{l}"] = np.ascontiguousarray(sc.transpose(3, 2, 0, 1))
    a["cache_k"] = np.ascontiguousarray(i["cache_k"][0].transpose(0, 3, 2, 1))
    a["cache_v"] = i["cache_v"][0].reshape(-1, PAGE, H * DV)
    a["pages"] = np.ascontiguousarray(i["page_table"].astype(np.int32))
    a["state_ret"] = np.ascontiguousarray(i["state_ret"][0].reshape(NB, 2, P, DV).transpose(2, 0, 1, 3))
    a["state_gla"] = np.ascontiguousarray(i["state_gla"][0].transpose(2, 0, 1, 3))
    return a


OUTPUTS = {"rotated": [6, T, GW], "values": [4, T, GW], "ret_prompt": [P, 2, DV], "ret_sample": [P, NB, 2, DV],
           "x_out": [P, KB, T], "gla_prompt": [P, H, 256], "gla_sample": [P, NB, H, 256],
           "conv0": [P, 2 * FB, 2 * C9], "conv1": [P, 2 * FB, 2 * C9]}


def kernel(**inputs):
    import concourse.bacc as _bacc
    from concourse.bass_utils import run_bass_kernel_spmd

    arrays = lay_out({n: np.asarray(v) for n, v in inputs.items()})
    nc = _bacc.Bacc("TRN2", target_bir_lowering=False, num_devices=1)
    a = {n: nc.dram_tensor(n, list(v.shape), mybir.dt.from_np(v.dtype), kind="ExternalInput").ap()
         for n, v in arrays.items()}
    outs = {n: nc.dram_tensor(n, s, F32, kind="ExternalOutput").ap() for n, s in OUTPUTS.items()}
    decoder_step(nc, a, outs)
    nc.finalize()
    r = run_bass_kernel_spmd(nc, [arrays], core_ids=[0]).results[0]
    r = {n: np.asarray(r[n]).reshape(s) for n, s in OUTPUTS.items()}

    x = r["x_out"].transpose(2, 1, 0).reshape(T, D)
    kb = r["rotated"][4:6].transpose(1, 0, 2).reshape(T, H, DV)
    vb = r["values"][VB_GROUP:].transpose(1, 0, 2).reshape(T, H, DV)
    conv = np.stack([r[n].reshape(P, FB, 2, 2 * C9).transpose(3, 2, 1, 0).reshape(C9, 2, 2 * FB * P)
                     for n in ("conv0", "conv1")])
    out = (x[None, :SEQ], x[SEQ:].reshape(NB, NS, D),
           kb[None, None, :SEQ], vb[None, None, :SEQ],
           kb[SEQ:].reshape(1, NB, NS, H, DV), vb[SEQ:].reshape(1, NB, NS, H, DV),
           r["ret_prompt"].reshape(2, 64, 2, DV).transpose(2, 0, 1, 3).reshape(1, 1, H, 64, DV),
           r["ret_sample"].reshape(2, 64, NB, 2, DV).transpose(2, 3, 0, 1, 4).reshape(1, NB, H, 64, DV),
           r["gla_prompt"].transpose(1, 0, 2)[None, None], r["gla_sample"].transpose(1, 2, 0, 3)[None],
           conv[:, 0:1], conv[:, 1:])
    return tuple(np.ascontiguousarray(o) for o in out)
```

```python
from contextlib import ExitStack

import numpy as np
import concourse.bass as bass
from concourse import mybir

F32 = mybir.dt.float32
F32R = mybir.dt.float32r
I32 = mybir.dt.int32
ALU = mybir.AluOpType
ACT = mybir.ActivationFunctionType
AX = mybir.AxisListType
LN_EXP = "natural_log_exp_and_others"

P = 128
D = 1024
KB = D // P
SEQ = 1024
NB = 8
NS = 4
TS = NB * NS
T = SEQ + TS
NT = 3
TT = T // NT
PT = SEQ - 2 * TT
CH = 128
NCH = SEQ // CH
TILES = NCH + 1
H = 4
DV = 128
PAST = 2048
PAGE = 128
NPG = PAST // PAGE
FB = 22
UW = KB * P
GW = 256
EPS = 1e-6
TAU = 16.0
LAM_INIT = 0.2
NEG = -1e30
C9 = 1 + NB
NMOD = 6 * KB
LEVELS = [64, 32, 16, 8, 4, 2, 1]

def const_columns():
    at, n = {}, 0
    for name, w in (("ident", P), ("causal", P), ("decay", H * P), ("decq", H * P), ("deck", H),
                    ("decc", 2), ("cos", TILES * 32), ("sin", TILES * 64), ("sdecay", H * TS),
                    ("sdecq", H * TS), ("sdeck", H), ("sdecc", 2), ("smask", NS), ("sel", H * NS),
                    ("bmask", NB), ("maps", 2 * TS)):
        at[name] = (n, n + w)
        n += w
    return at, n


CONST, NCONST = const_columns()
VEC = {}
NVEC = 0
for _n, _w in (("b_ada", 2 * NMOD), ("g_pre_mix", 2 * KB), ("g_post_mix", 2 * KB), ("g_pre_ffn", 2 * KB),
               ("g_post_ffn", 2 * KB), ("g_diff", 1), ("g_gla", 2), ("b_gate", 4), ("conv_b", 4 * FB),
               ("conv_w", 12 * FB)):
    VEC[_n] = (NVEC, NVEC + _w)
    NVEC += _w


class Kit:

    def __init__(self, nc, stack, tag, spare=None):
        self.nc, self.stack, self.tag, self.spare, self.used = nc, stack, tag, spare, 0

    def sb(self, name, shape, dt=F32):
        n = int(np.prod(shape[1:]))
        if self.spare is not None and dt != F32R and self.used + n <= self.spare.shape[1]:
            view = self.spare[0:shape[0], self.used:self.used + n]
            self.used += n
            if dt != F32:
                view = view.bitcast(dt)
            names = "abcd"[:len(shape) - 1]
            return view.rearrange(f"p ({' '.join(names)}) -> p {' '.join(names)}",
                                  **dict(zip(names[1:], shape[2:]))) if len(shape) > 2 else view
        return self.stack.enter_context(self.nc.sbuf_tensor(f"{self.tag}_{name}", shape, dt))

    def ps(self, name, shape, dt=F32):
        return self.stack.enter_context(self.nc.psum_tensor(f"{self.tag}_{name}", shape, dt))

    taken = []

    def sem(self, name):
        Kit.taken.append(self.nc.alloc_semaphore(f"{self.tag}_{name}"))
        return Kit.taken[-1]


def recycle_semaphores(nc):
    nc.clear_and_free_semaphores(Kit.taken)
    Kit.taken = []
    with nc.Block():
        pass


class Seq:

    def __init__(self, eng, sem):
        self.eng, self.sem, self.n, self.base = eng, sem, 0, 0

    def link(self, ins):
        ins.then_inc(self.sem, 1)
        self.n += 1
        self.eng.wait_ge(self.sem, self.base + self.n)
        return ins


def cols(t, name, table=CONST):
    a, b = table[name]
    return t[:, a:b]


def third(ap, n):
    return ap[:, :, n * TT:(n + 1) * TT]


def bc(ap, shape):
    return ap.to_broadcast(shape)


def stage_load(nc, g, consts, vecs):
    with ExitStack() as stack:
        k = Kit(nc, stack, "load")
        landed = k.sem("landed")
        lam_rows = k.sb("lam_rows", [P, 4, 64])
        prod = k.sb("prod", [P, 2, 64])
        dots = k.sb("dots", [P, 2])
        exps = k.sb("exps", [P, 2])
        ch, ex = k.sem("dve"), k.sem("exp")
        block = stack.enter_context(nc.Block())

        @block.sync
        def _(sp):
            sp.dma_start(g.const[:], consts).then_inc(landed, 16)
            sp.dma_start(g.vec[:], vecs).then_inc(landed, 16)
            for i, v in enumerate(g.lam_in):
                sp.dma_start(lam_rows[:, i, :], v.to_broadcast([P, 64])).then_inc(landed, 16)

        @block.vector
        def _(dve):
            nc.vector.memset(g.ones[:], 1.0)
            nc.vector.memset(g.eps[:], EPS)
            dve.wait_ge(landed, 96)
            chain = Seq(dve, ch)
            for i in range(2):
                chain.link(nc.vector.tensor_tensor(prod[:, i, :], lam_rows[:, 2 * i, :], lam_rows[:, 2 * i + 1, :],
                                                   ALU.mult))
            chain.link(nc.vector.tensor_reduce(out=dots[:], in_=prod[:], axis=AX.X, op=ALU.add))
            gd = g.vcol("g_diff")
            chain.link(nc.vector.tensor_scalar(gd, gd, 1.0 - LAM_INIT, None, ALU.mult))
            dve.wait_ge(ex, 1)
            chain.link(nc.vector.tensor_tensor(g.lam[:, 0:1], exps[:, 0:1], exps[:, 1:2], ALU.subtract))
            chain.link(nc.vector.tensor_scalar(g.lam[:, 1:2], g.lam[:, 0:1], LAM_INIT, -1.0, ALU.add, ALU.mult))

        @block.scalar
        def _(act):
            act.wait_ge(ch, 3)
            nc.scalar.activation(exps[:], dots[:], ACT.Exp).then_inc(ex, 1)


UA = 256
BA = UA // P
NUA = 2 * NMOD // BA


class Modulation:

    def __init__(self, nc, g, k, w_ada, first):
        self.nc, self.g, self.w_ada, self.first = nc, g, w_ada, first
        self.w = [k.sb(f"ada_w{i}", [P, KB, UA]) for i in range(2)]
        self.rows = k.sb("ada_rows", [P, UA])
        self.acc = k.ps("ada_acc", [P, UA])
        self.turned_rows = k.ps("ada_turned", [P, BA, P])
        self.landed = [k.sem(f"ada_landed{i}") for i in range(2)]
        self.multiplied, self.taken, self.turned, self.added = (
            k.sem(f"ada_{x}") for x in ("multiplied", "taken", "turned", "added"))

    def start_tensor(self, pe):
        pe.sem_inc(self.turned, 1)

    def start_scalar(self, act):
        act.sem_inc(self.taken, 1)

    def start_vector(self, dve):
        dve.sem_inc(self.added, 1)

    def load(self, queue, n, parity):
        queue.dma_start(self.w[parity][:, None], self.w_ada[bass.ds(n + self.first, 1)].rearrange(
            "o p k c -> p o k c")).then_inc(self.landed[parity], 16)

    def multiply(self, pe, n, parity, landed_at):
        pe.wait_ge(self.landed[parity], landed_at)
        pe.wait_ge(self.taken, n + 1)
        for r in range(KB // 4):
            for t in range(4):
                last = self.nc.tensor.matmul(self.acc[32 * t:32 * t + 32, :], self.g.silu_c[:, 4 * r + t, :],
                                             self.w[parity][:, 4 * r + t, :], start=(r == 0), stop=(r == KB // 4 - 1))
        last.then_inc(self.multiplied, 1)

    def take(self, act, n):
        act.wait_ge(self.multiplied, n + 1)
        act.wait_ge(self.turned, n + 1)
        self.nc.scalar.activation(self.rows[:], self.acc[:], ACT.Copy).then_inc(self.taken, 1)

    def turn(self, pe, n):
        pe.wait_ge(self.taken, n + 2)
        pe.wait_ge(self.added, n + 1)
        for j in range(BA):
            last = self.nc.tensor.transpose(self.turned_rows[:, j, :], self.rows[:, j * P:(j + 1) * P], self.g.ident())
        last.then_inc(self.turned, 1)

    def add(self, dve, n):
        dve.wait_ge(self.turned, n + 2)
        parts = self.turned_rows[:].rearrange("p j (t c) -> p j c t", t=4)[:, :, 0:C9, :]
        out = self.g.mod[:].rearrange("p l b c -> p (l b) c")[:, bass.ds((n + self.first) * BA, BA), :]
        self.nc.vector.tensor_reduce(out=out, in_=parts, axis=AX.X, op=ALU.add).then_inc(self.added, 1)

    def finish(self, chain, l, parts):
        nc, g = self.nc, self.g

        def per_feature(name, at, n):
            a = VEC[name][0] + at
            return bc(g.vec[:, a:a + n].rearrange("p (b c) -> p b c", c=1), [P, n, C9])

        for part in parts:
            m = g.mod[:, l, part * KB:(part + 1) * KB, :]
            chain.link(nc.vector.tensor_tensor(m, m, per_feature("b_ada", l * NMOD + part * KB, KB), ALU.add))
            if part in (1, 4):
                chain.link(nc.vector.tensor_scalar(m, m, 1.0, None, ALU.add))
            name = {1: "g_pre_mix", 2: "g_post_mix", 4: "g_pre_ffn", 5: "g_post_ffn"}.get(part)
            if name:
                chain.link(nc.vector.tensor_tensor(m, m, per_feature(name, l * KB, KB), ALU.mult))


def stage_modulation(nc, g, w_ada, cT_dram, n_units):
    with ExitStack() as stack:
        k = Kit(nc, stack, "ada")
        cT = k.sb("cT", [P, KB, C9])
        c_in, zeroed, silu, dv = k.sem("c_in"), k.sem("zeroed"), k.sem("silu"), k.sem("dv")
        ada = Modulation(nc, g, k, w_ada, 0)
        block = stack.enter_context(nc.Block())

        @block.sync
        def _(sp):
            sp.dma_start(cT[:], cT_dram).then_inc(c_in, 16)
            for n in range(n_units):
                if n >= 2:
                    sp.wait_ge(ada.multiplied, n - 1)
                ada.load(sp, n, n % 2)

        @block.scalar
        def _(act):
            ada.start_scalar(act)
            act.wait_ge(c_in, 16)
            act.wait_ge(zeroed, 1)
            nc.scalar.activation(g.silu_c[:, :, 0:C9], cT[:], ACT.Silu).then_inc(silu, 1)
            for n in range(n_units):
                ada.take(act, n)

        @block.tensor
        def _(pe):
            ada.start_tensor(pe)
            pe.wait_ge(silu, 1)
            for n in range(n_units + 1):
                if n < n_units:
                    ada.multiply(pe, n, n % 2, 16 * (n // 2 + 1))
                if n:
                    ada.turn(pe, n - 1)

        @block.vector
        def _(dve):
            nc.vector.memset(g.silu_c[:], 0.0).then_inc(zeroed, 1)
            ada.start_vector(dve)
            for n in range(n_units):
                ada.add(dve, n)
            dve.wait_ge(ada.added, n_units + 1)
            ada.finish(Seq(dve, dv), 0, range(n_units * BA // KB))


NP = 6
W = T // NP
PW = SEQ - (NP - 1) * W


def piece(ap, n):
    return ap[:, :, n * W:(n + 1) * W]


def stage_norm(nc, g, tag, spare, y, post, pre, x_in, x_out):
    with ExitStack() as stack:
        k = Kit(nc, stack, tag, spare)
        x = [k.sb(f"x{n}", [P, KB, W]) for n in range(NP)]
        NSL = 3
        sq = [k.sb(f"sq{z}", [P, KB, W]) for z in range(NSL)]
        hf = [k.sb(f"hf{z}", [P, KB, W]) for z in range(NSL)]
        root = [k.sb(f"root{z}", [P, W]) for z in range(NSL)]
        rstd = [k.sb(f"rstd{z}", [P, W]) for z in range(NSL)]
        ss = [k.ps(f"ss{z}", [P, 512]) for z in range(NSL)]
        x_landed = [k.sem(f"x_landed{n}") for n in range(NP)]
        x_stored, squared, summed, logged, rooted, dv, scaled, hid = (
            k.sem(s) for s in ("x_stored", "squared", "summed", "logged", "rooted", "dve", "scaled", "hi"))
        block = stack.enter_context(nc.Block())
        if y is None:
            jobs = [("x", n) for n in range(NP)]
        elif pre is None:
            jobs = [("y", n) for n in range(NP)]
        else:
            AHEAD = 3
            jobs = [("y", n) for n in range(AHEAD)]
            for n in range(AHEAD, NP):
                jobs += [("x", n - AHEAD), ("y", n)]
            jobs += [("x", n) for n in range(NP - AHEAD, NP)]
        at = {}

        def mod(spec, off):
            l, part = spec
            return g.mod[:, l, (part + off) * KB:(part + off + 1) * KB, :]

        def sample_mod(spec, off):
            return bc(mod(spec, off)[:, :, 1:C9].rearrange("p b (c t) -> p b c t", t=1), [P, KB, NB, NS])

        def sample_cols(t):
            return t[:, :, PW:W].rearrange("p b (c t) -> p b c t", t=NS)

        def prompt_cols(n):
            return W if n < NP - 1 else PW

        @block.vector
        def _(dve):
            chain = Seq(dve, dv)

            def add_to_x(j, n):
                ys, pc = piece(y, n), prompt_cols(n)
                dve.wait_ge(rooted, j + 1)
                chain.link(nc.vector.tensor_tensor(ys, ys, bc(rstd[j % NSL][:, None, :], [P, KB, W]), ALU.mult))
                at[("rstd", j)] = chain.n
                dve.wait_ge(x_landed[n], 16)
                for b in range(KB):
                    last = nc.vector.scalar_tensor_tensor(
                        out=x[n][:, b, 0:pc], in0=ys[:, b, 0:pc], scalar=mod(post, 0)[:, b, 0:1],
                        in1=x[n][:, b, 0:pc], op0=ALU.mult, op1=ALU.add)
                if n == NP - 1:
                    sy, sx = sample_cols(ys), sample_cols(x[n])
                    chain.link(nc.vector.tensor_tensor(sy, sy, sample_mod(post, 0), ALU.mult))
                    last = nc.vector.tensor_tensor(sx, sx, sy, ALU.add)
                chain.link(last)
                at[("x", n)] = chain.n

            def normalise_x(j, n):
                h = hf[n % NSL]
                dve.wait_ge(rooted, j + 1)
                if n >= NSL:
                    dve.wait_ge(hid, n - NSL + 1)
                chain.link(nc.vector.tensor_tensor(h[:], x[n][:], bc(rstd[j % NSL][:, None, :], [P, KB, W]), ALU.mult))
                at[("rstd", j)] = chain.n
                if n == NP - 1:
                    sh = sample_cols(h)
                    for off, op in ((1, ALU.mult), (0, ALU.add)):
                        chain.link(nc.vector.tensor_tensor(sh, sh, sample_mod(pre, off), op))
                at[("h", n)] = chain.n

            def low(n):
                dve.wait_ge(hid, n + 1)
                chain.link(nc.vector.tensor_tensor(piece(g.alo, n), hf[n % NSL][:], piece(g.ahi, n).bitcast(F32),
                                                   ALU.subtract))

            for j in range(len(jobs) + 2):
                if j >= 2 and jobs[j - 2][0] == "x":
                    low(jobs[j - 2][1])
                if j < len(jobs):
                    (add_to_x if jobs[j][0] == "y" else normalise_x)(j, jobs[j][1])

        @block.sync
        def _(sp):
            for n in range(NP):
                sp.dma_start(x[n][:], x_in[:, :, n * W:(n + 1) * W]).then_inc(x_landed[n], 16)
            if y is not None:
                for n in range(NP):
                    sp.wait_ge(dv, at[("x", n)])
                    sp.dma_start(x_out[:, :, n * W:(n + 1) * W], x[n][:]).then_inc(x_stored, 16)
                sp.wait_ge(x_stored, 16 * NP)

        @block.scalar
        def _(act):
            nc.scalar.preload_act_table_set(LN_EXP)
            def square(j, kind, n):
                if kind == "y":
                    src = piece(y, n)
                else:
                    src = x[n][:]
                    if y is None:
                        act.wait_ge(x_landed[n], 16)
                    else:
                        act.wait_ge(dv, at[("x", n)])
                if j >= NSL:
                    act.wait_ge(summed, j - NSL + 1)
                nc.scalar.activation(sq[j % NSL][:], src, ACT.Square).then_inc(squared, 1)

            def reciprocal_root(j):
                act.wait_ge(summed, j + 1)
                if j >= NSL:
                    act.wait_ge(rooted, j - NSL + 1)
                nc.scalar.activation(root[j % NSL][:], ss[j % NSL][:, 0:W], ACT.Ln, scale=1.0 / D,
                                     bias=g.eps[:, 0:1]).then_inc(logged, 1)
                act.wait_ge(logged, j + 1)
                if j >= NSL:
                    act.wait_ge(dv, at[("rstd", j - NSL)])
                nc.scalar.activation(rstd[j % NSL][:], root[j % NSL][:], ACT.Exp, scale=-0.5).then_inc(rooted, 1)

            def scale_and_shift(n):
                pc = prompt_cols(n)
                act.wait_ge(dv, at[("h", n)])
                for b in range(KB):
                    last = nc.scalar.activation(hf[n % NSL][:, b, 0:pc], hf[n % NSL][:, b, 0:pc], ACT.Identity,
                                                scale=mod(pre, 1)[:, b, 0:1], bias=mod(pre, 0)[:, b, 0:1])
                last.then_inc(scaled, 1)

            for j in range(len(jobs) + 3):
                if j < len(jobs):
                    square(j, *jobs[j])
                if 2 <= j < len(jobs) + 2:
                    reciprocal_root(j - 2)
                if j >= 3 and jobs[j - 3][0] == "x":
                    scale_and_shift(jobs[j - 3][1])

        @block.tensor
        def _(pe):
            for j in range(len(jobs)):
                pe.wait_ge(squared, j + 1)
                if j >= NSL:
                    pe.wait_ge(logged, j - NSL + 1)
                for b in range(KB):
                    last = nc.tensor.matmul(ss[j % NSL][:, 0:W], g.ones[:], sq[j % NSL][:, b, :],
                                            start=(b == 0), stop=(b == KB - 1))
                last.then_inc(summed, 1)

        if pre is not None:
            @block.gpsimd
            def _(pool):
                for n in range(NP):
                    pool.wait_ge(scaled, n + 1)
                    nc.gpsimd.tensor_tensor(piece(g.ahi, n), hf[n % NSL][:], bc(g.ones[:, 0:1, None], [P, KB, W]),
                                            ALU.mult).then_inc(hid, 1)


def split_first(nc, act, dve, st, hi, lo, landed, made, chain):
    if act is not None:
        act.wait_ge(landed[0], 16)
        nc.scalar.activation(hi[0][:], st[0][:], ACT.Copy).then_inc(chain, 1)
    else:
        dve.wait_ge(chain, 1)
        nc.vector.tensor_tensor(lo[0][:], st[0][:], hi[0][:].bitcast(F32), ALU.subtract).then_inc(made, 1)


def split_units(nc, pool, g, n_pairs, st, hi, lo, landed, made, freed, free_at, pool_chain):
    def split(i, u):
        pool.wait_ge(landed[u], i * 16 + 16)
        pool.wait_ge(freed, free_at(i, u))
        shape = [P, st[u].shape[1]]
        nc.gpsimd.tensor_tensor(hi[u][:], st[u][:], bc(g.ones[:, 0:1], shape), ALU.mult).then_inc(pool_chain, 1)
        pool.wait_ge(pool_chain, i * 2 + (u + 1))
        nc.gpsimd.tensor_tensor(lo[u][:], st[u][:], hi[u][:].bitcast(F32), ALU.subtract).then_inc(made, 1)

    pool.wait_ge(made, 1)
    split(0, 1)
    with pool.Fori(1, n_pairs) as i:
        for u in range(2):
            split(i, u)


def three_passes(nc, out, whi, wlo, xhi, xlo, nk):
    n = 0
    for kk in range(nk):
        for a, b in ((whi, xhi), (whi, xlo), (wlo, xhi)):
            last = nc.tensor.matmul(out, a(kk), b(kk), start=(n == 0), stop=(n == 3 * nk - 1))
            n += 1
    return last


def stage_linear(nc, g, tag, w, sections):
    n_units = sum(s[0] for s in sections)
    with ExitStack() as stack:
        k = Kit(nc, stack, tag)
        st = [k.sb(f"st{i}", [P, UW]) for i in range(2)]
        hi = [k.sb(f"hi{i}", [P, UW], F32R) for i in range(2)]
        lo = [k.sb(f"lo{i}", [P, UW], F32R) for i in range(2)]
        acc = [k.ps(f"acc{i}", [P, NT, 512]) for i in range(2)]
        landed = [k.sem(f"landed{i}") for i in range(2)]
        made, used, taken, pc = k.sem("made"), k.sem("used"), k.sem("taken"), k.sem("pool")
        stored = k.sem("stored")
        block = stack.enter_context(nc.Block())

        @block.sync
        def _(sp):
            for u in range(2):
                sp.dma_start(st[u][:], w[u]).then_inc(landed[u], 16)
            with sp.Fori(1, n_units // 2) as i:
                for u in range(2):
                    sp.wait_ge(made, i * 2 + (u - 1))
                    sp.dma_start(st[u][:], w[i * 2 + u]).then_inc(landed[u], 16)

        @block.gpsimd
        def _(pool):
            split_units(nc, pool, g, n_units // 2, st, hi, lo, landed, made, used,
                        lambda i, u: i * 2 + (u + 1), pc)

        @block.tensor
        def _(pe):
            pe.sem_inc(used, 2)
            with pe.Fori(0, n_units // 2) as i:
                for u in range(2):
                    pe.wait_ge(made, i * 2 + (u + 1))
                    pe.wait_ge(taken, i * 2 + (u + 1))
                    for n in range(NT):
                        last = three_passes(nc, acc[u][:, n, 0:TT],
                                            lambda kk: hi[u][:, kk * P:(kk + 1) * P],
                                            lambda kk: lo[u][:, kk * P:(kk + 1) * P],
                                            lambda kk: third(g.ahi, n)[:, kk, :],
                                            lambda kk: third(g.alo, n)[:, kk, :], KB)
                    last.then_inc(used, 1)

        @block.vector
        def _(dve):
            split_first(nc, None, dve, st, hi, lo, landed, made, pc)

        @block.scalar
        def _(act):
            split_first(nc, act, None, st, hi, lo, landed, made, pc)
            act.sem_inc(taken, 2)
            at = 0
            for count, evacuate, store in sections:
                with act.Fori(at // 2, (at + count) // 2) as i:
                    for u in range(2):
                        act.wait_ge(used, i * 2 + (u + 3))
                        evacuate(i * 2 + (u - at), acc[u][:, :, 0:TT]).then_inc(taken, 1)
                        if store is not None:
                            act.wait_ge(taken, i * 2 + (u + 3))
                            dst, src = store(i * 2 + (u - at))
                            act.dma_start(dst, src).then_inc(stored, 16)
                at += count
            n_stored = sum(count for count, _, store in sections if store is not None)
            if n_stored:
                act.wait_ge(stored, 16 * n_stored)


class State:

    def __init__(self, nc, stack):
        def sb(name, shape, dt=F32):
            return stack.enter_context(nc.sbuf_tensor(name, shape, dt))

        self.const = sb("const", [P, NCONST])
        self.vec = sb("vec", [P, NVEC])
        self.ones = sb("ones", [P, P])
        self.eps = sb("eps", [P, 1])
        self.lam = sb("lam", [P, 2])
        self.mod = sb("mod", [P, 2, NMOD, C9])



    def col(self, name):
        return cols(self.const, name)

    def ident(self):
        return cols(self.const, "ident")

    def vcol(self, name):
        return cols(self.vec, name, VEC)

    def conv(self, l, c):
        cw, cb = VEC["conv_w"][0] + l * 2 * FB * 3, VEC["conv_b"][0] + l * 2 * FB
        return (lambda tap: self.vec[:, bass.ds(c * 3 + (cw + tap), 1)]), self.vec[:, bass.ds(c + cb, 1)]


def by_thirds(ap):
    return ap.rearrange("p o (n t) -> p (o n) t", n=NT)


def stage_project(nc, g, tag, spare, w, rotated, plain, dst, w_ada=None, ada_first=0):
    (n_rot, rot_out), (n_plain, plain_out) = rotated, plain
    passes = n_rot + n_plain
    with ExitStack() as stack:
        k = Kit(nc, stack, tag, spare)
        GU = KB * GW
        st = [k.sb(f"st{i}", [P, GU]) for i in range(2)]
        hi = [k.sb(f"hi{i}", [P, GU], F32R) for i in range(2)]
        lo = [k.sb(f"lo{i}", [P, GU], F32R) for i in range(2)]
        NR = 3
        res = [k.sb(f"res{i}", [P, GW]) for i in range(NR)]
        acc = [k.ps(f"acc{i}", [P, 512]) for i in range(NR)]
        landed = [k.sem(f"landed{i}") for i in range(2)]
        stored = [k.sem(f"stored{i}") for i in range(NR)]
        made, summed, pc = k.sem("made"), k.sem("summed"), k.sem("pool")
        ready, turned, copied = k.sem("ready"), k.sem("turned"), k.sem("copied")
        if n_rot:
            xc = k.sb("xc", [P, GW])
            xs = k.sb("xs", [P, GW])
            turn = [k.ps(f"turn{i}", [P, 2, P]) for i in range(2)]
            rc = k.sem("rc")
        UNITS = 8
        if w_ada is not None:
            ada = Modulation(nc, g, k, w_ada, ada_first)
            ada_dv = k.sem("ada_dv")
        block = stack.enter_context(nc.Block())
        rows = [P] * NCH + [TS]
        DEPTH = 2 * TILES

        @block.sync
        def _(sp):
            for u in range(2):
                sp.dma_start(st[u][:], w[u]).then_inc(landed[u], 16)
            with sp.Fori(1, passes) as i:
                for u in range(2):
                    sp.wait_ge(made, i * 2 + (u - 1))
                    sp.dma_start(st[u][:], w[i * 2 + u]).then_inc(landed[u], 16)

        @block.gpsimd
        def _(pool):
            split_units(nc, pool, g, passes, st, hi, lo, landed, made, summed,
                        lambda i, u: i * DEPTH + (u + 1) * TILES, pc)

        @block.tensor
        def _(pe):
            pe.sem_inc(summed, DEPTH)
            if w_ada is not None:
                ada.start_tensor(pe)

            def modulation(i, q):
                c, second = divmod(q - 2, 2)
                if second:
                    ada.turn(pe, i * UNITS + c)
                else:
                    ada.multiply(pe, i * UNITS + c, c % 2, i * (UNITS // 2 * 16) + 16 * (c // 2 + 1))

            def transposes(i, q):
                pe.wait_ge(ready, i * DEPTH + (q + 1 + NR))
                pe.wait_ge(copied, i * DEPTH + (q + 1))
                for j in range(2):
                    last = nc.tensor.transpose(turn[q % 2][:, j, :], res[q % NR][:, j * P:(j + 1) * P], g.ident())
                last.then_inc(turned, 1)

            def products(i, rotate):
                for q in range(DEPTH):
                    u, t = divmod(q, TILES)
                    r = rows[t]
                    if t == 0:
                        pe.wait_ge(made, i * 2 + (u + 1))
                    pe.wait_ge(ready, i * DEPTH + (q + 1))
                    last = three_passes(nc, acc[q % NR][0:r, 0:GW],
                                        lambda kk: g.ahi[:, kk, t * P:t * P + r],
                                        lambda kk: g.alo[:, kk, t * P:t * P + r],
                                        lambda kk: hi[u][:, kk * GW:(kk + 1) * GW],
                                        lambda kk: lo[u][:, kk * GW:(kk + 1) * GW], KB)
                    last.then_inc(summed, 1)
                    if rotate and q >= 1:
                        transposes(i, q - 1)
                    if w_ada is not None and q >= 2:
                        modulation(i, q)
                if rotate:
                    transposes(i, DEPTH - 1)

            if n_rot:
                with pe.Fori(0, n_rot) as i:
                    products(i, True)
            with pe.Fori(n_rot, passes) as i:
                products(i, False)

        @block.vector
        def _(dve):
            split_first(nc, None, dve, st, hi, lo, landed, made, pc)
            if w_ada is not None:
                ada.start_vector(dve)
            if n_rot:
                with dve.Fori(0, n_rot) as i:
                    for q in range(DEPTH):
                        if w_ada is not None and q >= 4 and q % 2 == 0:
                            ada.add(dve, i * UNITS + (q // 2 - 2))
                        t = q % TILES
                        r = rows[t]
                        x = acc[q % NR][0:r, 0:GW].rearrange("p (h m d) -> p h m d", h=4, m=2)
                        c4 = xc[0:r].rearrange("p (h m d) -> p h m d", h=4, m=2)
                        s4 = xs[0:r].rearrange("p (h m d) -> p h m d", h=4, m=2)
                        cos = g.col("cos")[0:r, t * 32:(t + 1) * 32]
                        sin = g.col("sin")[0:r, t * 64:(t + 1) * 64].rearrange("p (m d) -> p m d", m=2)
                        dve.wait_ge(summed, i * DEPTH + (q + 1 + DEPTH))
                        dve.wait_ge(ready, i * DEPTH + (q + NR))
                        nc.vector.tensor_tensor(c4, x, bc(cos[:, None, None, :], [r, 4, 2, 32]), ALU.mult)
                        for m in range(2):
                            last = nc.vector.tensor_tensor(s4[:, :, m, :], x[:, :, 1 - m, :],
                                                           bc(sin[:, None, m, :], [r, 4, 32]), ALU.mult)
                        last.then_inc(rc, 1)
                        dve.wait_ge(rc, i * DEPTH + (q + 1))
                        dve.wait_ge(stored[q % NR], (i * (DEPTH // NR) + (q // NR + 1)) * 16)
                        dve.wait_ge(turned, i * DEPTH + (q + 1))
                        nc.vector.tensor_tensor(res[q % NR][0:r], xc[0:r], xs[0:r], ALU.add).then_inc(ready, 1)
                    if w_ada is not None:
                        ada.add(dve, i * UNITS + (UNITS - 1))
            if w_ada is not None:
                with dve.Fori(n_rot, passes) as i:
                    for c in range(UNITS):
                        ada.add(dve, i * UNITS + c)
                dve.wait_ge(ada.added, passes * UNITS + 1)
                chain = Seq(dve, ada_dv)
                ada.finish(chain, 0, range(2, 6))
                ada.finish(chain, 1, range(6))

        @block.scalar
        def _(act):
            split_first(nc, act, None, st, hi, lo, landed, made, pc)
            for s in range(NR):
                act.sem_inc(stored[s], 16)
            act.sem_inc(copied, 2)
            act.sem_inc(turned, NR)
            act.sem_inc(ready, NR)
            if w_ada is not None:
                ada.start_scalar(act)

            def finish(i, rotate):
                if w_ada is not None:
                    for c in range(2):
                        ada.load(act, i * UNITS + c, c)
                for q in range(DEPTH):
                    if w_ada is not None and q >= 2 and q % 2 == 0:
                        c = q // 2 - 1
                        ada.take(act, i * UNITS + c)
                        if c + 2 < UNITS:
                            ada.load(act, i * UNITS + (c + 2), c % 2)
                    u, t = divmod(q, TILES)
                    r = rows[t]
                    if not rotate:
                        act.wait_ge(summed, i * DEPTH + (q + 1 + DEPTH))
                        act.wait_ge(stored[q % NR], (i * (DEPTH // NR) + (q // NR + 1)) * 16)
                        nc.scalar.activation(res[q % NR][0:r], acc[q % NR][0:r, 0:GW], ACT.Copy).then_inc(ready, 1)
                    act.wait_ge(ready, i * DEPTH + (q + 1 + NR))
                    out, group = (rot_out, i * 2 + u) if rotate else (plain_out, i * 2 + (u - 2 * n_rot))
                    act.dma_start(out[bass.ds(group, 1), t * P:t * P + r, :].rearrange("o p n -> p o n"),
                                  res[q % NR][0:r, None, :]).then_inc(stored[q % NR], 16)
                    if rotate:
                        act.wait_ge(turned, i * DEPTH + (q + 1 + NR))
                        nc.scalar.activation(dst[:, bass.ds(i * 4 + 2 * u, 2), t * P:t * P + r],
                                             turn[q % 2][:, :, 0:r], ACT.Copy).then_inc(copied, 1)

            if n_rot:
                with act.Fori(0, n_rot) as i:
                    finish(i, True)
            with act.Fori(n_rot, passes) as i:
                finish(i, False)
            for s in range(NR):
                act.wait_ge(stored[s], (passes * (DEPTH // NR) + 1) * 16)


def stage_ffn(nc, g, tag, l, w, y, conv_in, conv_out):
    PAIRS = FB // 2
    with ExitStack() as stack:
        k = Kit(nc, stack, tag)
        NSL = 3
        st = [k.sb(f"st{i}", [P, UW]) for i in range(2)]
        hi = [k.sb(f"hi{i}", [P, UW], F32R) for i in range(NSL)]
        lo = [k.sb(f"lo{i}", [P, UW], F32R) for i in range(NSL)]
        HIST = SEQ + 2
        UC = HIST + NB * (NS + 2)
        up = [k.sb(f"up{i}", [P, UC]) for i in range(2)]
        cv = [k.sb(f"cv{i}", [P, UC]) for i in range(2)]
        ghi = [k.sb(f"ghi{j}", [P, T], F32R) for j in range(2)]
        glo = [k.sb(f"glo{j}", [P, T], F32R) for j in range(2)]
        cin = k.sb("cin", [P, 2 * FB, NB, 2])
        cout = k.sb("cout", [P, 2 * FB, 2 * C9])
        acc = [k.ps(f"acc{i}", [P, NT, 512]) for i in range(2)]
        landed = [k.sem(f"landed{i}") for i in range(2)]
        made, used, pc = k.sem("made"), k.sem("used"), k.sem("pool")
        up_taken, down_taken, down_summed = k.sem("up_taken"), k.sem("down_taken"), k.sem("down_summed")
        cin_in, cout_out, affine, gelued, hid = (k.sem(x) for x in ("cin", "cout", "affine", "gelu", "hi"))
        conv = [k.sem(f"conv{i}") for i in range(2)]
        tap, prod, lod, zeroed = k.sem("tap"), k.sem("prod"), k.sem("lo"), k.sem("zeroed")
        block = stack.enter_context(nc.Block())

        def samples(t):
            return t[:, HIST:UC].rearrange("p (b c) -> p b c", c=NS + 2)

        @block.sync
        def _(sp):
            for u in range(2):
                sp.dma_start(st[u][:], w[u]).then_inc(landed[u], 16)
            sp.dma_start(cin[:], conv_in).then_inc(cin_in, 16)
            with sp.Fori(1, PAIRS * 3) as i:
                for u in range(2):
                    sp.wait_ge(made, i * 2 + (u - 1))
                    sp.dma_start(st[u][:], w[i * 2 + u]).then_inc(landed[u], 16)
            sp.wait_ge(up_taken, 2 * FB)
            sp.wait_ge(affine, 2 * FB)
            sp.dma_start(conv_out, cout[:]).then_inc(cout_out, 16)
            sp.wait_ge(cout_out, 16)

        @block.gpsimd
        def _(pool):
            def split(i, u):
                pool.wait_ge(landed[u % 2], i * 48 + 16 * (u // 2 + 1))
                pool.wait_ge(used, i * 6 + (u + 1))
                nc.gpsimd.tensor_tensor(hi[u % NSL][:], st[u % 2][:], bc(g.ones[:, 0:1], [P, UW]),
                                        ALU.mult).then_inc(pc, 1)
                pool.wait_ge(pc, i * 6 + (u + 1))
                nc.gpsimd.tensor_tensor(lo[u % NSL][:], st[u % 2][:], hi[u % NSL][:].bitcast(F32),
                                        ALU.subtract).then_inc(made, 1)

            pool.wait_ge(made, 1)
            for u in range(1, 6):
                split(0, u)
            with pool.Fori(1, PAIRS) as i:
                for u in range(6):
                    split(i, u)

        @block.tensor
        def _(pe):
            pe.sem_inc(used, NSL)

            def up_unit(s, a, made_at, wait_sem, wait_at):
                pe.wait_ge(made, made_at)
                if wait_sem is not None:
                    pe.wait_ge(wait_sem, wait_at)
                for n in range(NT):
                    last = three_passes(nc, acc[a][:, n, 0:TT],
                                        lambda kk: hi[s][:, kk * P:(kk + 1) * P],
                                        lambda kk: lo[s][:, kk * P:(kk + 1) * P],
                                        lambda kk: third(g.ahi, n)[:, kk, :],
                                        lambda kk: third(g.alo, n)[:, kk, :], KB)
                last.then_inc(used, 1)

            def down(i, s0, s1, made_at, up_at, down_at):
                pe.wait_ge(made, made_at)
                pe.wait_ge(lod, i * 2)
                for m in range(KB):
                    if m < 2:
                        pe.wait_ge(up_taken, up_at + (m - 1))
                    else:
                        pe.wait_ge(down_taken, down_at + (m - 1))
                    for n in range(NT):
                        last = three_passes(nc, acc[m % 2][:, n, 0:TT],
                                            lambda j: hi[(s0, s1)[j]][:, m * P:(m + 1) * P],
                                            lambda j: lo[(s0, s1)[j]][:, m * P:(m + 1) * P],
                                            lambda j: ghi[j][:, n * TT:(n + 1) * TT],
                                            lambda j: glo[j][:, n * TT:(n + 1) * TT], 2)
                    if m < KB - 1:
                        last.then_inc(down_summed, 1)
                    else:
                        last.then_inc(used, 2)

            up_unit(0, 0, 1, None, 0)
            up_unit(1, 1, 2, None, 0)
            up_unit(2, 0, 3, up_taken, 1)
            up_unit(0, 1, 4, up_taken, 2)
            with pe.Fori(1, PAIRS) as i:
                up_unit(1, 0, i * 6 - 1, up_taken, i * 4 - 1)
                up_unit(2, 1, i * 6, up_taken, i * 4)
                down(i, 0, 1, i * 6 + 2, i * 4 + 2, i * 8 - 8)
                up_unit(2, 0, i * 6 + 3, down_taken, i * 8 - 1)
                up_unit(0, 1, i * 6 + 4, down_taken, i * 8)
            down(PAIRS, 1, 2, PAIRS * 6, PAIRS * 4, PAIRS * 8 - 8)

        @block.scalar
        def _(act):
            split_first(nc, act, None, st, hi, lo, landed, made, pc)
            act.wait_ge(cin_in, 16)

            def hidden(n, j, first, used_a, used_b, down_used):
                for x in range(2):
                    c = n * 2 + x
                    act.wait_ge(used, (used_a, used_b)[x])
                    if not first:
                        act.wait_ge(conv[x], n)
                    nc.scalar.activation(up[x][:, 2:2 + 2 * TT].rearrange("p (n t) -> p n t", n=2),
                                         acc[x][:, 0:2, 0:TT], ACT.Copy)
                    nc.scalar.activation(up[x][:, 2 + 2 * TT:HIST], acc[x][:, 2, 0:PT], ACT.Copy)
                    nc.scalar.activation(samples(up[x])[:, :, 2:], acc[x][:, 2, PT:TT].rearrange(
                        "p (b t) -> p b t", t=NS), ACT.Copy)
                    nc.scalar.activation(samples(up[x])[:, None, :, 0:2], cin[:, bass.ds(c, 1), :, :],
                                         ACT.Copy).then_inc(up_taken, 1)
                    act.wait_ge(up_taken, c + 1)
                    nc.scalar.activation(cout[:, bass.ds(c, 1), 0:2], up[x][:, None, SEQ:HIST], ACT.Copy)
                    nc.scalar.activation(cout[:, bass.ds(c, 1), 2:].rearrange("p o (b t) -> p o b t", t=2),
                                         samples(up[x])[:, None, :, NS:], ACT.Copy)
                    if not first:
                        act.wait_ge(lod if x == 0 else prod, n)
                    wv, bv = g.conv(l, c)
                    nc.scalar.activation(cv[x][:, 2:], up[x][:, 2:], ACT.Identity, scale=wv(2), bias=bv)\
                        .then_inc(affine, 1)
                act.wait_ge(conv[0], n + 1)
                nc.scalar.activation(cv[0][:, 2:], cv[0][:, 2:], ACT.Gelu_apprx_tanh).then_inc(gelued, 1)
                act.wait_ge(prod, n + 1)
                if down_used is not None:
                    act.wait_ge(used, down_used)
                nc.scalar.activation(ghi[j][:, 0:SEQ], cv[0][:, 2:HIST], ACT.Copy)
                nc.scalar.activation(ghi[j][:, SEQ:T].rearrange("p (b t) -> p b t", t=NS),
                                     samples(cv[0])[:, :, 2:], ACT.Copy).then_inc(hid, 1)

            hidden(0, 0, True, 1 + NSL, 2 + NSL, None)
            hidden(1, 1, False, 3 + NSL, 4 + NSL, None)
            with act.Fori(1, PAIRS) as i:
                hidden(i * 2, 0, False, i * 6 + (NSL - 1), i * 6 + NSL, i * 6 + (NSL + 2))
                hidden(i * 2 + 1, 1, False, i * 6 + (NSL + 3), i * 6 + (NSL + 4), None)

        @block.vector
        def _(dve):
            split_first(nc, None, dve, st, hi, lo, landed, made, pc)
            for x in range(2):
                nc.vector.memset(up[x][:, 0:2], 0.0)
            nc.vector.memset(y[:], 0.0).then_inc(zeroed, 1)
            dve.wait_ge(zeroed, 1)

            def taps(n, x):
                wv, _ = g.conv(l, n * 2 + x)
                dve.wait_ge(affine, n * 2 + (x + 1))
                nc.vector.scalar_tensor_tensor(out=cv[x][:, 2:], in0=up[x][:, 1:UC - 1], scalar=wv(1),
                                               in1=cv[x][:, 2:], op0=ALU.mult, op1=ALU.add).then_inc(tap, 1)
                dve.wait_ge(tap, n * 2 + (x + 1))
                nc.vector.scalar_tensor_tensor(out=cv[x][:, 2:], in0=up[x][:, 0:UC - 2], scalar=wv(0),
                                               in1=cv[x][:, 2:], op0=ALU.mult, op1=ALU.add).then_inc(conv[x], 1)

            def gate(n):
                dve.wait_ge(gelued, n + 1)
                dve.wait_ge(conv[1], n + 1)
                nc.vector.tensor_tensor(cv[0][:, 2:], cv[0][:, 2:], cv[1][:, 2:], ALU.mult).then_inc(prod, 1)

            def low(n, j):
                dve.wait_ge(hid, n + 1)
                nc.vector.tensor_tensor(glo[j][:, 0:SEQ], cv[0][:, 2:HIST], ghi[j][:, 0:SEQ].bitcast(F32),
                                        ALU.subtract)
                nc.vector.tensor_tensor(glo[j][:, SEQ:T].rearrange("p (b t) -> p b t", t=NS),
                                        samples(cv[0])[:, :, 2:],
                                        ghi[j][:, SEQ:T].bitcast(F32).rearrange("p (b t) -> p b t", t=NS),
                                        ALU.subtract).then_inc(lod, 1)

            def add(i, m, first_used):
                if m < KB - 1:
                    dve.wait_ge(down_summed, i * 7 + (m - 6))
                else:
                    dve.wait_ge(used, first_used)
                ym = by_thirds(y[:, m:m + 1, :])
                nc.vector.tensor_tensor(ym, ym, acc[m % 2][:, :, 0:TT], ALU.add).then_inc(down_taken, 1)

            for n in range(2):
                taps(n, 0)
                taps(n, 1)
                gate(n)
                low(n, n)
            with dve.Fori(1, PAIRS) as i:
                u = i * 6 + (NSL + 2)
                add(i, 0, u)
                taps(i * 2, 0)
                add(i, 1, u)
                taps(i * 2, 1)
                add(i, 2, u)
                add(i, 3, u)
                gate(i * 2)
                for m in range(4, KB):
                    add(i, m, u)
                low(i * 2, 0)
                taps(i * 2 + 1, 0)
                taps(i * 2 + 1, 1)
                gate(i * 2 + 1)
                low(i * 2 + 1, 1)
            for m in range(KB):
                add(PAIRS, m, PAIRS * 6 + NSL)


QA, QB, KA, KBK = 0, 2, 6, 8
KA_GROUP, VA_GROUP, VB_GROUP = 3, 0, 2
PG = 4
GP = NPG // PG


def load_pages(sp, ids, q, cache):
    return [sp.value_load(ids[0:1, bass.ds(q * NPG + j, 1)], min_val=0, max_val=cache.shape[0] - 1) for j in range(NPG)]


def load_page(sp, cache, page, order, dst, j):
    return sp.dma_start(dst[:, j:j + 1], cache[bass.ds(page, 1)].rearrange(order))


def stage_retention(nc, g, qkT, rot, val, o, state_in, state_out, sstate_out, pages, ids, cache_k, kt):
    with ExitStack() as stack:
        k = Kit(nc, stack, "ret")
        v = [k.sb(f"v{z}", [P, H, DV]) for z in range(2)]
        kn = [k.sb(f"kn{z}", [P, 256]) for z in range(2)]
        kc = [k.sb(f"kc{z}", [P, 2, CH]) for z in range(2)]
        qz = [k.sb(f"qz{z}", [P, H, CH]) for z in range(2)]
        qd = [k.sb(f"qd{z}", [P, H, CH]) for z in range(2)]
        ks = [k.sb(f"ks{z}", [P, 256]) for z in range(2)]
        sm = [k.sb(f"sm{z}", [P, H, CH]) for z in range(2)]
        S = k.sb("S", [P, 2, DV])
        ps_s = [k.ps(f"ps_s{z}", [P, H, CH]) for z in range(2)]
        ps_o = [k.ps(f"ps_o{z}", [P, H, CH]) for z in range(2)]
        ps_d = k.ps("ps_d", [P, 2, 4 * DV])
        v_in = [k.sem(f"v_in{z}") for z in range(2)]
        zeroed, kcopied, qready, scored, masked = (k.sem(x) for x in ("zeroed", "kcopied", "qready", "scored", "masked"))
        summed, deltaed, stated, copied = (k.sem(x) for x in ("summed", "deltaed", "stated", "copied"))
        state_stored = k.sem("state_stored")
        block = stack.enter_context(nc.Block())

        def v_src(at, n):
            return val[VA_GROUP:VA_GROUP + 2, at, :].rearrange("g p f -> p g f")

        @block.sync
        def _(sp):
            def load(z, at):
                sp.dma_start(v[z][:].rearrange("p (g h) e -> p g (h e)", g=2), v_src(at, CH)).then_inc(v_in[z], 16)
                sp.dma_start(kn[z][:], rot[KA_GROUP, at, :]).then_inc(v_in[z], 16)

            for z in range(2):
                load(z, slice(z * CH, (z + 1) * CH))
            with sp.Fori(1, NCH // 2) as i:
                for z in range(2):
                    sp.wait_ge(deltaed, i * 2 + (z + 1))
                    load(z, bass.ds(i * 2 * CH + z * CH, CH))
            sp.wait_ge(stated, NCH + 1)
            sp.dma_start(state_out, S[:]).then_inc(state_stored, 16)
            sp.wait_ge(state_stored, 16)

        @block.scalar
        def _(act):
            act.sem_inc(copied, 2)
            with act.Fori(0, NCH // 2) as i:
                for z in range(2):
                    act.wait_ge(scored, i * 2 + (z + 1))
                    nc.scalar.activation(kc[z][:], qkT[:, KA:KA + 2, bass.ds(i * 2 * CH + z * CH, CH)],
                                         ACT.Copy).then_inc(kcopied, 1)
                for z in range(2):
                    act.wait_ge(summed, i * 2 + (z + 1))
                    nc.scalar.activation(o[:, 0:H, bass.ds(i * 2 * CH + z * CH, CH)], ps_o[z][:],
                                         ACT.Copy).then_inc(copied, 1)

        @block.tensor
        def _(pe):
            pe.sem_inc(scored, 2)
            pe.sem_inc(deltaed, 2)

            def score(i, z):
                pe.wait_ge(kcopied, i * 2 + (z + 1))
                pe.wait_ge(qready, i * 2 + (z + 1))
                for h in range(H):
                    last = nc.tensor.matmul(ps_s[z][:, h, :], kc[z][:, h // 2, :], qz[z][:, h, :],
                                            start=True, stop=True)
                last.then_inc(scored, 1)

            with pe.Fori(0, NCH // 2) as i:
                for z in range(2):
                    score(i, z)
                for z in range(2):
                    pe.wait_ge(v_in[z], i * 32 + 32)
                    pe.wait_ge(masked, i * 2 + (z + 1))
                    pe.wait_ge(stated, i * 2 + (z + 1))
                    pe.wait_ge(copied, i * 2 + (z + 1))
                    for h in range(H):
                        nc.tensor.matmul(ps_o[z][:, h, :], v[z][:, h, :], sm[z][:, h, :], start=True, stop=False)
                        last = nc.tensor.matmul(ps_o[z][:, h, :], S[:, h // 2, :], qd[z][:, h, :],
                                                start=False, stop=True)
                    last.then_inc(summed, 1)
                    for h in range(H):
                        last = nc.tensor.matmul(ps_d[64 * (h % 2):64 * (h % 2) + 64, 0, (h // 2) * DV:(h // 2 + 1) * DV],
                                                ks[z][:, h * 64:(h + 1) * 64], v[z][:, h, :], start=True, stop=True)
                    last.then_inc(deltaed, 1)

        @block.vector
        def _(dve):
            for z in range(2):
                nc.vector.memset(qz[z][:], 0.0)
            nc.vector.memset(S[:], 0.0).then_inc(zeroed, 1)
            dve.wait_ge(zeroed, 1)
            dve.sem_inc(stated, 1)
            with dve.Fori(0, NCH // 2) as i:
                for z in range(2):
                    at = bass.ds(i * 2 * CH + z * CH, CH)
                    dve.wait_ge(deltaed, i * 2 + (z + 1))
                    for s in range(2):
                        last = nc.vector.tensor_copy(qz[z][64 * s:64 * s + 64, s::2, :],
                                                     qkT[64 * s:64 * s + 64, QA:QA + 2, at])
                    last.then_inc(qready, 1)
                    dve.wait_ge(qready, i * 2 + (z + 1))
                    nc.vector.tensor_tensor(qd[z][:], qz[z][:], g.col("decq").rearrange("p (h i) -> p h i", h=H), ALU.mult)
                    dve.wait_ge(v_in[z], i * 32 + 32)
                    nc.vector.tensor_tensor(ks[z][:].rearrange("p (h d) -> p h d", h=H),
                                            kn[z][:].rearrange("p (h d) -> p h d", h=H),
                                            bc(g.col("deck")[:, :, None], [P, H, 64]), ALU.mult)
                    dve.wait_ge(scored, i * 2 + (z + 3))
                    nc.vector.tensor_tensor(sm[z][:], ps_s[z][:], g.col("decay").rearrange("p (h i) -> p h i", h=H),
                                            ALU.mult).then_inc(masked, 1)
                for z in range(2):
                    dve.wait_ge(deltaed, i * 2 + (z + 3))
                    for b in range(2):
                        last = nc.vector.scalar_tensor_tensor(
                            out=S[:, b, :], in0=S[:, b, :], scalar=g.col("decc")[:, b:b + 1],
                            in1=ps_d[:, 0, b * DV:(b + 1) * DV], op0=ALU.mult, op1=ALU.add)
                    last.then_inc(stated, 1)

    with ExitStack() as stack:
        k = Kit(nc, stack, "rets")
        v = k.sb("v", [TS, H, DV])
        vm = k.sb("vm", [P, H, NB, DV])
        zeroed = k.sem("zeroed")
        kn = k.sb("kn", [TS, 256])
        ks = k.sb("ks", [P, 256])
        qz = k.sb("qz", [P, H, TS])
        qd = k.sb("qd", [P, H, TS])
        sm = k.sb("sm", [TS, H, TS])
        ss = k.sb("ss", [P, NB, 2, DV])
        ps_s = k.ps("ps_s", [TS, H, TS])
        ps_o = k.ps("ps_o", [P, H, TS])
        ps_d = k.ps("ps_d", [P, 2, NB, DV])
        landed, out_done, ids_in, keys_in = (k.sem(x) for x in ("landed", "out_done", "ids_in", "keys_in"))
        qready, scored, masked, summed, deltaed, stated, dv = (
            k.sem(x) for x in ("qready", "scored", "masked", "summed", "deltaed", "stated", "dv"))
        block = stack.enter_context(nc.Block())

        @block.sync
        def _(sp):
            sp.dma_start(v[:].rearrange("p (g h) e -> p g (h e)", g=2),
                         val[VA_GROUP:VA_GROUP + 2, SEQ:T, :].rearrange("g p f -> p g f")).then_inc(landed, 16)
            sp.dma_start(kn[:], rot[KA_GROUP, SEQ:T, :]).then_inc(landed, 16)
            sp.dma_start(ss[:], state_in).then_inc(landed, 16)
            sp.dma_start(ids[:], pages.rearrange("b p -> (b p)")[None, :]).then_inc(ids_in, 16)
            sp.wait_ge(ids_in, 16)
            for j, page in enumerate(load_pages(sp, ids, 0, cache_k)):
                load_page(sp, cache_k, page, "o p h k -> p o h k", kt[j // GP], j % GP).then_inc(keys_in, 16)
            sp.wait_ge(stated, 1)
            sp.dma_start(sstate_out, ss[:]).then_inc(out_done, 16)
            sp.wait_ge(out_done, 16)
            sp.wait_ge(keys_in, 16 * NPG)

        @block.gpsimd
        def _(pool):
            for x in (ks, vm):
                nc.gpsimd.memset(x[:], 0.0).then_inc(zeroed, 1)

        @block.tensor
        def _(pe):
            pe.wait_ge(qready, 1)
            for h in range(H):
                last = nc.tensor.matmul(ps_s[:, h, :], qkT[:, KA + h // 2, SEQ:T], qz[:, h, :], start=True, stop=True)
            last.then_inc(scored, 1)
            pe.wait_ge(landed, 48)
            pe.wait_ge(masked, 1)
            for h in range(H):
                nc.tensor.matmul(ps_o[:, h, :], v[:, h, :], sm[:, h, :], start=True, stop=False)
                for b in range(NB):
                    last = nc.tensor.matmul(ps_o[:, h, b * NS:(b + 1) * NS], ss[:, b, h // 2, :],
                                            qd[:, h, b * NS:(b + 1) * NS], start=False, stop=(b == NB - 1))
            last.then_inc(summed, 1)
            for h in range(H):
                for n in range(2):
                    last = nc.tensor.matmul(ps_d[64 * (h % 2):64 * (h % 2) + 64, h // 2, n * 4:n * 4 + 4, :],
                                            ks[:, h * 64:(h + 1) * 64], vm[:, h, n * 4:n * 4 + 4, :],
                                            start=True, stop=True)
            last.then_inc(deltaed, 1)

        @block.vector
        def _(dve):
            chain = Seq(dve, dv)
            chain.link(nc.vector.memset(qz[:], 0.0))
            for s in range(2):
                last = nc.vector.tensor_copy(qz[64 * s:64 * s + 64, s::2, :], qkT[64 * s:64 * s + 64, QA:QA + 2, SEQ:T])
            last.then_inc(qready, 1)
            dve.wait_ge(qready, 1)
            nc.vector.tensor_tensor(qd[:], qz[:], g.col("sdecq").rearrange("p (h i) -> p h i", h=H), ALU.mult)
            dve.wait_ge(landed, 48)
            dve.wait_ge(zeroed, 2)
            nc.vector.tensor_tensor(ks[0:TS].rearrange("p (h d) -> p h d", h=H), kn[:].rearrange("p (h d) -> p h d", h=H),
                                    bc(g.col("sdeck")[0:TS, :, None], [TS, H, 64]), ALU.mult)
            for b in range(NB):
                nc.vector.tensor_scalar(vm[0:TS, :, b, :], v[:], g.col("bmask")[0:TS, b:b + 1], None, ALU.mult)
            dve.wait_ge(scored, 1)
            nc.vector.tensor_tensor(sm[:], ps_s[:], g.col("sdecay")[0:TS].rearrange("p (h i) -> p h i", h=H),
                                    ALU.mult).then_inc(masked, 1)
            dve.wait_ge(deltaed, 1)
            for b in range(2):
                last = nc.vector.scalar_tensor_tensor(out=ss[:, :, b, :], in0=ss[:, :, b, :],
                                                      scalar=g.col("sdecc")[:, b:b + 1], in1=ps_d[:, b, :, :],
                                                      op0=ALU.mult, op1=ALU.add)
            last.then_inc(stated, 1)

        @block.scalar
        def _(act):
            act.wait_ge(summed, 1)
            nc.scalar.activation(o[:, 0:H, SEQ:T], ps_o[:], ACT.Copy)


def stage_attention(nc, g, qkT, cache_k, cache_v, ids, kt, val, o):
    SC = 64 ** -0.5
    STEPS = 2 * NCH
    G = PG
    ROWS = 2 * H * NS
    SPP = NB * NCH // (H * NCH)
    SEQS = 2 * SPP
    WIN = STEPS // SEQS
    BT = 4
    with ExitStack() as stack:
        k = Kit(nc, stack, "att")
        v = [k.sb(f"v{u}", [P, NCH, DV]) for u in range(2)]
        qz = [k.sb(f"qz{z}", [P, 2, CH]) for z in range(2)]
        p = [k.sb(f"p{z}", [P, SEQ]) for z in range(3)]
        p2 = k.sb("second", [P, SEQ])
        aT = [k.sb(f"aT{z}", [P, NCH, CH]) for z in range(2)]
        mx, nm, sums, rs = (k.sb(x, [P, 2]) for x in ("mx", "nm", "sums", "rs"))
        ps_s = k.ps("ps_s", [P, 2, SEQ])
        ps_t = k.ps("ps_t", [P, BT, CH])
        ps_o = k.ps("ps_o", [P, 512])
        v_in = [k.sem(f"v_in{u}") for u in range(2)]
        zeroed, qready, scored, maxed, exped = (k.sem(x) for x in ("zeroed", "qready", "scored", "maxed", "exped"))
        mixed, turned, aready, summed, copied, dv = (
            k.sem(x) for x in ("mixed", "turned", "aready", "summed", "copied", "dv"))

        vt = [k.sb(f"vt{n}", [P, GP, H * DV]) for n in range(G)]
        vn = k.sb("vn", [NS, H * DV])
        cqz = k.sb("cqz", [P, H * (ROWS + 2 * NS)])
        ckn = k.sb("ckn", [P, H, NS])
        cp = k.sb("cp", [P, GP * PAGE])
        cpn = k.sb("cpn", [P, NS])
        cpT = k.sb("cpT", [P, GP, P])
        cpnT = k.sb("cpnT", [NS, P])
        os_ = k.sb("os", [P, H * DV])
        cmx, csums = k.sb("cmx", [P, 2]), k.sb("csums", [P, 2])
        cm, cnm, cs, cw = (k.sb(x, [P, 1]) for x in ("cm", "cnm", "cs", "cw"))
        erow, wrow = k.sb("erow", [1, G, ROWS]), k.sb("wrow", [1, G, ROWS])
        top, total, coef = (k.sb(x, [1, ROWS]) for x in ("top", "total", "coef"))
        bank_a = k.ps("bank_a", [P, 512])
        bank_b = k.ps("bank_b", [P, 512])
        vn_in = k.sem("vn_in")
        k_in = [k.sem(f"k_in{n}") for n in range(G)]
        cv_in = [k.sem(f"cv_in{n}") for n in range(G)]
        c_zeroed, c_qready, c_scored, c_maxed, c_exped, c_sums, c_turned, c_pready = (
            k.sem(f"c_{x}") for x in ("zeroed", "qready", "scored", "maxed", "exped", "sums", "turned", "pready"))
        c_diff, c_rexp, c_weighted, c_summed, c_wcol, c_scaled, c_picked, c_copied, c_dv = (
            k.sem(f"c_{x}") for x in ("diff", "rexp", "weighted", "summed", "wcol", "scaled", "picked", "copied", "dv"))
        block = stack.enter_context(nc.Block())
        W_COL, PICK = slice(0, 1), 16
        NEW_T, M_ROW, S_ROW, NEW = slice(0, P), slice(P, 2 * P), slice(2 * P, 3 * P), slice(3 * P, 3 * P + NS)

        def batches(s):
            return s % NCH // BT + 1

        PASS_BT = sum(batches(s) for s in range(STEPS))

        def batch_at(s):
            return sum(batches(x) for x in range(s))

        def new_cols(i, r):
            return bass.ds(i * (SEQS * NS) + (SEQ + r * NS), NS)

        @block.sync
        def _(sp):
            def load(n, cache, page, order, dst, sem):
                for j in range(GP):
                    load_page(sp, cache, page[n * GP + j], order, dst, j).then_inc(sem, 16)

            def values(q, page):
                sp.wait_ge(c_summed, q + 1)
                sp.dma_start(vn[:].rearrange("t (g f) -> t g f", g=2), val[VB_GROUP:VB_GROUP + 2,
                             bass.ds(q * NS + SEQ, NS), :].rearrange("g t f -> t g f")).then_inc(vn_in, 16)
                for n in range(G):
                    load(n, cache_v, page, "o p f -> p o f", vt[n], cv_in[n])

            for n in range(G):
                sp.sem_inc(k_in[n], 16 * GP)
            values(0, load_pages(sp, ids, 0, cache_v))
            with sp.Fori(1, NB) as q:
                page = load_pages(sp, ids, q, cache_k)
                sp.wait_ge(c_scored, q + 1)
                for n in range(G):
                    load(n, cache_k, page, "o p h k -> p o h k", kt[n], k_in[n])
                values(q, page)

        @block.gpsimd
        def _(pool):
            for z in range(2):
                last = nc.gpsimd.memset(qz[z][:], 0.0)
            last.then_inc(zeroed, 1)
            pool.wait_ge(zeroed, 1)
            with pool.Fori(0, H // 2) as i:
                for s in range(STEPS):
                    u, qb = divmod(s, NCH)
                    pool.wait_ge(scored, i * (2 * STEPS) + (2 * s + 2))
                    for m in range(2):
                        last = nc.gpsimd.tensor_copy(
                            qz[s % 2][64 * m:64 * m + 64, m:m + 1, :],
                            qkT[64 * m:64 * m + 64, bass.ds(i * 2 + (QB + u), 1), qb * CH:(qb + 1) * CH])
                    last.then_inc(qready, 1)

        @block.tensor
        def _(pe):
            pe.sem_inc(scored, 4)
            pe.sem_inc(turned, PASS_BT)
            pe.sem_inc(summed, STEPS)
            pe.sem_inc(c_scored, 1)
            pe.sem_inc(c_summed, 1)

            def score(i, s):
                u, qb = divmod(s, NCH)
                pe.wait_ge(qready, i * STEPS + (s + 1))
                for m in range(2):
                    pe.wait_ge(exped, i * (2 * STEPS) + (2 * s + m + 1))
                    for a in range(0, (qb + 1) * CH, 512):
                        b = min(a + 512, (qb + 1) * CH)
                        last = nc.tensor.matmul(ps_s[:, m, a:b], qz[s % 2][:, m, :],
                                                qkT[:, bass.ds(i * 2 + (KBK + u), 1), a:b].rearrange("p o k -> p (o k)"),
                                                start=True, stop=True)
                    last.then_inc(scored, 1)

            def turn(i, s, c):
                if c == 0:
                    pe.wait_ge(mixed, i * STEPS + (s + 1))
                pe.wait_ge(aready, i * PASS_BT + (batch_at(s) + c + 1))
                for j in range(c * BT, min(c * BT + BT, s % NCH + 1)):
                    last = nc.tensor.transpose(ps_t[:, j % BT, :], p[s % 3][:, j * CH:(j + 1) * CH], g.ident())
                last.then_inc(turned, 1)

            def product(i, s):
                u, qb = divmod(s, NCH)
                if qb == 0:
                    pe.wait_ge(v_in[u], i * 16 + 16)
                pe.wait_ge(aready, i * PASS_BT + (batch_at(s + 1) + 1))
                pe.wait_ge(copied, i * STEPS + (s + 1))
                for j in range(qb + 1):
                    last = nc.tensor.matmul(ps_o[:, 0:CH], v[u][:, j, :], aT[s % 2][:, j, :],
                                            start=(j == 0), stop=(j == qb))
                last.then_inc(summed, 1)

            def cached_scores(i, r):
                pe.wait_ge(c_qready, i * SEQS + (r + 1))
                pe.wait_ge(c_scaled, i * SEQS + (r + 1))
                for h in range(H):
                    for n in range(G):
                        nc.tensor.matmul(bank_b[n * ROWS:(n + 1) * ROWS, NEW], cqz[:, h * ROWS:(h + 1) * ROWS],
                                         ckn[:, h, :], start=(h == 0), stop=(h == H - 1))
                pe.wait_ge(c_copied, i * SEQS + (r + 1))
                for n in range(G):
                    pe.wait_ge(k_in[n], i * (SEQS * 16 * GP) + (r + 1) * (16 * GP))
                for h in range(H):
                    for n in range(G):
                        last = nc.tensor.matmul(bank_a[n * ROWS:(n + 1) * ROWS, :], cqz[:, h * ROWS:(h + 1) * ROWS],
                                                kt[n][:, :, h, :], start=(h == 0), stop=(h == H - 1))
                last.then_inc(c_scored, 1)

            def cached_turns(i, r):
                pe.wait_ge(c_sums, i * SEQS + (r + 1))
                for j in range(GP):
                    nc.tensor.transpose(bank_a[:, j * P:(j + 1) * P], cp[:, j * PAGE:(j + 1) * PAGE], g.ident())
                nc.tensor.matmul(bank_b[0:NS, NEW_T], cpn[:], g.ident(), start=True, stop=True)
                nc.tensor.matmul(bank_b[0:1, M_ROW], cm[:], g.ident(), start=True, stop=True)
                nc.tensor.matmul(bank_b[0:1, S_ROW], cs[:], g.ident(), start=True, stop=True).then_inc(c_turned, 1)

            def cached_products(i, r):
                pe.wait_ge(c_pready, i * SEQS + (r + 1))
                pe.wait_ge(c_weighted, i * SEQS + (r + 1))
                nc.tensor.matmul(bank_a[:, W_COL], wrow[:].rearrange("o g r -> o (g r)"), g.ones[0:1, 0:1],
                                 start=True, stop=True)
                pe.wait_ge(vn_in, i * (SEQS * 16) + (r + 1) * 16)
                for n in range(G):
                    pe.wait_ge(cv_in[n], i * (SEQS * 16 * GP) + (r + 1) * (16 * GP))
                for j in range(GP):
                    for n in range(G):
                        nc.tensor.matmul(bank_b[n * ROWS:(n + 1) * ROWS, :], cpT[:, j, n * ROWS:(n + 1) * ROWS],
                                         vt[n][:, j, :], start=(j == 0), stop=(j == GP - 1 and n < G - 1))
                n = G - 1
                nc.tensor.matmul(bank_b[n * ROWS:(n + 1) * ROWS, :], cpnT[:, n * ROWS:(n + 1) * ROWS], vn[:],
                                 start=False, stop=True).then_inc(c_summed, 1)

            def cached_picks(i, r):
                pe.wait_ge(c_scaled, i * SEQS + (r + 2))
                for h in range(H):
                    last = nc.tensor.matmul(bank_a[:, PICK + h * NS:PICK + (h + 1) * NS], os_[:, h * DV:(h + 1) * DV],
                                            g.col("sel")[:, h * NS:(h + 1) * NS], start=True, stop=True)
                last.then_inc(c_picked, 1)

            with pe.Fori(0, H // 2) as i:
                for s in range(STEPS + 3):
                    if s < STEPS:
                        score(i, s)
                    if 2 <= s < STEPS + 2:
                        for c in range(batches(s - 2)):
                            turn(i, s - 2, c)
                    if s < STEPS:
                        (cached_scores, cached_turns, cached_products, cached_picks)[s % WIN](i, s // WIN)
                    if s >= 3:
                        product(i, s - 3)

        @block.vector
        def _(dve):
            start = Seq(dve, c_zeroed)
            start.link(nc.vector.memset(cqz[:], 0.0))
            maps = g.col("maps")[0:1]
            start.link(nc.vector.scalar_tensor_tensor(out=coef[:], in0=maps[:, ROWS:2 * ROWS], scalar=g.lam[0:1, 1:2],
                                                      in1=maps[:, 0:ROWS], op0=ALU.mult, op1=ALU.add))

            LINKS = 7

            def masked_max(i, s):
                qb = s % NCH
                L = (qb + 1) * CH
                for m in range(2):
                    link = i * (LINKS * STEPS) + (LINKS * s + 2 * m)
                    diag = ps_s[:, m, qb * CH:L]
                    dve.wait_ge(scored, i * (2 * STEPS) + (2 * s + m + 5))
                    nc.vector.tensor_tensor(diag, diag, g.col("causal"), ALU.add).then_inc(dv, 1)
                    dve.wait_ge(dv, link + 1)
                    nc.vector.tensor_reduce(out=mx[:, m:m + 1], in_=ps_s[:, m, 0:L], axis=AX.X, op=ALU.max)\
                        .then_inc(dv, 1)
                    dve.wait_ge(dv, link + 2)
                    dve.wait_ge(exped, i * (2 * STEPS) + (2 * s + m + 1))
                    nc.vector.tensor_scalar(nm[:, m:m + 1], mx[:, m:m + 1], -SC, None, ALU.mult).then_inc(maxed, 1)

            def mix(i, s):
                L = (s % NCH + 1) * CH
                link = i * (LINKS * STEPS) + (LINKS * s + 4)
                dve.wait_ge(exped, i * (2 * STEPS) + (2 * s + 4))
                nc.vector.reciprocal(rs[:], sums[:]).then_inc(dv, 1)
                dve.wait_ge(dv, link + 1)
                nc.vector.tensor_tensor(rs[:, 1:2], rs[:, 1:2], g.lam[:, 1:2], ALU.mult).then_inc(dv, 1)
                mine = p[s % 3][:, 0:L]
                nc.vector.tensor_scalar(mine, mine, rs[:, 0:1], None, ALU.mult).then_inc(dv, 1)
                dve.wait_ge(dv, link + 3)
                nc.vector.scalar_tensor_tensor(out=mine, in0=p2[:, 0:L], scalar=rs[:, 1:2], in1=mine, op0=ALU.mult, op1=ALU.add).then_inc(mixed, 1)

            C_LINKS = 8

            def cached_chain(i, r, n):
                chain = Seq(dve, c_dv)
                chain.base = i * (SEQS * C_LINKS) + (r * C_LINKS + n)
                return chain

            def cached_queries(i, r):
                dve.wait_ge(c_scored, i * SEQS + (r + 1))
                nc.vector.tensor_copy(ckn[:], qkT[:, KBK:KBK + H, new_cols(i, r)])
                for m in range(2):
                    last = nc.vector.tensor_copy(
                        cqz[64 * m:64 * m + 64, :].rearrange("p (h c) -> p h c", h=H)[:, :, m * NS:(m + 1) * NS],
                        qkT[64 * m:64 * m + 64, QB:QB + H, new_cols(i, r)])
                last.then_inc(c_qready, 1)

            def cached_max(i, r):
                chain = cached_chain(i, r, 0)
                dve.wait_ge(c_scored, i * SEQS + (r + 2))
                chain.link(nc.vector.tensor_tensor(bank_b[:, NEW], bank_b[:, NEW], g.col("smask"), ALU.add))
                nc.vector.tensor_reduce(out=cmx[:, 0:1], in_=bank_a[:], axis=AX.X, op=ALU.max)
                chain.link(nc.vector.tensor_reduce(out=cmx[:, 1:2], in_=bank_b[:, NEW], axis=AX.X, op=ALU.max))
                dve.wait_ge(c_turned, i * SEQS + (r + 1))
                chain.link(nc.vector.tensor_reduce(out=cm[:], in_=cmx[:], axis=AX.X, op=ALU.max))
                dve.wait_ge(c_exped, i * SEQS + (r + 1))
                nc.vector.tensor_scalar(cnm[:], cm[:], -SC, None, ALU.mult).then_inc(c_maxed, 1)

            def cached_sums(i, r):
                dve.wait_ge(c_exped, i * SEQS + (r + 2))
                nc.vector.tensor_reduce(out=cs[:], in_=csums[:], axis=AX.X, op=ALU.add).then_inc(c_sums, 1)

            def rows(cols_):
                return bank_b[0:1, cols_].rearrange("o (g r) -> o g r", g=G)

            def cached_top(i, r):
                chain = cached_chain(i, r, 3)
                dve.wait_ge(c_turned, i * SEQS + (r + 2))
                dve.wait_ge(c_pready, i * SEQS + (r + 1))
                chain.link(nc.vector.tensor_reduce(out=top[:], in_=bank_b[0:1, M_ROW].rearrange("o (g r) -> o r g", g=G),
                                                   axis=AX.X, op=ALU.max))
                nc.vector.tensor_tensor(erow[:], rows(M_ROW), bc(top[:, None, :], [1, G, ROWS]),
                                        ALU.subtract).then_inc(c_diff, 1)

            def cached_weights(i, r):
                chain = cached_chain(i, r, 4)
                dve.wait_ge(c_rexp, i * SEQS + (r + 1))
                dve.wait_ge(c_wcol, i * SEQS + (r + 1))
                chain.link(nc.vector.tensor_tensor(wrow[:], erow[:], rows(S_ROW), ALU.mult))
                chain.link(nc.vector.tensor_reduce(out=total[:], in_=wrow[:].rearrange("o g r -> o r g"), axis=AX.X,
                                                   op=ALU.add))
                chain.link(nc.vector.reciprocal(total[:], total[:]))
                chain.link(nc.vector.tensor_tensor(total[:], total[:], coef[:], ALU.mult))
                nc.vector.tensor_tensor(wrow[:], erow[:], bc(total[:, None, :], [1, G, ROWS]),
                                        ALU.mult).then_inc(c_weighted, 1)

            def cached_column(i, r):
                dve.wait_ge(c_summed, i * SEQS + (r + 2))
                nc.vector.tensor_copy(cw[:], bank_a[:, W_COL]).then_inc(c_wcol, 1)

            def cached_output(i, r):
                dve.wait_ge(c_picked, i * SEQS + (r + 1))
                nc.vector.tensor_copy(o[:, H:2 * H, new_cols(i, r)],
                                      bank_a[:, PICK:PICK + H * NS].rearrange("p (h t) -> p h t", h=H)).then_inc(c_copied, 1)

            with dve.Fori(0, H // 2) as i:
                for s in range(STEPS):
                    r, w = divmod(s, WIN)
                    if w == 0:
                        cached_queries(i, r)
                    if w == 1:
                        cached_sums(i, r)
                    if w == 2:
                        cached_weights(i, r)
                    masked_max(i, s)
                    mix(i, s)
                    (cached_max, cached_top, cached_column, cached_output)[w](i, r)

        @block.scalar
        def _(act):
            act.sem_inc(exped, 2)
            act.sem_inc(aready, 1)
            act.sem_inc(copied, 1)
            for x in (c_exped, c_scaled, c_copied, c_turned, c_wcol):
                act.sem_inc(x, 1)

            def exps(i, s):
                L = (s % NCH + 1) * CH
                if s >= 3:
                    act.wait_ge(turned, i * PASS_BT + (PASS_BT + batch_at(s - 2)))
                else:
                    before = max(x for x in range(STEPS) if x % 3 == s)
                    act.wait_ge(turned, i * PASS_BT + batch_at(before + 1))
                if s:
                    act.wait_ge(mixed, i * STEPS + s)
                for m in range(2):
                    act.wait_ge(maxed, i * (2 * STEPS) + (2 * s + m + 1))
                    nc.scalar.activation((p[s % 3], p2)[m][:, 0:L], ps_s[:, m, 0:L], ACT.Exp, scale=SC,
                                         bias=nm[:, m:m + 1], accum_out=sums[:, m:m + 1]).then_inc(exped, 1)

            def take_turned(i, s, c):
                act.wait_ge(turned, i * PASS_BT + (PASS_BT + batch_at(s) + c + 1))
                if c == 0:
                    act.wait_ge(summed, i * STEPS + (s + 1 + STEPS - 2))
                n = min(BT, s % NCH + 1 - c * BT)
                nc.scalar.activation(aT[s % 2][:, c * BT:c * BT + n, :], ps_t[:, 0:n, :], ACT.Copy).then_inc(aready, 1)

            def take_product(i, s):
                u, qb = divmod(s, NCH)
                act.wait_ge(summed, i * STEPS + (s + 1 + STEPS))
                nc.scalar.activation(o[:, bass.ds(i * 2 + (H + u), 1), qb * CH:(qb + 1) * CH], ps_o[:, None, 0:CH],
                                     ACT.Copy).then_inc(copied, 1)

            def cached_exps(i, r):
                act.wait_ge(c_maxed, i * SEQS + (r + 1))
                nc.scalar.activation(cp[:], bank_a[:], ACT.Exp, scale=SC, bias=cnm[:], accum_out=csums[:, 0:1])
                nc.scalar.activation(cpn[:], bank_b[:, NEW], ACT.Exp, scale=SC, bias=cnm[:],
                                     accum_out=csums[:, 1:2]).then_inc(c_exped, 1)

            def cached_take(i, r):
                act.wait_ge(c_turned, i * SEQS + (r + 2))
                nc.scalar.activation(cpT[:].rearrange("p j r -> p (j r)"), bank_a[:], ACT.Copy)
                nc.scalar.activation(cpnT[:], bank_b[0:NS, NEW_T], ACT.Copy).then_inc(c_pready, 1)
                act.wait_ge(c_diff, i * SEQS + (r + 1))
                nc.scalar.activation(erow[:], erow[:], ACT.Exp, scale=SC).then_inc(c_rexp, 1)

            def cached_scale(i, r):
                act.wait_ge(c_wcol, i * SEQS + (r + 2))
                act.wait_ge(c_summed, i * SEQS + (r + 2))
                nc.scalar.activation(os_[:], bank_b[:], ACT.Copy, scale=cw[:]).then_inc(c_scaled, 1)

            with act.Fori(0, H // 2) as i:
                for u in range(2):
                    act.wait_ge(summed, i * STEPS + (u + 1) * NCH)
                    act.dma_start(v[u][:], val[bass.ds(i + VB_GROUP, 1), 0:SEQ, u * DV:(u + 1) * DV].rearrange(
                        "o (c p) e -> p (o c) e", p=P)).then_inc(v_in[u], 16)
                for s in range(STEPS + 4):
                    if s < STEPS and s % WIN == 3:
                        cached_scale(i, s // WIN)
                    if 2 <= s < STEPS + 2:
                        for c in range(batches(s - 2)):
                            take_turned(i, s - 2, c)
                    if s >= 4:
                        take_product(i, s - 4)
                    if s < STEPS:
                        exps(i, s)
                    if s < STEPS and s % WIN == 0:
                        cached_exps(i, s // WIN)
                    if s < STEPS and s % WIN == 1:
                        cached_take(i, s // WIN)


def stage_heads(nc, g, tag, o, gate, plan):
    NBLK = max(len(b) for b, _, _ in plan)
    with ExitStack() as stack:
        k = Kit(nc, stack, tag)
        gb = [k.sb(f"g{z}", [P, NBLK, T]) for z in range(2)]
        sq = [k.sb(f"sq{z}", [P, NBLK, T]) for z in range(2)]
        ln = [k.sb(f"ln{z}", [P, T]) for z in range(2)]
        rstd = [k.sb(f"rstd{z}", [P, T]) for z in range(2)]
        ss = [k.ps(f"ss{z}", [P, NT, 512]) for z in range(2)]
        gated = [k.sem(f"gated{z}") for z in range(2)]
        squared, summed, logged, rooted, mixed, hid, dv = (
            k.sem(x) for x in ("squared", "summed", "logged", "rooted", "mixed", "hid", "dv"))
        block = stack.enter_context(nc.Block())
        at = {}

        def head(n):
            blocks = plan[n][0]
            return slice(blocks[0], blocks[0] + len(blocks))

        @block.sync
        def _(sp):
            gates = [0, 0]
            for n, (blocks, gate_at, _) in enumerate(plan):
                z, w = n % 2, len(blocks)
                if gate_at is not None:
                    if n >= 2:
                        sp.wait_ge(mixed, n - 1)
                    sp.dma_start(gb[z][:, 0:w, :], gate[:, gate_at:gate_at + w, :]).then_inc(gated[z], 16)
                    gates[z] += 16
                    at[("gate", n)] = gates[z]

        @block.scalar
        def _(act):
            nc.scalar.preload_act_table_set(LN_EXP)
            for n in range(len(plan) + 1):
                if n < len(plan):
                    if n >= 2:
                        act.wait_ge(summed, n - 1)
                    nc.scalar.activation(sq[n % 2][:, 0:len(plan[n][0]), :], o[:, head(n), :],
                                         ACT.Square).then_inc(squared, 1)
                if n:
                    m, z = n - 1, (n - 1) % 2
                    act.wait_ge(summed, m + 1)
                    if m >= 2:
                        act.wait_ge(rooted, m - 1)
                    nc.scalar.activation(by_thirds(ln[z][:, None, :]), ss[z][:, :, 0:TT], ACT.Ln,
                                         scale=1.0 / (len(plan[m][0]) * P), bias=g.eps[:, 0:1]).then_inc(logged, 1)
                    act.wait_ge(logged, m + 1)
                    if m >= 2:
                        act.wait_ge(mixed, m - 1)
                    nc.scalar.activation(rstd[z][:], ln[z][:], ACT.Exp, scale=-0.5).then_inc(rooted, 1)

        @block.gpsimd
        def _(pool):
            for n, (blocks, _, _) in enumerate(plan):
                pool.wait_ge(mixed, n + 1)
                nc.gpsimd.tensor_tensor(g.ahi[:, head(n), :], o[:, head(n), :],
                                        bc(g.ones[:, 0:1, None], [P, len(blocks), T]), ALU.mult).then_inc(hid, 1)

        @block.tensor
        def _(pe):
            for n, (blocks, _, _) in enumerate(plan):
                pe.wait_ge(squared, n + 1)
                if n >= 2:
                    pe.wait_ge(logged, n - 1)
                w = len(blocks)
                for t in range(NT):
                    for b in range(w):
                        last = nc.tensor.matmul(ss[n % 2][:, t, 0:TT], g.ones[:], sq[n % 2][:, b, t * TT:(t + 1) * TT],
                                                start=(b == 0), stop=(b == w - 1))
                last.then_inc(summed, 1)

        @block.vector
        def _(dve):
            chain = Seq(dve, dv)

            def low(n):
                dve.wait_ge(hid, n + 1)
                nc.vector.tensor_tensor(g.alo[:, head(n), :], o[:, head(n), :], g.ahi[:, head(n), :].bitcast(F32),
                                        ALU.subtract)

            for n, (blocks, gate_at, weights) in enumerate(plan):
                z = n % 2
                dve.wait_ge(rooted, n + 1)
                for i, b in enumerate(blocks):
                    x = o[:, b, :]
                    last = nc.vector.scalar_tensor_tensor(out=x, in0=x, scalar=weights[i] if weights else 1.0,
                                                          in1=rstd[z][:], op0=ALU.mult, op1=ALU.mult)
                if gate_at is None:
                    last.then_inc(mixed, 1)
                else:
                    chain.link(last)
                    dve.wait_ge(gated[z], at[("gate", n)])
                    nc.vector.tensor_tensor(o[:, head(n), :], o[:, head(n), :], gb[z][:, 0:len(blocks), :],
                                            ALU.mult).then_inc(mixed, 1)
                if n:
                    low(n - 1)
            low(len(plan) - 1)


def stage_gate(nc, g, w_a, w_gate, scan_mask, b):
    RANK = 16
    with ExitStack() as stack:
        k = Kit(nc, stack, "gate")
        w = k.sb("w", [P, KB * RANK])
        whi = k.sb("whi", [P, KB * RANK], F32R)
        wlo = k.sb("wlo", [P, KB * RANK], F32R)
        wg = k.sb("wg", [P, H * P])
        zeroed, w_in = k.sem("zeroed"), k.sem("w_in")
        mask = k.sb("mask", [P, T])
        aT = k.sb("aT", [P, T])
        ab = [k.sb(f"ab{i}", [P, T]) for i in range(2)]
        low = [k.sb(f"low{i}", [P, T]) for i in range(2)]
        z = [k.ps(f"z{i}", [P, NT, 512]) for i in range(2)]
        acc = z[1][0:RANK]
        landed, split, summed, taken, gated, expd, minned, subbed, scanned = (
            k.sem(x) for x in ("landed", "split", "summed", "taken", "gated", "expd", "minned", "subbed", "scanned"))
        block = stack.enter_context(nc.Block())

        @block.sync
        def _(sp):
            sp.dma_start(w[:], w_a).then_inc(w_in, 16)
            sp.dma_start(mask[:], scan_mask).then_inc(landed, 16)
            sp.wait_ge(zeroed, 1)
            sp.dma_start(wg[0:RANK, :], w_gate).then_inc(landed, 16)

        @block.gpsimd
        def _(pool):
            nc.gpsimd.memset(wg[:], 0.0).then_inc(zeroed, 1)
            nc.gpsimd.memset(aT[:], 0.0).then_inc(zeroed, 1)

        @block.tensor
        def _(pe):
            pe.wait_ge(split, 2)
            for n in range(NT):
                last = three_passes(nc, acc[:, n, 0:TT], lambda kk: whi[:, kk * RANK:(kk + 1) * RANK],
                                    lambda kk: wlo[:, kk * RANK:(kk + 1) * RANK],
                                    lambda kk: third(g.ahi, n)[:, kk, :], lambda kk: third(g.alo, n)[:, kk, :], KB)
            last.then_inc(summed, 1)
            pe.wait_ge(taken, 1)
            pe.wait_ge(landed, 32)
            for h in range(H):
                if h >= 2:
                    pe.wait_ge(expd, 3 * (h - 2) + 1)
                for n in range(NT):
                    last = nc.tensor.matmul(z[h % 2][:, n, 0:TT], wg[:, h * P:(h + 1) * P], aT[:, n * TT:(n + 1) * TT],
                                            start=True, stop=True)
                last.then_inc(gated, 1)

        @block.scalar
        def _(act):
            nc.scalar.preload_act_table_set(LN_EXP)
            act.wait_ge(summed, 1)
            act.wait_ge(zeroed, 2)
            nc.scalar.activation(by_thirds(aT[0:RANK, None, :]), acc[:, :, 0:TT], ACT.Copy).then_inc(taken, 1)
            for h in range(H):
                act.wait_ge(minned, h + 1)
                if h >= 2:
                    act.wait_ge(subbed, h - 1)
                x = ab[h % 2]
                nc.scalar.activation(by_thirds(x[:, None, :]), z[h % 2][:, :, 0:TT], ACT.Abs,
                                     bias=g.vcol("b_gate")[:, h:h + 1]).then_inc(expd, 1)
                act.wait_ge(expd, 3 * h + 1)
                nc.scalar.activation(x[:], x[:], ACT.Exp, scale=-1.0).then_inc(expd, 1)
                act.wait_ge(expd, 3 * h + 2)
                nc.scalar.activation(x[:], x[:], ACT.Ln, bias=1.0).then_inc(expd, 1)

        @block.vector
        def _(dve):
            dve.wait_ge(w_in, 16)
            nc.vector.tensor_copy(whi[:], w[:]).then_inc(split, 1)
            dve.wait_ge(split, 1)
            nc.vector.tensor_tensor(wlo[:], w[:], whi[:].bitcast(F32), ALU.subtract).then_inc(split, 1)

            def minimum(h):
                dve.wait_ge(gated, h + 1)
                if h >= 2:
                    dve.wait_ge(scanned, h - 1)
                nc.vector.tensor_scalar(by_thirds(low[h % 2][:, None, :]), z[h % 2][:, :, 0:TT],
                                        g.vcol("b_gate")[:, h:h + 1], 0.0, ALU.add, ALU.min).then_inc(minned, 1)

            minimum(0)
            for h in range(H):
                if h + 1 < H:
                    minimum(h + 1)
                dve.wait_ge(expd, 3 * h + 3)
                dve.wait_ge(minned, h + 1)
                nc.vector.tensor_tensor(low[h % 2][:], low[h % 2][:], ab[h % 2][:], ALU.subtract).then_inc(subbed, 1)
                dve.wait_ge(subbed, h + 1)
                if h == 0:
                    dve.wait_ge(landed, 32)
                nc.vector.tensor_tensor_scan(b[:, h, :], mask[:], low[h % 2][:], 0.0, ALU.mult,
                                             ALU.add).then_inc(scanned, 1)


def stage_gla(nc, g, qk, b, levels, v_dram, o, state_out, ahead):
    NL = len(LEVELS)
    IT = 1.0 / TAU
    DG = 256
    with ExitStack() as stack:
        k = Kit(nc, stack, "gla")
        lv = k.sb("lv", [P, NL + 1, P], I32)
        v = k.sb("v", [P, H, DG])
        E = [k.sb(f"E{l}", [P, H, CH]) for l in range(NL)]
        X = [k.sb(f"X{l}", [P, H, CH]) for l in range(NL)]
        ek, eq, kd, qe, kc, kdT, attT, attF = (
            k.sb(x, [P, H, CH]) for x in ("ek", "eq", "kd", "qe", "kc", "kdT", "attT", "attF"))
        ahead_in = k.sem("ahead_in")
        opened, opened_v = k.sem("opened"), k.sem("opened_v")
        el = k.sb("el", [P, H])
        S = k.sb("S", [P, H, DG])
        gram = [k.ps(f"gram{z}", [P, H, CH]) for z in range(2)]
        ps_t = k.ps("ps_t", [P, H, CH])
        ps_o = k.ps("ps_o", [P, 2 * H, CH])
        ps_d = k.ps("ps_d", [P, H, DG])
        v_in, lv_in, zeroed, out_done = k.sem("v_in"), k.sem("lv_in"), k.sem("zeroed"), k.sem("out_done")
        subbed, level_exped, k_exped, q_exped, l_exped, scaled, grammed, selected, kcopied, fixed = (
            k.sem(x) for x in ("subbed", "level_exped", "k_exped", "q_exped", "l_exped", "scaled", "grammed",
                               "selected", "kcopied", "fixed"))
        kd_made, qe_made, turned, kd_taken, summed, deltaed, stated, copied = (
            k.sem(x) for x in ("kd_made", "qe_made", "turned", "kd_taken", "summed", "deltaed", "stated", "copied"))
        block = stack.enter_context(nc.Block())
        NG = NL + 1

        def chunk(t, c):
            return t[:, :, bass.ds(c * CH, CH)]

        def halves(t, s):
            return t.rearrange("p h (n two s) -> p h n two s", two=2, s=s)

        @block.sync
        def _(sp):
            sp.dma_start(lv[:], levels).then_inc(lv_in, 16)
            for dst, src in ahead:
                sp.dma_start(dst, src).then_inc(ahead_in, 16)
            with sp.Fori(0, NCH) as i:
                sp.wait_ge(deltaed, i + 1)
                sp.dma_start(v[:], v_dram[:, bass.ds(i * CH, CH), :].rearrange("h p e -> p h e")).then_inc(v_in, 16)
            sp.wait_ge(ahead_in, 16 * len(ahead))
            sp.wait_ge(stated, NCH + 1)
            sp.dma_start(state_out, S[:]).then_inc(out_done, 16)
            sp.wait_ge(out_done, 16)

        @block.gpsimd
        def _(pool):
            with pool.Fori(0, NCH) as i:
                bt = chunk(b, i)
                for l, s in enumerate(LEVELS):
                    n = CH // (2 * s)
                    bh, eh = halves(bt, s), halves(E[l][:], s)
                    ref = bc(bh[:, :, :, 0, s - 1:s], [P, H, n, s])
                    pool.wait_ge(scaled, i * NL + (l + 1))
                    pool.sem_inc(opened, 1)
                    nc.gpsimd.tensor_tensor(eh[:, :, :, 0, :], ref, bh[:, :, :, 0, :], ALU.subtract)
                    nc.gpsimd.tensor_tensor(eh[:, :, :, 1, :], bh[:, :, :, 1, :], ref, ALU.subtract).then_inc(subbed, 1)
                pool.wait_ge(kd_made, i + 1)
                pool.sem_inc(opened, 1)
                nc.gpsimd.tensor_tensor(ek[:], bc(bt[:, :, CH - 1:CH], [P, H, CH]), bt, ALU.subtract).then_inc(subbed, 1)

        @block.scalar
        def _(act):
            act.sem_inc(kd_taken, 1)
            act.sem_inc(copied, 1)
            act.sem_inc(fixed, 1)

            def level_exps(c):
                for l in range(NL):
                    act.wait_ge(subbed, c * (NL + 1) + (l + 1))
                    nc.scalar.activation(E[l][:], E[l][:], ACT.Exp, scale=IT).then_inc(level_exped, 1)

            def state_exps(c):
                act.wait_ge(subbed, c * (NL + 1) + (NL + 1))
                nc.scalar.activation(ek[:], ek[:], ACT.Exp, scale=IT).then_inc(k_exped, 1)
                act.wait_ge(qe_made, c + 1)
                nc.scalar.activation(eq[:], chunk(b, c), ACT.Exp, scale=IT).then_inc(q_exped, 1)
                act.wait_ge(stated, c + 1)
                nc.scalar.activation(el[:, :, None], b[:, :, bass.ds(c * CH + (CH - 1), 1)], ACT.Exp,
                                     scale=IT).then_inc(l_exped, 1)

            def keys(c):
                act.wait_ge(grammed, c * NG + NG)
                nc.scalar.activation(kc[:], chunk(qk, c)[:, H:2 * H], ACT.Copy).then_inc(kcopied, 1)

            def fix_scores(c):
                act.wait_ge(selected, c * NG + (NG + 2))
                act.wait_ge(summed, c + 1)
                nc.scalar.activation(attF[:], attT[:], ACT.Copy).then_inc(fixed, 1)

            def take(c):
                act.wait_ge(turned, c + 2)
                act.wait_ge(deltaed, c + 1)
                nc.scalar.activation(kdT[:], ps_t[:], ACT.Copy).then_inc(kd_taken, 1)
                act.wait_ge(summed, c + 2)
                nc.scalar.activation(chunk(o, c), ps_o[:], ACT.Copy).then_inc(copied, 1)

            keys(0)
            level_exps(0)
            level_exps(1)
            state_exps(0)
            keys(1)
            fix_scores(0)
            with act.Fori(1, NCH - 1) as c:
                level_exps(c + 1)
                take(c - 1)
                state_exps(c)
                keys(c + 1)
                fix_scores(c)
            take(NCH - 2)
            state_exps(NCH - 1)
            fix_scores(NCH - 1)
            take(NCH - 1)

        @block.tensor
        def _(pe):
            pe.sem_inc(grammed, NG)
            pe.sem_inc(turned, 1)
            pe.sem_inc(summed, 1)
            pe.sem_inc(deltaed, 1)

            def scores(c, l):
                pe.wait_ge(selected, c * NG + (l + 1))
                if l < NL:
                    pe.wait_ge(scaled, c * NL + (NL + l + 1))
                else:
                    pe.wait_ge(kcopied, c + 1)
                for h in range(H):
                    rhs = X[l][:, h, :] if l < NL else chunk(qk, c)[:, h, :]
                    last = nc.tensor.matmul(gram[l % 2][:, h, :], (X[l] if l < NL else kc)[:, h, :], rhs,
                                            start=True, stop=True)
                last.then_inc(grammed, 1)

            def turn_keys(c):
                pe.wait_ge(kd_made, c + 2)
                pe.wait_ge(kd_taken, c + 1)
                for h in range(H):
                    last = nc.tensor.transpose(ps_t[:, h, :], kd[:, h, :], g.ident())
                last.then_inc(turned, 1)

            def outputs(c, heads):
                if heads[0] == 0:
                    pe.wait_ge(fixed, c + 2)
                    pe.wait_ge(qe_made, c + 2)
                    pe.wait_ge(v_in, c * 16 + 16)
                    pe.wait_ge(stated, c + 1)
                    pe.wait_ge(copied, c + 1)
                for h in heads:
                    for e in range(2):
                        nc.tensor.matmul(ps_o[:, 2 * h + e, :], v[:, h, e * P:(e + 1) * P], attF[:, h, :],
                                         start=True, stop=False)
                        last = nc.tensor.matmul(ps_o[:, 2 * h + e, :], S[:, h, e * P:(e + 1) * P], qe[:, h, :],
                                                start=False, stop=True)
                if heads[-1] == H - 1:
                    last.then_inc(summed, 1)

            def deltas(c):
                pe.wait_ge(kd_taken, c + 2)
                for h in range(H):
                    last = nc.tensor.matmul(ps_d[:, h, :], kdT[:, h, :], v[:, h, :], start=True, stop=True)
                last.then_inc(deltaed, 1)

            for l in range(NG):
                scores(0, l)
            with pe.Fori(1, NCH) as c:
                scores(c, 0)
                scores(c, 1)
                turn_keys(c - 1)
                scores(c, 2)
                outputs(c - 1, (0, 1))
                scores(c, 3)
                outputs(c - 1, (2, 3))
                scores(c, 4)
                deltas(c - 1)
                for l in range(5, NG):
                    scores(c, l)
            turn_keys(NCH - 1)
            outputs(NCH - 1, (0, 1, 2, 3))
            deltas(NCH - 1)

        @block.vector
        def _(dve):
            nc.vector.memset(S[:], 0.0)
            nc.vector.memset(attT[:], 0.0).then_inc(zeroed, 1)
            dve.wait_ge(zeroed, 1)
            dve.wait_ge(lv_in, 16)
            dve.sem_inc(stated, 1)
            dve.sem_inc(selected, 2)
            dve.sem_inc(scaled, NL)
            dve.sem_inc(kd_made, 1)
            dve.sem_inc(qe_made, 1)

            def scale_level(c, l):
                s = LEVELS[l]
                dve.wait_ge(level_exped, c * NL + (l + 1))
                dve.wait_ge(grammed, c * NG + (l + 1))
                xh, eh, th = halves(X[l][:], s), halves(E[l][:], s), halves(chunk(qk, c), s)
                nc.vector.tensor_tensor(xh[:, :, :, 0, :], th[:, H:2 * H, :, 0, :], eh[:, :, :, 0, :], ALU.mult)
                nc.vector.tensor_tensor(xh[:, :, :, 1, :], th[:, 0:H, :, 1, :], eh[:, :, :, 1, :],
                                        ALU.mult).then_inc(scaled, 1)

            def scale_keys(c):
                dve.wait_ge(k_exped, c + 1)
                dve.wait_ge(turned, c + 1)
                nc.vector.tensor_tensor(kd[:], chunk(qk, c)[:, H:2 * H], ek[:], ALU.mult).then_inc(kd_made, 1)

            def scale_queries(c):
                dve.wait_ge(q_exped, c + 1)
                dve.wait_ge(summed, c + 1)
                nc.vector.tensor_tensor(qe[:], chunk(qk, c)[:, 0:H], eq[:], ALU.mult).then_inc(qe_made, 1)

            def select(c, l):
                dve.wait_ge(grammed, c * NG + (NG + l + 1))
                dve.wait_ge(selected, c * NG + (l + 2))
                if l == 0:
                    dve.wait_ge(fixed, c + 1)
                dve.sem_inc(opened_v, 1)
                nc.vector.copy_predicated(attT[:], bc(lv[:, l, None, :], [P, H, CH]), gram[l % 2][:]).then_inc(selected, 1)

            def state(c):
                dve.wait_ge(deltaed, c + 2)
                dve.wait_ge(l_exped, c + 1)
                for h in range(H):
                    last = nc.vector.scalar_tensor_tensor(out=S[:, h, :], in0=S[:, h, :], scalar=el[:, h:h + 1],
                                                          in1=ps_d[:, h, :], op0=ALU.mult, op1=ALU.add)
                last.then_inc(stated, 1)

            def iteration(c, first=False, last=False):
                for l in range(NG):
                    if l < NL and not last:
                        scale_level(c + 1, l)
                    select(c, l)
                    if l == 4 and not first:
                        state(c - 1)
                    if l == 5:
                        scale_keys(c)
                    if l == 6:
                        scale_queries(c)

            for l in range(NL):
                scale_level(0, l)
            iteration(0, first=True)
            with dve.Fori(1, NCH - 1) as c:
                iteration(c)
            iteration(NCH - 1, last=True)
            state(NCH - 1)


def stage_gla_samples(nc, g, qk, b, levels, picks, v, ss, o, state_out):
    IT = 1.0 / TAU
    DG = 256
    LV = [l for l, s in enumerate(LEVELS) if 2 * s <= NS]
    with ExitStack() as stack:
        k = Kit(nc, stack, "glas")
        pick = k.sb("pick", [P, 2 * TS])
        lv = k.sb("lv", [P, len(LEVELS) + 1, P], I32)
        vm = [k.sb(f"vm{z}", [P, NB, DG]) for z in range(2)]
        zeroed = k.sem("zeroed")
        E = [k.sb(f"E{l}", [P, H, TS]) for l in range(len(LV))]
        X = [k.sb(f"X{l}", [P, H, TS]) for l in range(len(LV))]
        ek, eq, kd, qe = (k.sb(x, [P, H, TS]) for x in ("ek", "eq", "kd", "qe"))
        kdT = k.sb("kdT", [P, H, P])
        read = k.sb("read", [P, H, 2, DG])
        state_read, read_taken = k.sem("state_read"), k.sem("read_taken")
        attT = k.sb("attT", [TS, H, TS])
        el = k.sb("el", [P, H, NB])
        ps_g = k.ps("ps_g", [TS, len(LV) + 1, H, TS])
        ps_t = k.ps("ps_t", [TS, H, P])
        ps_o = k.ps("ps_o", [P, 2 * H, TS])
        ps_d = k.ps("ps_d", [P, NB, DG])
        landed, dv, exped, grammed, turned, taken, summed, deltaed, done, decayed, out_done = (
            k.sem(x) for x in ("landed", "dv", "exped", "grammed", "turned", "taken", "summed", "deltaed", "done",
                               "decayed", "out_done"))
        block = stack.enter_context(nc.Block())
        at = {}

        def halves(t, s):
            return t.rearrange("p h (n two s) -> p h n two s", two=2, s=s)

        def seqs(t):
            return t.rearrange("p h (b t) -> p h b t", t=NS)

        bt, qt, kt = b[:, :, SEQ:T], qk[:, 0:H, SEQ:T], qk[:, H:2 * H, SEQ:T]

        @block.sync
        def _(sp):
            sp.dma_start(lv[:], levels).then_inc(landed, 16)
            sp.dma_start(pick[:], picks).then_inc(landed, 16)
            for h in range(H):
                sp.wait_ge(done, h + 1)
                sp.dma_start(state_out[:, :, h, :], ss[:, :, h, :]).then_inc(out_done, 16)
            sp.wait_ge(out_done, 16 * H)

        def state(dve, h):
            dve.wait_ge(state_read, h + 1)
            nc.vector.tensor_tensor(ss[:, :, h, :], ss[:, :, h, :], bc(el[:, h, :, None], [P, NB, DG]),
                                    ALU.mult).then_inc(decayed, 1)
            dve.wait_ge(decayed, h + 1)
            dve.wait_ge(deltaed, h + 1)
            nc.vector.tensor_tensor(ss[:, :, h, :], ss[:, :, h, :], ps_d[:], ALU.add).then_inc(done, 1)

        @block.vector
        def _(dve):
            chain = Seq(dve, dv)
            for l, i in enumerate(LV):
                s = LEVELS[i]
                bh, eh = halves(bt, s), halves(E[l][:], s)
                ref = bc(bh[:, :, :, 0, s - 1:s], [P, H, TS // (2 * s), s])
                nc.vector.tensor_tensor(eh[:, :, :, 0, :], ref, bh[:, :, :, 0, :], ALU.subtract)
                nc.vector.tensor_tensor(eh[:, :, :, 1, :], bh[:, :, :, 1, :], ref, ALU.subtract)
            nc.vector.memset(attT[:], 0.0)
            for h in range(H):
                bh = bt[:, h, :].rearrange("p (b t) -> p b t", t=NS)
                last = nc.vector.tensor_tensor(ek[:, h, :].rearrange("p (b t) -> p b t", t=NS),
                                               bc(bh[:, :, NS - 1:NS], [P, NB, NS]), bh, ALU.subtract)
            chain.link(last)
            at["sub"] = chain.n
            dve.wait_ge(exped, 1)
            for l, i in enumerate(LV):
                s = LEVELS[i]
                xh, eh = halves(X[l][:], s), halves(E[l][:], s)
                nc.vector.tensor_tensor(xh[:, :, :, 0, :], halves(kt, s)[:, :, :, 0, :], eh[:, :, :, 0, :], ALU.mult)
                nc.vector.tensor_tensor(xh[:, :, :, 1, :], halves(qt, s)[:, :, :, 1, :], eh[:, :, :, 1, :], ALU.mult)
            nc.vector.tensor_tensor(kd[:], kt, ek[:], ALU.mult)
            chain.link(nc.vector.tensor_tensor(qe[:], qt, eq[:], ALU.mult))
            at["mult"] = chain.n
            dve.wait_ge(landed, 32)
            dve.wait_ge(grammed, 1)
            for l in range(len(LV) + 1):
                i = LV[l] if l < len(LV) else len(LEVELS)
                chain.link(nc.vector.copy_predicated(attT[:], bc(lv[0:TS, i, None, 0:TS], [TS, H, TS]), ps_g[:, l]))
            at["select"] = chain.n
            for h in range(H):
                if h < 2:
                    dve.wait_ge(zeroed, h + 2)
                else:
                    dve.wait_ge(deltaed, h - 1)
                chain.link(nc.vector.tensor_tensor(vm[h % 2][0:TS], bc(v[:, h, None, :], [TS, NB, DG]),
                                                   bc(g.col("bmask")[0:TS, :, None], [TS, NB, DG]), ALU.mult))
                at[("vm", h)] = chain.n
                if h:
                    state(dve, h - 1)
            state(dve, H - 1)

        @block.gpsimd
        def _(pool):
            for x in (kdT, *vm):
                nc.gpsimd.memset(x[:], 0.0).then_inc(zeroed, 1)

        @block.scalar
        def _(act):
            act.wait_ge(dv, at["sub"])
            for e in [*E, ek]:
                nc.scalar.activation(e[:], e[:], ACT.Exp, scale=IT)
            nc.scalar.activation(el[:], seqs(bt)[:, :, :, NS - 1], ACT.Exp, scale=IT)
            nc.scalar.activation(eq[:], bt, ACT.Exp, scale=IT).then_inc(exped, 1)
            act.wait_ge(turned, 1)
            act.wait_ge(zeroed, 1)
            nc.scalar.activation(kdT[0:TS], ps_t[:], ACT.Copy).then_inc(taken, 1)
            for h in range(H):
                act.wait_ge(state_read, h + 1)
                nc.scalar.activation(read[:, h], ps_d[:, 2 * h:2 * h + 2, :], ACT.Copy).then_inc(read_taken, 1)
            act.wait_ge(summed, 1)
            nc.scalar.activation(o[:, :, SEQ:T], ps_o[:], ACT.Copy)

        @block.tensor
        def _(pe):
            pe.wait_ge(dv, at["mult"])
            for l in range(len(LV) + 1):
                for h in range(H):
                    a, c = (X[l][:, h, :], X[l][:, h, :]) if l < len(LV) else (kt[:, h, :], qt[:, h, :])
                    last = nc.tensor.matmul(ps_g[:, l, h, :], a, c, start=True, stop=True)
            last.then_inc(grammed, 1)
            for h in range(H):
                last = nc.tensor.transpose(ps_t[:, h, :], kd[:, h, :], g.ident())
            last.then_inc(turned, 1)
            pe.wait_ge(landed, 32)
            for h in range(H):
                for n in range(4):
                    last = nc.tensor.matmul(ps_d[n * TS:(n + 1) * TS, 2 * h:2 * h + 2, :], qe[:, h, :],
                                            ss[:, 2 * n:2 * n + 2, h, :], start=True, stop=True)
                last.then_inc(state_read, 1)
            pe.wait_ge(dv, at["select"])
            for h in range(H):
                pe.wait_ge(read_taken, h + 1)
                for e in range(2):
                    nc.tensor.matmul(ps_o[:, 2 * h + e, :], v[:, h, e * P:(e + 1) * P], attT[:, h, :],
                                     start=True, stop=False)
                    for n in range(2):
                        last = nc.tensor.matmul(ps_o[:, 2 * h + e, :], read[:, h, n, e * P:(e + 1) * P],
                                                pick[:, n * TS:(n + 1) * TS], start=False, stop=(n == 1))
            last.then_inc(summed, 1)
            pe.wait_ge(taken, 1)
            for h in range(H):
                pe.wait_ge(dv, at[("vm", h)])
                if h:
                    pe.wait_ge(done, h)
                for n in range(NB // 2):
                    last = nc.tensor.matmul(ps_d[:, 2 * n:2 * n + 2, :], kdT[:, h, :], vm[h % 2][:, 2 * n:2 * n + 2, :],
                                            start=True, stop=True)
                last.then_inc(deltaed, 1)


def decoder_step(nc, a, outs):
    def scratch(name, shape):
        return nc.dram_tensor(name, shape, F32, kind="Internal").ap()

    Kit.taken = []
    x_0, x_1, x_2 = (scratch(f"x_{i}", [P, KB, T]) for i in range(3))
    v_gla = scratch("v_gla", [4, T, GW])
    gates = scratch("gates", [P, KB, T])
    with ExitStack() as life:
        g = State(nc, life)
        g.lam_in = [a[n] for n in ("lam_q1", "lam_k1", "lam_q2", "lam_k2")]

        def sb(stack, name, shape, dt=F32):
            return stack.enter_context(nc.sbuf_tensor(name, shape, dt))

        def operand(stack, tag):
            g.ahi, g.alo = (stack.enter_context(nc.sbuf_tensor(f"{tag}_{x}", [P, KB, T], F32R, side="right"))
                            for x in ("hi", "lo"))

        def copy_to(dst, scale=1.0):
            return lambda u, s: nc.scalar.activation(by_thirds(dst[:, bass.ds(u, 1), :]), s, ACT.Copy, scale=scale)

        def silu_to(dst):
            return lambda u, s: nc.scalar.activation(by_thirds(dst[:, bass.ds(u, 1), :]), s, ACT.Silu)

        def gate_store(u):
            return gates[:, bass.ds(u, 1), :], y[:, bass.ds(u, 1), :]

        stage_load(nc, g, a["consts"], a["vecs"])
        conditioning = life.enter_context(ExitStack())
        g.silu_c = conditioning.enter_context(nc.sbuf_tensor("silu_c", [P, KB, 32], F32, side="right"))
        stage_modulation(nc, g, a["w_ada"], a["cT"], 8)
        y_flat = sb(life, "y", [P, KB * T])
        y = y_flat[:].rearrange("p (k t) -> p k t", k=KB)

        with ExitStack() as first:
            with ExitStack() as projections:
                operand(projections, "h0")
                stage_norm(nc, g, "n0", y_flat[:], None, None, (0, 0), a["x"], None)
                stage_linear(nc, g, "ga", a["w_ga"], [(H, silu_to(y), gate_store)])
                qkT = sb(first, "qkT", [P, 12, T])
                stage_project(nc, g, "qkv", y_flat[:], a["w_qkv"], (3, outs["rotated"]), (2, outs["values"]), qkT,
                              a["w_ada"], 8)
            conditioning.close()
            ids = sb(first, "ids", [1, NB * NPG], I32)
            kt = [sb(first, f"kt{n}", [P, GP, H, PAGE]) for n in range(PG)]
            stage_retention(nc, g, qkT, outs["rotated"], outs["values"], y, a["state_ret"],
                            outs["ret_prompt"], outs["ret_sample"], a["pages"], ids, a["cache_k"], kt)
            stage_attention(nc, g, qkT, a["cache_k"], a["cache_v"], ids, kt, outs["values"], y)
        recycle_semaphores(nc)
        h = life.enter_context(ExitStack())
        operand(h, "h")
        stage_heads(nc, g, "hd0", y, gates,
                    [([h], h, None) for h in range(H)] + [([H + h], None, [g.vcol("g_diff")]) for h in range(H)])
        stage_linear(nc, g, "oab", a["w_out_ab"], [(KB, copy_to(y), None)])
        stage_norm(nc, g, "n1", None, y, (0, 2), (0, 3), a["x"], x_0)
        stage_ffn(nc, g, "f0", 0, a["w_ffn0"], y, a["conv_in0"], outs["conv0"])
        stage_norm(nc, g, "n2", None, y, (0, 5), (1, 0), x_0, x_1)

        recycle_semaphores(nc)
        stage_project(nc, g, "vc", y_flat[:], a["w_vc"], (0, None), (2, v_gla), None)
        with ExitStack() as second:
            qk = sb(second, "qk", [P, 2 * H, T])
            b = sb(second, "b", [P, H, T])
            stage_linear(nc, g, "qkr", a["w_qkr"],
                         [(H, copy_to(qk, DV ** -0.5), None), (H, copy_to(qk[:, H:2 * H, :]), None),
                          (2 * H, silu_to(y), gate_store)])
            stage_gate(nc, g, a["w_a"], a["w_gate"], a["scan"], b)
            h.close()
            states = sb(second, "sample_states", [P, NB, H, 256])
            v_samples = sb(second, "v_samples", [TS, H, 256])
            stage_gla(nc, g, qk, b, a["levels"], v_gla, y, outs["gla_prompt"],
                      [(states[:], a["state_gla"]), (v_samples[:], v_gla[:, SEQ:T, :].rearrange("h p e -> p h e"))])
            stage_gla_samples(nc, g, qk, b, a["levels"], a["picks"], v_samples, states, y, outs["gla_sample"])
        operand(life, "m")
        g_gla = g.vcol("g_gla")
        stage_heads(nc, g, "hd1", y, gates,
                    [([2 * h, 2 * h + 1], 2 * h, [g_gla[:, 0:1], g_gla[:, 1:2]]) for h in range(H)])
        stage_linear(nc, g, "oc", a["w_out_c"], [(KB, copy_to(y), None)])
        stage_norm(nc, g, "n3", None, y, (1, 2), (1, 3), x_1, x_2)
        stage_ffn(nc, g, "f1", 1, a["w_ffn1"], y, a["conv_in1"], outs["conv1"])
        stage_norm(nc, g, "n4", None, y, (1, 5), None, x_2, outs["x_out"])


def _constants():
    c = np.zeros((P, NCONST), np.float32)

    def put(name, a):
        a = np.asarray(a, np.float64).astype(np.float32)
        c[:a.shape[0], CONST[name][0]:CONST[name][1]] = a.reshape(a.shape[0], -1)

    i = np.arange(P)
    put("ident", np.eye(P))
    put("causal", np.where(i[None, :] <= i[:, None], 0.0, NEG))
    gamma = 1.0 - np.exp2(-5.0 - np.arange(H))
    scale = 64 ** -0.5
    rel = i[None, :] - i[:, None]
    put("decay", np.stack([np.where(rel >= 0, gm ** np.maximum(rel, 0), 0) for gm in gamma], 1) * scale)
    put("decq", np.broadcast_to(np.stack([gm ** (i + 1) for gm in gamma]), (P, H, P)))
    put("deck", np.stack([gm ** (P - 1 - i) for gm in gamma], 1) * scale)
    half = (i // 64)[:, None]
    pair = 2 * np.arange(2)[None, :] + half
    put("decc", gamma[pair] ** P)
    inv = (10000.0 ** (-np.arange(0, 64, 2) / 64)).astype(np.float32)
    pos = np.concatenate([np.arange(SEQ), PAST + np.tile(np.arange(NS), NB)]).astype(np.float32)
    ang = (pos[:, None] * inv[None, :]).astype(np.float32).astype(np.float64)
    ang = np.concatenate([ang, np.zeros((TILES * P - T, 32))]).reshape(TILES, P, 32).transpose(1, 0, 2)
    put("cos", np.cos(ang))
    put("sin", np.stack([-np.sin(ang), np.sin(ang)], 2))
    s = np.arange(TS)
    same = (s[:, None] // NS == s[None, :] // NS)
    srel = s[None, :] - s[:, None]
    put("sdecay", np.stack([np.where(same & (srel >= 0), gm ** np.maximum(srel, 0), 0) for gm in gamma], 1) * scale)
    put("sdecq", np.broadcast_to(np.stack([gm ** (s % NS + 1) for gm in gamma]), (P, H, TS)))
    put("sdeck", np.stack([gm ** (NS - 1 - s % NS) for gm in gamma], 1) * scale)
    put("sdecc", gamma[pair] ** NS)
    row = np.arange(P)
    allowed = (row[:, None] >= P - TS) & (np.arange(NS)[None, :] <= row[:, None] % NS)
    put("smask", np.where(allowed, 0.0, NEG))
    put("sel", np.stack([(row[:, None] % TS // 8 == h) & (row[:, None] % NS == np.arange(NS)[None, :])
                         for h in range(H)], 1))
    put("bmask", s[:, None] // NS == np.arange(NB)[None, :])
    put("maps", np.stack([s % 8 < NS, s % 8 >= NS])[None])
    t = np.arange(T)
    first = np.where(t < SEQ, t % CH == 0, (t - SEQ) % NS == 0)
    return c, np.broadcast_to(np.where(first, 0.0, 1.0), (P, T)).astype(np.float32)


def _picks():
    block, token = np.divmod(np.arange(P)[:, None], TS)
    s = np.arange(TS)[None]
    return np.concatenate([(token == s) & (s // NS == 2 * block + n) for n in range(2)], 1).astype(np.float32)


def _level_masks():
    i = np.arange(P)
    m = [((i[:, None] // (2 * s) == i[None, :] // (2 * s)) & (i[:, None] % (2 * s) < s) & (i[None, :] % (2 * s) >= s))
         for s in LEVELS]
    m.append(i[:, None] == i[None, :])
    return np.stack(m, 1).astype(np.int32)


def _units(w, width=P):
    n = w.shape[1] // width
    return np.ascontiguousarray(w.reshape(KB, P, n, width).transpose(2, 1, 0, 3).reshape(n, P, KB * width))


def _columns(v):
    return np.ascontiguousarray(v.reshape(-1, P).T)


def _hidden_order(v):
    v = v.reshape(v.shape[:-1] + (2, FB, P))
    return np.moveaxis(v, -3, -2).reshape(v.shape[:-3] + (2 * FB, P))


def _ffn_units(w_up, w_down):
    up = _units(w_up).reshape(2, FB, P, UW)
    down = w_down.reshape(FB, P, D)
    out = [up[0, 0], up[1, 0], up[0, 1], up[1, 1]]
    for p in range(1, FB // 2):
        out += [up[0, 2 * p], up[1, 2 * p], down[2 * p - 2], down[2 * p - 1], up[0, 2 * p + 1], up[1, 2 * p + 1]]
    out += [down[FB - 2], down[FB - 1]]
    return np.stack(out)


def _feature_major(prompt, sample):
    a = np.concatenate([prompt, sample.reshape(TS, -1)])
    return np.ascontiguousarray(a.reshape(T, -1, P).transpose(2, 1, 0))


def lay_out(i):
    a = {}
    a["consts"], a["scan"] = _constants()
    a["levels"] = _level_masks()
    a["picks"] = _picks()
    v = [_columns(i["b_ada"])] + [_columns(i[n]) for n in ("g_pre_mix", "g_post_mix", "g_pre_ffn", "g_post_ffn")]
    v += [_columns(i["g_diff"]), _columns(i["g_gla"]), _columns(i["b_gate_c"])]
    v += [_hidden_order(i["conv_b"]).reshape(-1, P).T]
    cw = _hidden_order(i["conv_w"])
    v += [cw.transpose(3, 0, 2, 1).reshape(P, -1)]
    a["vecs"] = np.ascontiguousarray(np.concatenate(v, 1))
    for n in ("lam_q1", "lam_k1", "lam_q2", "lam_k2"):
        a[n] = i[n].reshape(1, 64)
    a["x"] = _feature_major(i["x_prompt"][0], i["x_sample"])
    a["cT"] = np.ascontiguousarray(np.concatenate([i["c_prompt"], i["c_sample"]]).reshape(C9, KB, P).transpose(2, 1, 0))
    a["w_ada"] = np.concatenate([_units(i["w_ada"][l], UA) for l in range(2)]).reshape(NUA, P, KB, UA)
    w = i["w_in_ab"][0]
    qa, ka, va, ga, qb, kb, vb = np.split(w, [256, 512, 1024, 1536, 2048, 2560], axis=1)
    a["w_qkv"] = _units(np.concatenate([qa, qb, ka, kb, va, vb], 1), GW)
    a["w_ga"] = _units(ga)
    a["w_out_ab"] = _units(i["w_out_ab"][0])
    w = i["w_in_c"][0]
    q, k, vv, r, ga_ = np.split(w, [512, 1024, 2048, 3072], axis=1)
    a["w_qkr"] = _units(np.concatenate([q, k, r], 1))
    a["w_vc"] = _units(vv, GW)
    a["w_a"] = _units(ga_, 16)[0]
    a["w_gate"] = i["w_gate_c"][0]
    a["w_out_c"] = _units(i["w_out_c"][0])
    for l in range(2):
        a[f"w_ffn{l}"] = _ffn_units(i["w_up"][l], i["w_down"][l])
        sc = _hidden_order(i["state_conv"][l])
        a[f"conv_in{l}"] = np.ascontiguousarray(sc.transpose(3, 2, 0, 1))
    a["cache_k"] = np.ascontiguousarray(i["cache_k"][0].transpose(0, 3, 2, 1))
    a["cache_v"] = i["cache_v"][0].reshape(-1, PAGE, H * DV)
    a["pages"] = np.ascontiguousarray(i["page_table"].astype(np.int32))
    a["state_ret"] = np.ascontiguousarray(i["state_ret"][0].reshape(NB, 2, P, DV).transpose(2, 0, 1, 3))
    a["state_gla"] = np.ascontiguousarray(i["state_gla"][0].transpose(2, 0, 1, 3))
    return a


OUTPUTS = {"rotated": [6, T, GW], "values": [4, T, GW], "ret_prompt": [P, 2, DV], "ret_sample": [P, NB, 2, DV],
           "x_out": [P, KB, T], "gla_prompt": [P, H, 256], "gla_sample": [P, NB, H, 256],
           "conv0": [P, 2 * FB, 2 * C9], "conv1": [P, 2 * FB, 2 * C9]}


def kernel(**inputs):
    import concourse.bacc as _bacc
    from concourse.bass_utils import run_bass_kernel_spmd

    arrays = lay_out({n: np.asarray(v) for n, v in inputs.items()})
    nc = _bacc.Bacc("TRN2", target_bir_lowering=False, num_devices=1)
    a = {n: nc.dram_tensor(n, list(v.shape), mybir.dt.from_np(v.dtype), kind="ExternalInput").ap()
         for n, v in arrays.items()}
    outs = {n: nc.dram_tensor(n, s, F32, kind="ExternalOutput").ap() for n, s in OUTPUTS.items()}
    decoder_step(nc, a, outs)
    nc.finalize()
    r = run_bass_kernel_spmd(nc, [arrays], core_ids=[0]).results[0]
    r = {n: np.asarray(r[n]).reshape(s) for n, s in OUTPUTS.items()}

    x = r["x_out"].transpose(2, 1, 0).reshape(T, D)
    kb = r["rotated"][4:6].transpose(1, 0, 2).reshape(T, H, DV)
    vb = r["values"][VB_GROUP:].transpose(1, 0, 2).reshape(T, H, DV)
    conv = np.stack([r[n].reshape(P, FB, 2, 2 * C9).transpose(3, 2, 1, 0).reshape(C9, 2, 2 * FB * P)
                     for n in ("conv0", "conv1")])
    out = (x[None, :SEQ], x[SEQ:].reshape(NB, NS, D),
           kb[None, None, :SEQ], vb[None, None, :SEQ],
           kb[SEQ:].reshape(1, NB, NS, H, DV), vb[SEQ:].reshape(1, NB, NS, H, DV),
           r["ret_prompt"].reshape(2, 64, 2, DV).transpose(2, 0, 1, 3).reshape(1, 1, H, 64, DV),
           r["ret_sample"].reshape(2, 64, NB, 2, DV).transpose(2, 3, 0, 1, 4).reshape(1, NB, H, 64, DV),
           r["gla_prompt"].transpose(1, 0, 2)[None, None], r["gla_sample"].transpose(1, 2, 0, 3)[None],
           conv[:, 0:1], conv[:, 1:])
    return tuple(np.ascontiguousarray(o) for o in out)
```
